# Optimizing a Trainium2 kernel written in Bass

```python
import jax
import jax.numpy as jnp
from jax import lax
import numpy as np
import math
import jax, jax.numpy as jnp

D_MODEL = 1024
BATCH = 1
SEQ = 256
DEPTH = 1

CHUNK = 64

D_MIX = D_MODEL
N_GROUPS = 4
GROUP_W = D_MIX // N_GROUPS
HEAD_DIM = 64

FOX_HEADS = GROUP_W // HEAD_DIM
FOX_DH = HEAD_DIM
Q_BLOCK = 128
FOX_BIAS_INIT = 2.0

GDN_HEADS = GROUP_W // HEAD_DIM
GDN_DK = HEAD_DIM
GDN_DV = HEAD_DIM
GDN_CONV = 4

HG_HEADS = GROUP_W // HEAD_DIM
HG_DK = HEAD_DIM
HG_DV = HEAD_DIM
HG_KW = HG_HEADS * HG_DK

GLA_HEADS = GROUP_W // HEAD_DIM
GLA_DV = HEAD_DIM
GLA_DK = HEAD_DIM // 2
GLA_KW = GLA_HEADS * GLA_DK
GLA_RANK = 16
GLA_NORM = 16.0

LA_BLOCK = 16

D_FF = ((8 * D_MODEL // 3 + 255) // 256) * 256
FFN_CONV = 3
EPS = 1e-6

IN_SIZES = (
    3 * GROUP_W, FOX_HEADS,
    3 * GROUP_W, GDN_HEADS, GDN_HEADS, GROUP_W,
    HG_KW, HG_KW, GROUP_W, GROUP_W,
    2 * GLA_KW, GROUP_W, GLA_RANK, GROUP_W,
)
IN_COLS = sum(IN_SIZES)


def _cut_points(sizes):
    cuts, acc = [], 0
    for s in sizes[:-1]:
        acc += s
        cuts.append(acc)
    return cuts

def rms_norm(x, g):
    xf = x.astype(jnp.float32)
    y = xf * lax.rsqrt(jnp.mean(xf * xf, axis=-1, keepdims=True) + EPS)
    return (y * g.astype(jnp.float32)).astype(x.dtype)

def l2norm(x):
    return x * lax.rsqrt(jnp.sum(x * x, axis=-1, keepdims=True) + EPS)

def split_heads(t, n):
    b, s, w = t.shape
    return t.reshape(b, s, n, w // n).transpose(0, 2, 1, 3)

def merge_heads(t):
    b, h, s, d = t.shape
    return t.transpose(0, 2, 1, 3).reshape(b, s, h * d)

def causal_dwconv(x, w):
    k_w = w.shape[0]
    s = x.shape[1]
    xp = jnp.pad(x, ((0, 0), (k_w - 1, 0), (0, 0)))
    y = xp[:, 0:s] * w[0]
    for j in range(1, k_w):
        y = y + xp[:, j:j + s] * w[j]
    return y

def fox_attention(q, k, v, log_f):
    b, h, s, d = q.shape
    c = jnp.cumsum(log_f, axis=-1)
    nb = s // Q_BLOCK
    qb = q.reshape(b, h, nb, Q_BLOCK, d).transpose(2, 0, 1, 3, 4)
    cb = c.reshape(b, h, nb, Q_BLOCK).transpose(2, 0, 1, 3)
    pos_k = jnp.arange(s)
    scale = d ** -0.5

    def one_block(args):
        qi, ci, bi = args
        pos_q = bi * Q_BLOCK + jnp.arange(Q_BLOCK)
        logits = jnp.einsum('bhqd,bhkd->bhqk', qi, k) * scale + ci[..., :, None] - c[:, :, None, :]
        logits = jnp.where(pos_k[None, :] <= pos_q[:, None], logits, -jnp.inf)
        probs = jax.nn.softmax(logits, axis=-1)
        return jnp.einsum('bhqk,bhkd->bhqd', probs, v)

    o = lax.map(one_block, (qb, cb, jnp.arange(nb)))
    return o.transpose(1, 2, 0, 3, 4).reshape(b, h, s, d)

def gated_delta_chunked(q, k, v, g, beta):
    b, h, s, dk = q.shape
    dv = v.shape[-1]
    c = CHUNK
    n = s // c
    q = (q * dk ** -0.5).reshape(b, h, n, c, dk)
    k = k.reshape(b, h, n, c, dk)
    v = v.reshape(b, h, n, c, dv)
    beta = beta.reshape(b, h, n, c)
    G = jnp.cumsum(g.reshape(b, h, n, c), axis=-1)
    causal = jnp.tril(jnp.ones((c, c), bool))
    strict = jnp.tril(jnp.ones((c, c), bool), -1)
    decay = jnp.exp(jnp.where(causal, G[..., :, None] - G[..., None, :], -jnp.inf))
    kb = k * beta[..., None]
    m = jnp.where(strict, jnp.einsum('bhnrd,bhnsd->bhnrs', kb, k) * decay, 0.0)
    t_mat = m + jnp.eye(c, dtype=m.dtype)
    w = lax.linalg.triangular_solve(t_mat, kb * jnp.exp(G)[..., None],
                                    left_side=True, lower=True, unit_diagonal=True)
    u = lax.linalg.triangular_solve(t_mat, v * beta[..., None],
                                    left_side=True, lower=True, unit_diagonal=True)
    a_qk = jnp.where(causal, jnp.einsum('bhnrd,bhnsd->bhnrs', q, k) * decay, 0.0)
    q_in = q * jnp.exp(G)[..., None]
    k_out = k * jnp.exp(G[..., -1:] - G)[..., None]
    a_chunk = jnp.exp(G[..., -1])

    def step(state, inp):
        qi, ki, wi, ui, ai_qk, ai = inp
        v_new = ui - jnp.einsum('bhcd,bhde->bhce', wi, state)
        o = jnp.einsum('bhcd,bhde->bhce', qi, state) + jnp.einsum('bhrs,bhse->bhre', ai_qk, v_new)
        state = state * ai[..., None, None] + jnp.einsum('bhcd,bhce->bhde', ki, v_new)
        return state, o

    xs = tuple(jnp.moveaxis(t, 2, 0) for t in (q_in, k_out, w, u, a_qk, a_chunk))
    _, o = lax.scan(step, jnp.zeros((b, h, dk, dv), q.dtype), xs)
    return jnp.moveaxis(o, 0, 2).reshape(b, h, s, dv)

def gla_chunked(q, k, v, log_a, scale):
    b, h, s, dk = q.shape
    dv = v.shape[-1]
    c = LA_BLOCK
    n = s // c
    q = (q * scale).reshape(b, h, n, c, dk)
    k = k.reshape(b, h, n, c, dk)
    v = v.reshape(b, h, n, c, dv)
    G = jnp.cumsum(log_a.reshape(b, h, n, c, dk), axis=3)
    causal = jnp.tril(jnp.ones((c, c), bool))
    rel = jnp.where(causal[:, :, None], G[:, :, :, :, None, :] - G[:, :, :, None, :, :], -jnp.inf)
    a_intra = jnp.einsum('bhnrd,bhnsd,bhnrsd->bhnrs', q, k, jnp.exp(rel))
    o_intra = jnp.einsum('bhnrs,bhnse->bhnre', a_intra, v)
    g_last = G[:, :, :, -1]
    q_in = q * jnp.exp(G)
    k_out = k * jnp.exp(g_last[:, :, :, None, :] - G)
    a_chunk = jnp.exp(g_last)

    def step(state, inp):
        qi, ki, vi, ai = inp
        o = jnp.einsum('bhcd,bhde->bhce', qi, state)
        state = state * ai[..., None] + jnp.einsum('bhcd,bhce->bhde', ki, vi)
        return state, o

    xs = tuple(jnp.moveaxis(t, 2, 0) for t in (q_in, k_out, v, a_chunk))
    _, o_inter = lax.scan(step, jnp.zeros((b, h, dk, dv), q.dtype), xs)
    return (o_intra + jnp.moveaxis(o_inter, 0, 2)).reshape(b, h, s, dv)

def hgrn_lower_bounds(lb_param):
    cs = jnp.cumsum(jax.nn.softmax(lb_param.astype(jnp.float32), axis=0), axis=0)
    return cs - cs[0:1]

def token_mix(h, w_in, fox_qn_g, fox_kn_g, fox_b_f, fox_on_g, gdn_conv_w, gdn_a_log,
              gdn_dt_bias, gdn_on_g, lb, hg_on_g, gla_w_gk, gla_b_gk, gla_on_g):
    p = (h @ w_in).astype(jnp.float32)
    (fox_qkv, fox_f, gdn_qkv, gdn_b, gdn_a, gdn_z, hg_q, hg_f, hg_i, hg_g,
     gla_qk, gla_v, gla_gk, gla_g) = jnp.split(p, _cut_points(IN_SIZES), axis=-1)

    q, k, v = jnp.split(fox_qkv, 3, axis=-1)
    q = rms_norm(split_heads(q, FOX_HEADS), fox_qn_g)
    k = rms_norm(split_heads(k, FOX_HEADS), fox_kn_g)
    log_f = jax.nn.log_sigmoid(fox_f + fox_b_f).transpose(0, 2, 1)
    o_a = rms_norm(fox_attention(q, k, split_heads(v, FOX_HEADS), log_f), fox_on_g)

    qkv = jax.nn.silu(causal_dwconv(gdn_qkv, gdn_conv_w))
    q, k, v = jnp.split(qkv, 3, axis=-1)
    beta = jax.nn.sigmoid(gdn_b).transpose(0, 2, 1)
    g = (-jnp.exp(gdn_a_log) * jax.nn.softplus(gdn_a + gdn_dt_bias)).transpose(0, 2, 1)
    o_b = gated_delta_chunked(l2norm(split_heads(q, GDN_HEADS)), l2norm(split_heads(k, GDN_HEADS)),
                              split_heads(v, GDN_HEADS), g, beta)
    o_b = rms_norm(o_b, gdn_on_g) * jax.nn.silu(split_heads(gdn_z, GDN_HEADS))

    lbh = lb.reshape(HG_HEADS, 1, HG_DK)
    f_logit = split_heads(hg_f, HG_HEADS)
    log_forget = jnp.logaddexp(jnp.log(lbh), jnp.log1p(-lbh) + jax.nn.log_sigmoid(f_logit))
    k_in = (1.0 - lbh) * jax.nn.sigmoid(-f_logit)
    o_c = gla_chunked(jax.nn.silu(split_heads(hg_q, HG_HEADS)), k_in, split_heads(hg_i, HG_HEADS),
                      log_forget, HG_DK ** -0.5)
    o_c = rms_norm(o_c, hg_on_g) * jax.nn.silu(split_heads(hg_g, HG_HEADS))

    q, k = jnp.split(gla_qk, 2, axis=-1)
    log_a = jax.nn.log_sigmoid(gla_gk @ gla_w_gk + gla_b_gk) / GLA_NORM
    o_d = gla_chunked(split_heads(q, GLA_HEADS), split_heads(k, GLA_HEADS), split_heads(gla_v, GLA_HEADS),
                      split_heads(log_a, GLA_HEADS), GLA_DK ** -0.5)
    o_d = rms_norm(o_d, gla_on_g) * jax.nn.silu(split_heads(gla_g, GLA_HEADS))

    return jnp.concatenate([merge_heads(o_a), merge_heads(o_b), merge_heads(o_c), merge_heads(o_d)], axis=-1)

def conv_glu_ffn(h, w_up, conv_w, conv_b, w_down):
    u = causal_dwconv(h @ w_up, conv_w) + conv_b
    gate, up = jnp.split(u, 2, axis=-1)
    return (jax.nn.silu(gate) * up) @ w_down

def first_inputs(seed: int = 0) -> dict:
    key = jax.random.key(seed)
    ks = jax.random.split(key, 24)
    f32 = jnp.float32

    def nrm(k, shape, scale):
        return scale * jax.random.normal(k, shape, f32)

    def gain(k, n):
        return 1.0 + 0.1 * jax.random.normal(k, (DEPTH, n), f32)

    dt = jnp.exp(jax.random.uniform(ks[8], (DEPTH, GDN_HEADS), f32, jnp.log(1e-3), jnp.log(1e-1)))
    return {
        'x': nrm(ks[0], (BATCH, SEQ, D_MODEL), 1.0),
        'norm1_g': gain(ks[1], D_MODEL),
        'w_in': nrm(ks[2], (DEPTH, D_MODEL, IN_COLS), D_MODEL ** -0.5),
        'fox_qn_g': gain(ks[3], FOX_DH),
        'fox_kn_g': gain(ks[4], FOX_DH),
        'fox_b_f': FOX_BIAS_INIT + nrm(ks[5], (DEPTH, FOX_HEADS), 0.1),
        'fox_on_g': gain(ks[6], FOX_DH),
        'gdn_conv_w': nrm(ks[7], (DEPTH, GDN_CONV, 3 * GROUP_W), GDN_CONV ** -0.5),
        'gdn_a_log': jnp.log(jax.random.uniform(ks[9], (DEPTH, GDN_HEADS), f32, 1.0, 16.0)),
        'gdn_dt_bias': dt + jnp.log(-jnp.expm1(-dt)),
        'gdn_on_g': gain(ks[10], GDN_DV),
        'hg_lb': nrm(ks[11], (DEPTH, HG_KW), 0.1),
        'hg_on_g': gain(ks[12], HG_DV),
        'gla_w_gk': nrm(ks[13], (DEPTH, GLA_RANK, GLA_KW), GLA_RANK ** -0.5),
        'gla_b_gk': nrm(ks[14], (DEPTH, GLA_KW), 0.1),
        'gla_on_g': gain(ks[15], GLA_DV),
        'w_out': nrm(ks[16], (DEPTH, D_MIX, D_MODEL), D_MIX ** -0.5),
        'norm2_g': gain(ks[17], D_MODEL),
        'w_up': nrm(ks[18], (DEPTH, D_MODEL, 2 * D_FF), D_MODEL ** -0.5),
        'ffn_conv_w': nrm(ks[19], (DEPTH, FFN_CONV, 2 * D_FF), FFN_CONV ** -0.5),
        'ffn_conv_b': nrm(ks[20], (DEPTH, 2 * D_FF), 0.02),
        'w_down': nrm(ks[21], (DEPTH, D_FF, D_MODEL), D_FF ** -0.5),
    }

def first_block(x, norm1_g, w_in, fox_qn_g, fox_kn_g, fox_b_f, fox_on_g, gdn_conv_w, gdn_a_log,
              gdn_dt_bias, gdn_on_g, hg_lb, hg_on_g, gla_w_gk, gla_b_gk, gla_on_g, w_out,
              norm2_g, w_up, ffn_conv_w, ffn_conv_b, w_down):
    lower_bounds = hgrn_lower_bounds(hg_lb)
    for l in range(DEPTH):
        mixed = token_mix(rms_norm(x, norm1_g[l]), w_in[l], fox_qn_g[l], fox_kn_g[l], fox_b_f[l],
                          fox_on_g[l], gdn_conv_w[l], gdn_a_log[l], gdn_dt_bias[l], gdn_on_g[l],
                          lower_bounds[l], hg_on_g[l], gla_w_gk[l], gla_b_gk[l], gla_on_g[l])
        x = x + mixed.astype(x.dtype) @ w_out[l]
        x = x + conv_glu_ffn(rms_norm(x, norm2_g[l]), w_up[l], ffn_conv_w[l], ffn_conv_b[l], w_down[l])
    return x


DEPTH_2 = 2

N_A_LAYERS = DEPTH_2 // 2
N_B_LAYERS = DEPTH_2 - N_A_LAYERS
CONV_WIDTH = 3
N_HEADS = 8
HEAD_DIM_2 = D_MODEL // (2 * N_HEADS)
V_HEAD_DIM = 2 * HEAD_DIM_2
QK_WIDTH = N_HEADS * 2 * HEAD_DIM_2
V_WIDTH = N_HEADS * V_HEAD_DIM
D_FF_2 = ((8 * D_MODEL // 3 + 127) // 128) * 128
PLE_DIM = 256
N_BUCKETS = 32
MAX_DISTANCE = 128


def rms_norm_2(x, g):
    xf = x.astype(jnp.float32)
    y = xf * lax.rsqrt(jnp.mean(xf * xf, axis=-1, keepdims=True) + EPS)
    return (y * g.astype(jnp.float32)).astype(x.dtype)

def causal_dwconv_2(x, w):
    c = x.shape[-1]
    return lax.conv_general_dilated(
        x, w[:, None, :].astype(x.dtype), window_strides=(1,),
        padding=[(CONV_WIDTH - 1, 0)], dimension_numbers=('NWC', 'WIO', 'NWC'),
        feature_group_count=c)

def rel_bucket(dist):
    max_exact = N_BUCKETS // 2
    large = max_exact + (jnp.log(jnp.maximum(dist, 1).astype(jnp.float32) / max_exact)
                         / math.log(MAX_DISTANCE / max_exact)
                         * (N_BUCKETS - max_exact)).astype(jnp.int32)
    large = jnp.minimum(large, N_BUCKETS - 1)
    return jnp.where(dist < max_exact, dist, large)

def short_conv_mixer(h, w_in, w_conv, w_out):
    gb, gc, u = jnp.split(h @ w_in, 3, axis=-1)
    return (gb * causal_dwconv_2(gc * u, w_conv)) @ w_out

def conv_ffn(h, w_up, w_conv, w_down):
    gate, up = jnp.split(causal_dwconv_2(h @ w_up, w_conv), 2, axis=-1)
    return (jax.nn.silu(gate) * up) @ w_down

def per_layer_embed(x, p_i, g_pre, w_gate, w_proj, g_post):
    gate = jax.nn.sigmoid(rms_norm_2(x, g_pre) @ w_gate)
    return rms_norm_2(gate * (p_i @ w_proj), g_post)

def shared_kv(x, g_kv, w_kv):
    b, s, _ = x.shape
    k, v = jnp.split(rms_norm_2(x, g_kv) @ w_kv, [QK_WIDTH], axis=-1)
    return (k.reshape(b, s, N_HEADS, 2, HEAD_DIM_2),
            v.reshape(b, s, N_HEADS, V_HEAD_DIM))

def diff_attention(h, k, v, dist_bias, w_q, lam_vecs, subln_g, w_o, lambda_init):
    b, s, _ = h.shape
    nb = s // Q_BLOCK
    q = (h @ w_q).reshape(b, nb, Q_BLOCK, N_HEADS, 2, HEAD_DIM_2).transpose(1, 0, 2, 3, 4, 5)
    lv = lam_vecs.astype(jnp.float32)
    lam = jnp.exp(jnp.sum(lv[0] * lv[1])) - jnp.exp(jnp.sum(lv[2] * lv[3])) + lambda_init
    kf = k.astype(jnp.float32)
    vf = v.astype(jnp.float32)
    bias_tab = dist_bias.astype(jnp.float32)
    k_pos = jnp.arange(s)
    scale = HEAD_DIM_2 ** -0.5

    def block(args):
        qb, blk = args
        q_pos = blk * Q_BLOCK + jnp.arange(Q_BLOCK)
        dist = q_pos[:, None] - k_pos[None, :]
        bias = jnp.take(bias_tab, jnp.maximum(dist, 0), axis=0).transpose(2, 0, 1)
        logits = jnp.einsum('bqhmd,bkhmd->bhmqk', qb.astype(jnp.float32), kf) * scale
        logits = logits + bias[None, :, None]
        logits = jnp.where((dist >= 0)[None, None, None], logits, -jnp.inf)
        probs = jax.nn.softmax(logits, axis=-1)
        attn = probs[:, :, 0] - lam * probs[:, :, 1]
        return jnp.einsum('bhqk,bkhe->bqhe', attn, vf)

    o = lax.map(block, (q, jnp.arange(nb)))
    o = o.transpose(1, 0, 2, 3, 4).reshape(b, s, N_HEADS, V_HEAD_DIM)
    o = rms_norm_2(o, subln_g) * (1.0 - lambda_init)
    return o.reshape(b, s, V_WIDTH).astype(h.dtype) @ w_o

def second_inputs(seed: int = 0) -> dict:
    key = jax.random.key(seed)
    ks = jax.random.split(key, 24)
    f32 = jnp.float32

    def nrm(k, shape, scale):
        return jax.random.normal(k, shape, f32) * scale

    def gain(k, shape):
        return 1.0 + 0.05 * jax.random.normal(k, shape, f32)

    return {
        "x": nrm(ks[0], (BATCH, SEQ, D_MODEL), 1.0),
        "p": nrm(ks[1], (DEPTH_2, BATCH, SEQ, PLE_DIM), 1.0),
        "g_pre_mix": gain(ks[2], (DEPTH_2, D_MODEL)),
        "g_post_mix": gain(ks[3], (DEPTH_2, D_MODEL)),
        "g_pre_ffn": gain(ks[4], (DEPTH_2, D_MODEL)),
        "g_post_ffn": gain(ks[5], (DEPTH_2, D_MODEL)),
        "g_pre_ple": gain(ks[6], (DEPTH_2, D_MODEL)),
        "g_post_ple": gain(ks[7], (DEPTH_2, D_MODEL)),
        "w_sc_in": nrm(ks[8], (N_A_LAYERS, D_MODEL, 3 * D_MODEL), D_MODEL ** -0.5),
        "w_sc_conv": nrm(ks[9], (N_A_LAYERS, CONV_WIDTH, D_MODEL), CONV_WIDTH ** -0.5),
        "w_sc_out": nrm(ks[10], (N_A_LAYERS, D_MODEL, D_MODEL), D_MODEL ** -0.5),
        "g_kv": gain(ks[11], (D_MODEL,)),
        "w_kv": nrm(ks[12], (D_MODEL, QK_WIDTH + V_WIDTH), D_MODEL ** -0.5),
        "rel_bias": nrm(ks[13], (N_BUCKETS, N_HEADS), 0.5),
        "w_q": nrm(ks[14], (N_B_LAYERS, D_MODEL, QK_WIDTH), D_MODEL ** -0.5),
        "diff_lambda": nrm(ks[15], (N_B_LAYERS, 4, HEAD_DIM_2), 0.1),
        "g_subln": gain(ks[16], (N_B_LAYERS, V_HEAD_DIM)),
        "w_o": nrm(ks[17], (N_B_LAYERS, V_WIDTH, D_MODEL), V_WIDTH ** -0.5),
        "w_ffn_up": nrm(ks[18], (DEPTH_2, D_MODEL, 2 * D_FF_2), D_MODEL ** -0.5),
        "w_ffn_conv": nrm(ks[19], (DEPTH_2, CONV_WIDTH, 2 * D_FF_2), CONV_WIDTH ** -0.5),
        "w_ffn_down": nrm(ks[20], (DEPTH_2, D_FF_2, D_MODEL), D_FF_2 ** -0.5),
        "w_ple_gate": nrm(ks[21], (DEPTH_2, D_MODEL, D_MODEL), D_MODEL ** -0.5),
        "w_ple_proj": nrm(ks[22], (DEPTH_2, PLE_DIM, D_MODEL), PLE_DIM ** -0.5),
    }

def second_block(x, p, g_pre_mix, g_post_mix, g_pre_ffn, g_post_ffn, g_pre_ple, g_post_ple,
              w_sc_in, w_sc_conv, w_sc_out, g_kv, w_kv, rel_bias, w_q, diff_lambda,
              g_subln, w_o, w_ffn_up, w_ffn_conv, w_ffn_down, w_ple_gate, w_ple_proj):
    s = x.shape[1]
    dist_bias = jnp.take(rel_bias, rel_bucket(jnp.arange(s)), axis=0)
    k = None
    v = None
    for i in range(DEPTH_2):
        h = rms_norm_2(x, g_pre_mix[i])
        if i < N_A_LAYERS:
            mix = short_conv_mixer(h, w_sc_in[i], w_sc_conv[i], w_sc_out[i])
        else:
            j = i - N_A_LAYERS
            if j == 0:
                k, v = shared_kv(x, g_kv, w_kv)
            lambda_init = 0.8 - 0.6 * math.exp(-0.3 * i)
            mix = diff_attention(h, k, v, dist_bias, w_q[j], diff_lambda[j], g_subln[j],
                                 w_o[j], lambda_init)
        x = x + rms_norm_2(mix, g_post_mix[i])
        ffn = conv_ffn(rms_norm_2(x, g_pre_ffn[i]), w_ffn_up[i], w_ffn_conv[i], w_ffn_down[i])
        x = x + rms_norm_2(ffn, g_post_ffn[i])
        x = x + per_layer_embed(x, p[i], g_pre_ple[i], w_ple_gate[i], w_ple_proj[i], g_post_ple[i])
    return x


def setup_inputs(seed=0):
    out = dict(first_inputs(seed))
    for name, value in second_inputs(seed + 1).items():
        if name != "x":
            out[name + "_2"] = value
    return out


def reference(
    x, norm1_g, w_in, fox_qn_g, fox_kn_g, fox_b_f, fox_on_g, gdn_conv_w, gdn_a_log, gdn_dt_bias,
    gdn_on_g, hg_lb, hg_on_g, gla_w_gk, gla_b_gk, gla_on_g, w_out, norm2_g, w_up, ffn_conv_w,
    ffn_conv_b, w_down, p_2, g_pre_mix_2, g_post_mix_2, g_pre_ffn_2, g_post_ffn_2, g_pre_ple_2,
    g_post_ple_2, w_sc_in_2, w_sc_conv_2, w_sc_out_2, g_kv_2, w_kv_2, rel_bias_2, w_q_2,
    diff_lambda_2, g_subln_2, w_o_2, w_ffn_up_2, w_ffn_conv_2, w_ffn_down_2, w_ple_gate_2,
    w_ple_proj_2,
):
    x = first_block(
        x, norm1_g, w_in, fox_qn_g, fox_kn_g, fox_b_f, fox_on_g, gdn_conv_w, gdn_a_log,
        gdn_dt_bias, gdn_on_g, hg_lb, hg_on_g, gla_w_gk, gla_b_gk, gla_on_g, w_out, norm2_g,
        w_up, ffn_conv_w, ffn_conv_b, w_down,
    )
    return second_block(
        x, p_2, g_pre_mix_2, g_post_mix_2, g_pre_ffn_2, g_post_ffn_2, g_pre_ple_2, g_post_ple_2,
        w_sc_in_2, w_sc_conv_2, w_sc_out_2, g_kv_2, w_kv_2, rel_bias_2, w_q_2, diff_lambda_2,
        g_subln_2, w_o_2, w_ffn_up_2, w_ffn_conv_2, w_ffn_down_2, w_ple_gate_2, w_ple_proj_2,
    )


_drawn_inputs = setup_inputs


def setup_inputs(seed=0):
    import zlib

    import numpy as np

    out = dict(_drawn_inputs(seed))
    spreads = {}
    factors = {'fox_b_f': 67.952, 'gla_b_gk': 3.324, 'ffn_conv_b': 2.87, 'g_pre_ple_2': 4.64}
    for name, (base, spread) in spreads.items():
        noise = np.random.default_rng([zlib.crc32(name.encode()), seed]).standard_normal(out[name].shape)
        drawn = base * np.exp(spread * noise) if base else spread * noise
        out[name] = jnp.asarray(drawn.astype(out[name].dtype))
    for name, factor in factors.items():
        out[name] = (out[name] * factor).astype(out[name].dtype)
    return out
```

```python
import math
from contextlib import ExitStack

import numpy as np

import concourse.bass as bass
from concourse import mybir

F = mybir.dt.float32
R = mybir.dt.float32r
I32 = mybir.dt.int32
ALU = mybir.AluOpType
ACT = mybir.ActivationFunctionType
AX = mybir.AxisListType.X

P = 128
TOK = 256
TT = TOK // P
D = 1024
KC = D // P
BLK = 2048
RING = 3
EPS = 1e-6
ARENA = 24496
NEG = -1e30
D_FF = 2816
FT = D_FF // P
PAIRS = FT // 2
HEADS = 4
DH = 64
CHUNK = 64
GROUP = 256
TABLES = "natural_log_exp_and_others"

STEP = {}
N_BLOCKS = 0
for _name, _n in (("mix_in", 15), ("mix_out", 4), ("ffn0", 3 * PAIRS), ("sc_in", 12), ("sc_out", 4),
                  ("ffn1", 3 * PAIRS), ("ple_proj0", 1), ("ple_gate0", 4), ("att_k", 4), ("att_v", 4),
                  ("att_q", 4), ("att_out", 4), ("ffn2", 3 * PAIRS), ("ple_proj1", 1), ("ple_gate1", 4)):
    STEP[_name] = N_BLOCKS
    N_BLOCKS += _n

W_IN = {"fox_q": 0, "fox_k": 256, "fox_v": 512, "fox_f": 768, "gdn_q": 772, "gdn_k": 1028, "gdn_v": 1284,
        "gdn_b": 1540, "gdn_a": 1544, "gdn_z": 1548, "hg_q": 1804, "hg_f": 2060, "hg_i": 2316,
        "hg_g": 2572, "gla_qk": 2828, "gla_v": 3084, "gla_gk": 3340, "gla_g": 3356}
MIX_ORDER = ("small", "gdn_q", "gdn_k", "gdn_v", "hg_f", "hg_q", "fox_q", "fox_k", "fox_v", "gla_qk",
             "gla_v", "hg_i", "gdn_z", "hg_g", "gla_g")
CHANNEL_MAJOR = ("gdn_q", "gdn_k", "gdn_v", "hg_q", "gla_qk")
TOKM = {n: i for i, n in enumerate(("fox_q", "fox_k", "fox_v", "hg_f", "hg_i", "gla_v", "gdn_z", "hg_g", "gla_g"))}
SMALL = 28

MASKS = ("tri", "ones", "after", "fox_add", "blk_tri", "blk_after", "ind0", "ind1", "gdn_add", "m1",
         "t1", "t2", "t4", "t8", "t16", "t32", "e1", "e2", "e4", "e8", "e16", "e32", "e64")
MASK = {n: i for i, n in enumerate(MASKS)}

PC, N_PC = {}, 0
for _name, _n in (("norm1", 8), ("norm2", 8), ("pre_mix0", 8), ("pre_ffn0", 8), ("pre_ple0", 8),
                  ("pre_mix1", 8), ("kv", 8), ("pre_ffn1", 8), ("pre_ple1", 8), ("subln", 1),
                  ("sc_conv", 24), ("gdn_conv", 24), ("ffn_conv0", 3 * 2 * FT), ("ffn_bias", 2 * FT),
                  ("ffn_conv1", 3 * 2 * FT), ("ffn_conv2", 3 * 2 * FT)):
    PC[_name] = N_PC
    N_PC += _n

ROW, N_ROW = {}, 0
for _name, _n in (("fox_b_f", 4), ("gdn_dt", 4), ("gdn_a_log", 4), ("fox_qn", 64), ("fox_kn", 64), ("fox_on", 64),
                  ("gdn_on", 64), ("hg_on", 64), ("gla_on", 64), ("b_gk", 128), ("lambda", 256)):
    ROW[_name] = N_ROW
    N_ROW += _n

TURN = {}
_chunks = 0
for _name, _n in (("norm1", 8), ("mixed", 8), ("norm2", 8), ("pre_mix0", 8), ("pre_ffn0", 8), ("p0", 2), ("pre_ple0", 8),
                  ("pre_mix1", 8), ("att", 8), ("pre_ffn1", 8), ("p1", 2), ("pre_ple1", 8)):
    TURN[_name] = (_chunks, _chunks // 2, _n)
    _chunks += _n

N_HEADS = 8
LAMBDA_INIT = 0.8 - 0.6 * math.exp(-0.3)
N_DIST = 384
BIAS_ROWS = 33


def build(nc, weights, x_in, masks_in, ident_in, channel_in, row_in, w_gk_in, post_in, p_in, table_in,
          onehot_in, flip_in, out):
    bias_dram = nc.dram_tensor("bias_by_distance", (N_HEADS, N_DIST), F, kind="Internal").ap()
    with ExitStack() as ctx:
        sems = {}

        def sem(name):
            if name not in sems:
                sems[name] = ctx.enter_context(nc.semaphore(name))
            return sems[name]

        def sb(name, shape, dt=F):
            return ctx.enter_context(nc.sbuf_tensor(name, shape, dt))

        raw = sb("raw", [P, RING, BLK])
        w_hi = sb("w_hi", [P, RING, BLK], R)
        w_lo = sb("w_lo", [P, RING, BLK], R)
        x = sb("x", [P, TT, D])
        xn = sb("xn", [P, TT, D])
        h_hi = sb("h_hi", [P, KC, TOK], R)
        h_lo = sb("h_lo", [P, KC, TOK], R)
        channel = sb("channel", [P, N_PC])
        row = sb("row", [P, N_ROW])
        ident = sb("ident", [P, P])
        stat = sb("stat", [P, 64])
        eps = sb("eps", [P, 1])
        zeros_r = sb("zeros_r", [P, 512], R)
        arena_offset = -(-nc.sbuf_base // 32) * 32
        fence = sb("arena", [P, ARENA])

        arena = {"at": 0, "n": 0}

        def place(shape):
            n = int(np.prod(shape[1:]))
            at = arena["at"]
            arena["at"] += n
            assert arena["at"] <= ARENA, arena
            v = fence[0:shape[0], at:at + n]
            if len(shape) == 3:
                v = v.rearrange("p (a b) -> p a b", a=shape[1])
            elif len(shape) == 4:
                v = v.rearrange("p (a b c) -> p a b c", a=shape[1], b=shape[2])
            return v

        masks = place([P, len(MASKS), P])
        tokm = place([P, TT, len(TOKM), GROUP])
        small = place([P, TT, SMALL])
        chm = place([P, 12, TOK])
        gate_z = place([P, TT, 8])
        gate_l = place([P, TT, 8])
        lf = place([P, TT, HEADS])
        nlf = place([P, TT, HEADS])
        gd = place([P, TT, HEADS])
        ngd = place([P, TT, HEADS])
        beta = place([P, TT, HEADS])
        ea = place([P, HEADS])
        e_g = place([P, TT, HEADS])
        e_rest = place([P, TT, HEADS])
        e_last = place([P, TT, 2, HEADS])
        be_g = place([P, TT, HEADS])
        la = place([P, TT, 3, P])
        gk_t = place([16, TOK])
        w_gk = place([16, P])
        sq = place([P, 1024])
        mix_at = arena["at"]
        qn = place([P, 8, DH])
        kn = place([P, 8, DH])
        kbg = place([P, 8, DH])
        vb = place([P, 8, DH])
        ko = place([P, 8, DH])
        qi = place([P, 8, DH])
        w_t = place([P, 2, TOK])
        u_gd = place([P, 8, DH])
        v_new = place([P, 8, DH])
        state = place([P, 2, DH])
        dec = place([P, 8, P])
        dec_t = place([P, 8, P])
        m_gd = place([P, 8, P])
        mt_gd = place([P, 8, P])
        a_qk = place([P, 8, P])
        c_t = place([P, 8, P])
        inv, inv_t, y_gd = dec, dec_t, m_gd
        gdn_at = arena["at"]
        arena["at"] = mix_at
        fq_t = place([P, 2, TOK])
        fk_t = place([P, 2, TOK])
        probs0 = place([P, HEADS, P])
        probs1 = place([P, HEADS, TOK])
        probs_t = place([P, 12, P])
        arena["at"] = mix_at
        w_lv = place([P, 2, 768])
        z_lv = place([P, 2, 768])
        a_la = place([P, 16, P])
        a_top = place([P, 8, P])

        PS = ctx.enter_context(nc.psum_tensor("PS", [P, 8, 512], F))
        low4 = PS[:, 0:4, :].rearrange("p b n -> p (b n)").rearrange("p (t n) -> p t n", t=TT)
        high4 = PS[:, 4:8, :].rearrange("p b n -> p (b n)").rearrange("p (t n) -> p t n", t=TT)

        operand_offset = arena_offset + 4 * (ARENA - 2 * KC * TOK)
        act_hi = nc.alloc_sbuf_tensor_at("act_hi", [P, KC, TOK], R, offset=operand_offset)
        act_lo = nc.alloc_sbuf_tensor_at("act_lo", [P, KC, TOK], R, offset=operand_offset + 4 * KC * TOK)
        arena["at"] = 0
        hid_hi = act_hi[:, 0:2, :]
        hid_lo = act_lo[:, 0:2, :]
        p_hi = act_hi[:, 2:4, :]
        p_lo = act_lo[:, 2:4, :]
        y_gate = place([P, 2, TOK])
        y_up = place([P, 2, TOK])
        s_gate = place([P, 2, TOK])
        hidden = place([P, 2, TOK])
        junk = place([P, TT, D])
        post_g = place([P, D])
        p_tok = place([P, TT, TOK])
        gate_s = place([P, TT, D])
        q_t = place([P, N_HEADS, TOK])
        k_t = place([P, N_HEADS, TOK])
        v_tok = place([P, TT, D])
        bias_t = place([P, N_HEADS, TOK])
        bias_rev = junk.rearrange("p t (h n) -> p (t h) n", n=TOK)
        flip = place([P, P])
        lg1 = place([P, 2, TOK])
        lg0 = place([P, 2, P])
        at_w = place([P, 3, P])
        at_wt = place([P, 3, P])
        table = place([BIAS_ROWS, N_HEADS])
        onehot = place([BIAS_ROWS, N_DIST])
        bias_row = place([N_HEADS, N_DIST])
        lam = place([P, 8])
        att_stat = place([P, 16])
        assert arena["at"] <= ARENA - 2 * KC * TOK

        def mask(name):
            return masks[:, MASK[name], :]

        def ch(name, j=0):
            return channel[:, PC[name] + j:PC[name] + j + 1]

        def rows(name, n):
            return row[:, ROW[name]:ROW[name] + n]

        def unit(v, n):
            return v.rearrange("p (u o) -> p u o", o=1).to_broadcast([P, v.shape[1], n])

        def units(v, n):
            return v.rearrange("p (o m) -> p o m", o=1).to_broadcast([P, n, v.shape[1]])

        def group_view(grp):
            return xn[:, :, grp * GROUP:(grp + 1) * GROUP]

        def u_of(t, h):
            return (h % 2) * 4 + t * 2 + h // 2

        def la_unit(t, h):
            return u_of(t, h) if h < 4 else 8 + (h - 4) * 2 + t

        def pair_bank(t, h):
            bank, at = (h % 2, (t * 2 + h // 2) * P) if h < 4 else (h - 2, t * P)
            return PS[:, bank, at:at + P]

        def la_top_unit(h):
            return (h % 2) * 2 + h // 2 if h < 4 else h

        ALL_UNITS = [(t, h) for t in range(TT) for h in range(HEADS)]

        def th(v):
            return v.rearrange("p t h -> p (t h)")

        raw_loaded = [sem(f"raw_loaded{s}") for s in range(RING)]
        hi_ready, lo_ready, block_used = sem("hi_ready"), sem("lo_ready"), sem("block_used")
        chunks_turned, part_hi, part_ready = sem("chunks_turned"), sem("part_hi"), sem("part_ready")
        inputs = sem("inputs_loaded")
        N_INPUTS = 3 * 16

        block = ctx.enter_context(nc.Block())

        @block.sync
        def _(sp):
            sp.dma_start(x[:, :, :], x_in.rearrange("(t p) n -> p t n", p=P)).then_inc(inputs, 16)
            sp.dma_start(ident[:, :], ident_in).then_inc(inputs, 16)
            sp.dma_start(channel[:, :], channel_in).then_inc(inputs, 16)
            for s in range(RING):
                sp.dma_start(raw[:, s, :], weights[s]).then_inc(raw_loaded[s], 16)
            sp.dma_start(row[:, :], row_in.partition_broadcast(P)).then_inc(sem("mix_inputs"), 16)
            sp.dma_start(w_gk, w_gk_in).then_inc(sem("mix_inputs"), 16)
            sp.dma_start(masks, masks_in).then_inc(sem("mix_inputs"), 16)
            whole = (N_BLOCKS - RING) // RING
            with sp.Fori(1, 1 + whole) as i:
                for s in range(RING):
                    sp.wait_ge(lo_ready, RING * i + (s - RING + 1))
                    sp.dma_start(raw[:, s, :], weights[bass.ds(RING * i + s, 1)].rearrange("a p n -> (a p) n")) \
                        .then_inc(raw_loaded[s], 16)
            for n in range(RING + whole * RING, N_BLOCKS):
                sp.wait_ge(lo_ready, n - RING + 1)
                sp.dma_start(raw[:, n % RING, :], weights[n]).then_inc(raw_loaded[n % RING], 16)
            sp.wait_ge(sem("result"), 1)
            sp.dma_start(out.rearrange("(t p) n -> p t n", p=P), x[:, :, :]).then_inc(sem("stored"), 16)
            sp.wait_ge(sem("stored"), 16)

        @block.gpsimd
        def _(pool):
            pool.memset(zeros_r[:, :].bitcast(F), 0.0).then_inc(sem("zeros"), 1)
            pool.memset(eps[:, :], EPS).then_inc(sem("eps_set"), 1)
            pool.wait_ge(sem("mix_done"), 1)
            pool.dma_start(flip, flip_in).then_inc(sem("flip_loaded"), 16)
            pool.memset(table, NEG).then_inc(sem("table_row"), 1)
            pool.wait_ge(sem("table_row"), 1)
            pool.dma_start(table[0:BIAS_ROWS - 1, :], table_in).then_inc(sem("table_loaded"), 16)
            pool.dma_start(onehot, onehot_in).then_inc(sem("table_loaded"), 16)
            pool.wait_ge(sem("bias_rows"), 1)
            pool.dma_start(bias_dram, bias_row).then_inc(sem("bias_stored"), 16)
            pool.wait_ge(sem("bias_stored"), 16)
            toeplitz = bass.AP(tensor=bias_dram.tensor, offset=0, ap=[[1, P], [N_DIST, N_HEADS], [1, TOK]])
            for n in range(6):
                if n:
                    pool.wait_ge(sem("post_used"), n)
                pool.dma_start(post_g, post_in[n].partition_broadcast(P)).then_inc(sem("post_loaded"), 16)
                if n == 3:
                    pool.wait_ge(sem("tokens_ready"), 7)
                    pool.dma_start(bias_rev, toeplitz).then_inc(sem("bias_loaded"), 16)
                if n in (0, 3):
                    if n == 3:
                        pool.wait_ge(chunks_turned, TURN["p0"][0] + 2)
                    pool.dma_start(p_tok, p_in[n // 3].rearrange("(t p) n -> p t n", p=P)).then_inc(sem("p_loaded"), 16)

        @block.tensor
        def _(pe):
            def mm(o, lhs, rhs, start=True, stop=True):
                return pe.matmul(o, lhs, rhs, start=start, stop=stop)

            def block_ready(n):
                pe.wait_ge(hi_ready, n + 1)
                pe.wait_ge(lo_ready, n + 1)

            def columns(n0, slot, bank, operand, channel_major=True, n=TOK):
                block_ready(n0)
                a_hi, a_lo = operand
                for f in range(2):
                    for k in range(KC):
                        if channel_major:
                            at = k * 256 + f * P
                            ws_hi, ws_lo = w_hi[:, slot, at:at + P], w_lo[:, slot, at:at + P]
                            o = PS[:, bank, f * TOK:(f + 1) * TOK]
                            mm(o, ws_hi, a_hi[:, k, :], k == 0, False)
                            mm(o, ws_hi, a_lo[:, k, :], False, False)
                            last = mm(o, ws_lo, a_hi[:, k, :], False, k == KC - 1)
                        else:
                            tok = slice(f * P, (f + 1) * P)
                            ws_hi, ws_lo = w_hi[:, slot, k * 256:k * 256 + n], w_lo[:, slot, k * 256:k * 256 + n]
                            o = PS[:, bank, f * TOK:f * TOK + n]
                            mm(o, a_hi[:, k, tok], ws_hi, k == 0, False)
                            mm(o, a_hi[:, k, tok], ws_lo, False, False)
                            last = mm(o, a_lo[:, k, tok], ws_hi, False, k == KC - 1)
                last.then_inc(block_used, 1)

            def row_block(n0, slot, acc, operand, k0, first, final):
                block_ready(n0)
                a_hi, a_lo = operand
                for kk in range(2):
                    for t in range(TT):
                        tok = slice(t * P, (t + 1) * P)
                        parts = ((a_hi, w_hi), (a_hi, w_lo), (a_lo, w_hi))
                        for j, (a, w) in enumerate(parts):
                            for half in range(2):
                                at = kk * D + half * 512
                                last = pe.matmul(acc[:, t, half * 512:(half + 1) * 512], a[:, k0 + kk, tok],
                                                 w[:, slot, at:at + 512], start=first and kk == 0 and j == 0,
                                                 stop=final and kk == 1 and j == 2, skip_group_check=True)
                last.then_inc(block_used, 1)

            def turn(name, src, chunks):
                for j in range(chunks):
                    for t in range(TT):
                        last = pe.transpose(PS[:, 4 + j // 2, (j % 2) * TOK + t * P:(j % 2) * TOK + (t + 1) * P],
                                            src[:, t, j * P:(j + 1) * P], ident[:, :])
                    last.then_inc(chunks_turned, 1)

            def operand_ready(name):
                _, banks, chunks = TURN[name]
                pe.wait_ge(part_ready, banks + chunks // 2)

            pe.wait_ge(inputs, N_INPUTS)
            pe.wait_ge(sem("tokens_ready"), 1)
            turn("norm1", xn, 8)
            operand_ready("norm1")

            def gates():
                pe.wait_ge(sem("gates_ready"), 1)
                pe.wait_ge(sem("mix_inputs"), 48)
                o = PS[:, 0, :]
                for t in range(TT):
                    mm(o[:, t * 4:t * 4 + 4], mask("blk_tri"), gd[:, t, :])
                    mm(o[:, 8 + t * 4:12 + t * 4], mask("blk_after"), gd[:, t, :])
                    for c in range(2):
                        at = 16 + (t * 2 + c) * 4
                        last = mm(o[:, at:at + 4], mask(f"ind{c}"), gd[:, t, :])
                last.then_inc(sem("gate_sums"), 1)
                for t in range(TT):
                    last = pe.transpose(PS[0:16, 1, t * P:(t + 1) * P], small[:, t, 12:28], ident[:, :])
                last.then_inc(sem("gk_turned"), 1)
                pe.wait_ge(sem("gk_copied"), 1)
                for t in range(TT):
                    last = mm(PS[:, 1, 256 + t * P:256 + (t + 1) * P], gk_t[:, t * P:(t + 1) * P], w_gk)
                last.then_inc(sem("gk_projected"), 1)

            def gdn_tokens():
                pe.wait_ge(sem("gdn_convolved"), 1)
                pe.wait_ge(sem("gk_read"), 1)
                for s in range(3):
                    for t in range(TT):
                        for f in range(2):
                            last = pe.transpose(PS[:, s, t * TOK + f * P:t * TOK + (f + 1) * P],
                                                chm[:, 2 * s + f, t * P:(t + 1) * P], ident[:, :])
                last.then_inc(sem("gdn_token_major"), 1)

            def gdn_channels():
                pe.wait_ge(sem("gdn_normed"), 1)
                for s, v in enumerate((qn, kn, qi)):
                    w = v.rearrange("p (t c) d -> p t (c d)", t=TT)
                    for pair in range(2):
                        for t in range(TT):
                            last = pe.transpose(PS[:, s, pair * TOK + t * P:pair * TOK + (t + 1) * P],
                                                w[:, t, pair * P:(pair + 1) * P], ident[:, :])
                last.then_inc(sem("gdn_channel_major"), 1)

            def unit_of(v, t, h):
                return v[64 * (h % 2):64 * (h % 2) + 64, h // 2, t * P:(t + 1) * P]

            qn_t, kn_t, qi_t = chm[:, 0:2, :], chm[:, 2:4, :], chm[:, 4:6, :]
            bank2 = lambda b: PS[:, b:b + 2, :].rearrange("p b n -> p (b n)").rearrange("p (u n) -> p u n", n=P)

            def gdn_grams():
                pe.wait_ge(sem("gdn_copied"), 1)
                for t, h in ALL_UNITS:
                    u = u_of(t, h)
                    mm(bank2(0)[:, u, :], unit_of(kn_t, t, h), unit_of(kn_t, t, h))
                    g_b = gd[:, t, h:h + 1].to_broadcast([P, P])
                    ng_b = ngd[:, t, h:h + 1].to_broadcast([P, P])
                    o = bank2(2)[:, u, :]
                    mm(o, mask("blk_tri"), g_b, True, False)
                    mm(o, ng_b, mask("blk_tri"), False, False)
                    last = mm(o, ident[:, :], mask("gdn_add"), False, True)
                last.then_inc(sem("decay_logs"), 1)
                for t, h in ALL_UNITS:
                    last = mm(bank2(6)[:, u_of(t, h), :], unit_of(kn_t, t, h), unit_of(qn_t, t, h))
                last.then_inc(sem("qk_gram"), 1)
                pe.wait_ge(sem("decay"), 1)
                for u in range(8):
                    last = pe.transpose(bank2(2)[:, u, :], dec[:, u, :], ident[:, :])
                last.then_inc(sem("decay_turned"), 1)
                pe.wait_ge(sem("m_ready"), 1)
                for u in range(8):
                    last = pe.transpose(bank2(0)[:, u, :], m_gd[:, u, :], ident[:, :])
                last.then_inc(sem("m_turned"), 1)

            def gdn_invert(lv):
                pe.wait_ge(sem("inv_ready"), lv + 1)
                pe.wait_ge(sem("ct_ready"), lv + 1)
                for u in range(8):
                    last = mm(bank2(2)[:, u, :], c_t[:, u, :], inv[:, u, :])
                last.then_inc(sem("cx"), 1)
                pe.wait_ge(sem("cx_copied"), lv + 1)
                for u in range(8):
                    if lv < 4:
                        mm(bank2(6)[:, u, :], inv_t[:, u, :], y_gd[:, u, :])
                    last = mm(bank2(0)[:, u, :], y_gd[:, u, :], inv_t[:, u, :])
                last.then_inc(sem("xcx"), 1)

            def gdn_solve():
                pe.wait_ge(sem("inv_ready"), 6)
                for t, h in ALL_UNITS:
                    m, u = u_of(t, h), t * HEADS + h
                    mm(PS[:, 2, u * DH:(u + 1) * DH], inv_t[:, m, :], vb[:, u, :])
                    a = 64 * (h % 2)
                    at = (h // 2) * TOK + t * P
                    last = mm(PS[a:a + 64, 3, at:at + P], kbg[:, u, :], inv_t[:, m, :])
                last.then_inc(sem("solved"), 1)

            def gdn_chunk(c):
                t, half = divmod(c, 2)
                r = slice(64 * half, 64 * half + 64)
                tok = slice(c * CHUNK, (c + 1) * CHUNK)
                pe.wait_ge(sem("state_ready"), c + 1)
                if c == 0:
                    pe.wait_ge(sem("solution"), 1)
                for h in range(HEADS):
                    a = slice(64 * (h % 2), 64 * (h % 2) + 64)
                    bank, at = 3 * (h % 2), (h // 2) * DH
                    mm(PS[r, bank, at:at + DH], w_t[a, h // 2, tok], state[a, h // 2, :])
                    at += P * (1 + t)
                    last = mm(PS[r, bank, at:at + DH], qi_t[a, h // 2, tok], state[a, h // 2, :])
                last.then_inc(sem("w_state"), 1)
                pe.wait_ge(sem("v_new"), c + 1)
                for h in range(HEADS):
                    a = slice(64 * (h % 2), 64 * (h % 2) + 64)
                    u = t * HEADS + h
                    mm(PS[r, 1, u * DH:(u + 1) * DH], a_qk[r, u_of(t, h), 64 * half:64 * half + 64], v_new[r, u, :])
                    last = mm(PS[a, 2, (h // 2) * DH:(h // 2 + 1) * DH], ko[r, u, :], v_new[r, u, :])
                last.then_inc(sem("chunk_done"), 1)

            def fox():
                pe.wait_ge(sem("fox_normed"), 1)
                for s in range(2):
                    for pair in range(2):
                        for t in range(TT):
                            last = pe.transpose(PS[:, s, pair * TOK + t * P:pair * TOK + (t + 1) * P],
                                                tokm[:, t, s, pair * P:(pair + 1) * P], ident[:, :])
                last.then_inc(sem("fox_turned"), 1)
                pe.wait_ge(sem("fox_copied"), 1)
                for h in range(HEADS):
                    a = slice(64 * (h % 2), 64 * (h % 2) + 64)
                    q, k = fq_t[a, h // 2, :], fk_t[a, h // 2, :]
                    n0 = nlf[:, 0, h:h + 1].to_broadcast([P, P])
                    n1 = nlf[:, 1, h:h + 1].to_broadcast([P, P])
                    hh, pair = h % 2, h // 2
                    o = PS[:, 2 + hh, pair * P:(pair + 1) * P]
                    mm(o, q[:, 0:P], k[:, 0:P], True, False)
                    mm(o, n0, mask("tri"), False, False)
                    mm(o, ident[:, :], mask("fox_add"), False, True)
                    o = PS[:, hh, pair * TOK:(pair + 1) * TOK]
                    tri_ones = masks[:, MASK["tri"]:MASK["tri"] + 2, :].rearrange("p a n -> p (a n)")
                    mm(o, q[:, P:TOK], k, True, False)
                    mm(o, n0, tri_ones, False, False)
                    mm(o[:, P:TOK], n1, mask("tri"), False, False)
                    last = mm(o[:, P:TOK], ident[:, :], mask("fox_add"), False, True)
                last.then_inc(sem("fox_logits"), 1)
                pe.wait_ge(sem("fox_probs"), 8)
                for h in range(HEADS):
                    pe.transpose(PS[:, 3, h * P:(h + 1) * P], probs0[:, h, :], ident[:, :])
                    for j in range(2):
                        last = pe.transpose(PS[:, 6 + h // 2, ((h % 2) * 2 + j) * P:((h % 2) * 2 + j + 1) * P],
                                            probs1[:, h, j * P:(j + 1) * P], ident[:, :])
                last.then_inc(sem("fox_probs_turned"), 1)
                pe.wait_ge(sem("fox_probs_copied"), 2)
                for h in range(HEADS):
                    v = lambda t: tokm[:, t, TOKM["fox_v"], h * DH:(h + 1) * DH]
                    mm(PS[:, 2, h * DH:(h + 1) * DH], probs_t[:, h, :], v(0))
                    o = PS[:, 2, 256 + h * DH:256 + (h + 1) * DH]
                    mm(o, probs_t[:, 4 + 2 * h, :], v(0), True, False)
                    last = mm(o, probs_t[:, 5 + 2 * h, :], v(1), False, True)
                last.then_inc(sem("fox_out"), 1)

            def la_keys():
                pe.wait_ge(sem("hg_keys"), 1)
                for f in range(2):
                    for t in range(TT):
                        last = pe.transpose(PS[:, 6, f * TOK + t * P:f * TOK + (t + 1) * P],
                                            tokm[:, t, TOKM["hg_f"], f * P:(f + 1) * P], ident[:, :])
                last.then_inc(sem("hg_keys_turned"), 1)

            exps = PS[:, 6:8, :].rearrange("p b n -> p (b n)")

            def la_exponents(lv):
                if lv:
                    pe.wait_ge(sem("level_exp"), lv)
                else:
                    pe.wait_ge(sem("la_ready"), 1)
                for f in range(3):
                    for t in range(TT):
                        m = mask(f"e{1 << lv}") if lv < 7 else mask("after" if t == 0 else "tri")
                        last = mm(exps[:, f * TOK + t * P:f * TOK + (t + 1) * P], la[:, t, f, :], m)
                last.then_inc(sem("exps"), 1)

            def la_rows(h):
                if h < 4:
                    return slice(64 * (h % 2), 64 * (h % 2) + 64), h // 2
                return slice(32 * (h - 4), 32 * (h - 4) + 32), 2

            def la_pairs(lv):
                if lv >= 0:
                    pe.wait_ge(sem("level_operand"), lv + 1)
                if lv >= 0:
                    pe.wait_ge(sem("pairs_read"), lv + 1)
                for h in range(8):
                    r, f = la_rows(h)
                    k, q = ((chm[r, 9 + f, :], chm[r, 6 + f, :]) if lv < 0 else
                            (z_lv[r, lv % 2, f * TOK:(f + 1) * TOK],) * 2)
                    if lv < 7:
                        for t in range(TT):
                            c = slice(t * P, (t + 1) * P)
                            last = mm(pair_bank(t, h), k[:, c], q[:, c])
                    else:
                        last = mm(pair_bank(0, h), k[:, 0:P], q[:, P:TOK])
                last.then_inc(sem("pairs"), 1)

            def la_all():
                pe.wait_ge(sem("la_keys"), 1)
                la_exponents(0)
                pe.wait_ge(sem("pairs_free"), 1)
                la_pairs(-1)
                for lv in range(8):
                    if lv < 7:
                        la_exponents(lv + 1)
                    la_pairs(lv)
                pe.wait_ge(sem("pairs_read"), 9)
                for h in range(8):
                    src = tokm[:, :, TOKM["hg_i"] if h < 4 else TOKM["gla_v"], (h % 4) * DH:(h % 4 + 1) * DH]
                    o = lambda t: PS[:, 6 + h // 4, t * 256 + (h % 4) * DH:t * 256 + (h % 4 + 1) * DH]
                    mm(o(0), a_la[:, la_unit(0, h), :], src[:, 0, :])
                    mm(o(1), a_top[:, la_top_unit(h), :], src[:, 0, :], True, False)
                    last = mm(o(1), a_la[:, la_unit(1, h), :], src[:, 1, :], False, True)
                last.then_inc(sem("la_out"), 1)

            between = {0: [gates], 3: [gdn_tokens, gdn_channels], 4: [gdn_grams],
                       5: [lambda: gdn_invert(0)], 6: [lambda: gdn_invert(1)], 7: [lambda: gdn_invert(2)],
                       8: [lambda: gdn_invert(3)], 9: [lambda: gdn_invert(4)], 10: [gdn_solve],
                       11: [lambda: gdn_chunk(0)], 12: [lambda: gdn_chunk(1)], 13: [lambda: gdn_chunk(2)],
                       14: [lambda: gdn_chunk(3), fox, la_keys, la_all]}
            for n, what in enumerate(MIX_ORDER):
                if n >= 2:
                    pe.wait_ge(sem(f"proj_bank_read{n % 2}"), n // 2)
                columns(n, n % RING, 4 + n % 2, (h_hi, h_lo), what in CHANNEL_MAJOR, SMALL if n == 0 else 256)
                for piece in between.get(n, ()):
                    piece()

            pe.wait_ge(sem("tokens_ready"), 2)
            turn("mixed", xn, 8)
            operand_ready("mixed")

            def rows_4(name, acc, operand):
                for j in range(4):
                    n = STEP[name] + j
                    row_block(n, n % RING, acc, operand, 2 * j, j == 0, j == 3)

            rows_4("mix_out", low4, (act_hi, act_lo))

            def ffn(f):
                n0 = STEP[f"ffn{f}"]
                slot = lambda j: (n0 + j) % RING
                columns(n0, slot(0), 4, (h_hi, h_lo))
                columns(n0 + 1, slot(1), 5, (h_hi, h_lo))
                for t in range(TT):
                    for half in range(2):
                        pe.matmul(low4[:, t, half * 512:(half + 1) * 512], zeros_r[:, 0:P], zeros_r[:, :],
                                  start=True, stop=False, skip_group_check=True)
                with pe.Fori(1, PAIRS) as i:
                    n = n0 - 1 + 3 * i
                    pe.wait_ge(sem("gate_convolved"), PAIRS * f + i)
                    columns(n, slot(2), 4, (h_hi, h_lo))
                    pe.wait_ge(sem("up_read"), PAIRS * f + i)
                    columns(n + 1, slot(0), 5, (h_hi, h_lo))
                    pe.wait_ge(sem("hidden_split"), PAIRS * f + i)
                    row_block(n + 2, slot(1), low4, (hid_hi, hid_lo), 0, False, False)
                pe.wait_ge(sem("hidden_split"), PAIRS * (f + 1))
                n = n0 + 3 * PAIRS - 1
                row_block(n, n % RING, low4, (hid_hi, hid_lo), 0, False, True)

            pe.wait_ge(sem("zeros"), 1)
            pe.wait_ge(sem("tokens_ready"), 3)
            turn("norm2", xn, 8)
            operand_ready("norm2")
            ffn(0)

            pe.wait_ge(sem("tokens_ready"), 4)
            turn("pre_mix0", xn, 8)
            operand_ready("pre_mix0")
            pe.wait_ge(sem("table_loaded"), 32)
            mm(PS[0:N_HEADS, 7, 0:N_DIST], table, onehot).then_inc(sem("bias_by_head"), 1)
            n0 = STEP["sc_in"]
            with pe.Fori(0, 4) as i:
                for j in range(3):
                    pe.wait_ge(sem("sc_bank_read"), 3 * i + (j + 1))
                    columns(n0 + j + 3 * i, (n0 + j) % RING, 4 + j, (h_hi, h_lo))
            pe.wait_ge(sem("sc_hidden"), 4)
            rows_4("sc_out", low4, (act_hi, act_lo))

            def ffn_and_ple(layer):
                pe.wait_ge(sem("tokens_ready"), 5 if layer == 0 else 9)
                turn(f"pre_ffn{layer}", xn, 8)
                operand_ready(f"pre_ffn{layer}")
                ffn(1 + layer)
                pe.wait_ge(sem("p_loaded"), 16 * (layer + 1))
                turn(f"p{layer}", p_tok, 2)
                operand_ready(f"p{layer}")
                pe.wait_ge(sem("low4_read"), layer + 1)
                n = STEP[f"ple_proj{layer}"]
                row_block(n, n % RING, low4, (p_hi, p_lo), 0, True, True)
                pe.wait_ge(sem("tokens_ready"), 6 if layer == 0 else 10)
                turn(f"pre_ple{layer}", xn, 8)
                operand_ready(f"pre_ple{layer}")
                rows_4(f"ple_gate{layer}", high4, (h_hi, h_lo))

            ffn_and_ple(0)

            pe.wait_ge(sem("tokens_ready"), 7)
            turn("pre_mix1", xn, 8)
            operand_ready("pre_mix1")
            pe.wait_ge(sem("flip_loaded"), 16)
            pe.wait_ge(sem("bias_loaded"), 16)
            for b in range(4):
                last = mm(PS[:, b, :], flip, bias_rev[:, 2 * b:2 * b + 2, :].rearrange("p h n -> p (h n)"))
            last.then_inc(sem("bias_flipped"), 1)
            for j in range(4):
                n = STEP["att_k"] + j
                if j >= 2:
                    pe.wait_ge(sem(f"att_bank_read{j % 2}"), j // 2)
                columns(n, n % RING, 4 + j % 2, (act_hi, act_lo))
            pe.wait_ge(sem("bias_copied"), 1)
            rows_4("att_v", low4, (act_hi, act_lo))
            for j in range(4):
                n = STEP["att_q"] + j
                pe.wait_ge(sem(f"att_bank_read{j % 2}"), 2 + j // 2)
                columns(n, n % RING, 4 + j % 2, (h_hi, h_lo))
            for h in range(N_HEADS):
                if h:
                    pe.wait_ge(sem("logits_read"), h)
                else:
                    pe.wait_ge(sem("heads_ready"), 1)
                for m in range(2):
                    r = slice(64 * m, 64 * m + 64)
                    mm(PS[:, 6 + m, 0:TOK], q_t[r, h, P:TOK], k_t[r, h, :])
                    last = mm(PS[:, 6 + m, TOK:TOK + P], q_t[r, h, 0:P], k_t[r, h, 0:P])
                last.then_inc(sem("logits"), 1)
                pe.wait_ge(sem("att_weights"), h + 1)
                if h:
                    pe.wait_ge(sem("head_read"), h)
                for j in range(3):
                    last = pe.transpose(PS[:, 4, j * P:(j + 1) * P], at_w[:, j, :], ident[:, :])
                last.then_inc(sem("att_turned"), 1)
                pe.wait_ge(sem("att_copied"), h + 1)
                v = lambda t: v_tok[:, t, h * P:(h + 1) * P]
                mm(PS[:, 5, P:TOK], at_wt[:, 0, :], v(0), True, False)
                mm(PS[:, 5, P:TOK], at_wt[:, 1, :], v(1), False, True)
                last = mm(PS[:, 5, 0:P], at_wt[:, 2, :], v(0))
                last.then_inc(sem("head_out"), 1)
            pe.wait_ge(sem("tokens_ready"), 8)
            turn("att", xn, 8)
            operand_ready("att")
            rows_4("att_out", low4, (act_hi, act_lo))
            ffn_and_ple(1)

        @block.scalar
        def _(act):
            own, count = sem("act_own"), [0]

            def mark(ins):
                count[0] += 1
                ins.then_inc(own, 1)

            def link(ins):
                mark(ins)
                act.wait_ge(own, count[0])

            def split(n, slot, lap, steady=True):
                act.wait_ge(raw_loaded[slot], 16 * lap)
                if steady:
                    act.wait_ge(block_used, n - (RING - 1))
                act.activation(w_hi[:, slot, :], raw[:, slot, :], ACT.Copy).then_inc(hi_ready, 1)

            def ahead(n):
                if n + 2 < N_BLOCKS:
                    split(n + 2, (n + 2) % RING, (n + 2) // RING + 1, n + 2 >= RING)

            def ahead_in_loop(n_base, i):
                m = n_base + 2
                split(m + 3 * i, m % RING, i + (m // RING + 1))

            def norm_stats(k, src1):
                s = stat[:, 2 * (k % 2):2 * (k % 2) + 2]
                act.activation(junk_of(k), src1, ACT.Square, accum_out=s[:, 1:2]).then_inc(own, 1)
                count[0] += 1
                act.wait_ge(own, count[0])
                act.wait_ge(sem("squares0"), k + 1)
                link(act.activation(s, s, ACT.Ln, scale=1.0 / D, bias=eps[:, :]))
                act.activation(s, s, ACT.Exp, scale=-0.5).then_inc(sem("rstd"), 1)

            def junk_of(k):
                return sq[:, 0:D] if k == 0 else junk[:, 1, :]

            def turned(name, chunks, operands):
                c0, p0, _ = TURN[name]
                for b in range(chunks // 2):
                    act.wait_ge(chunks_turned, c0 + 2 * b + 2)
                    for gain, hi, _ in operands:
                        for j in (2 * b, 2 * b + 1):
                            src = PS[:, 4 + b, (j % 2) * TOK:(j % 2 + 1) * TOK]
                            if gain is None:
                                ins = act.activation(hi[:, j, :], src, ACT.Copy)
                            else:
                                ins = act.activation(hi[:, j, :], src, ACT.Identity, scale=gain(j))
                    ins.then_inc(part_hi, 1)

            act.preload_act_table_set(TABLES)
            act.wait_ge(inputs, N_INPUTS)
            act.wait_ge(sem("eps_set"), 1)
            norm_stats(0, x[:, 1, :])
            split(0, 0, 1, False)
            split(1, 1, 1, False)
            turned("norm1", 8, [(lambda j: ch("norm1", j), h_hi, h_lo)])

            def gates():
                act.wait_ge(sem("gates_z"), 1)
                act.wait_ge(sem("mix_inputs"), 48)
                link(act.activation(gate_l, gate_z, ACT.Abs))
                link(act.activation(gate_l, gate_l, ACT.Exp, scale=-1.0))
                act.activation(gate_l, gate_l, ACT.Ln, bias=1.0)
                act.activation(ea, rows("gdn_a_log", 4), ACT.Exp)
                act.activation(beta, small[:, :, 8:12], ACT.Exp, scale=-1.0).then_inc(sem("gates_exp"), 1)
                act.wait_ge(sem("gate_sums"), 1)
                act.activation(th(e_g), PS[:, 0, 0:8], ACT.Exp)
                act.activation(th(e_rest), PS[:, 0, 8:16], ACT.Exp)
                act.activation(e_last.rearrange("p t c h -> p (t c h)"), PS[:, 0, 16:32], ACT.Exp) \
                    .then_inc(sem("gate_exps"), 1)
                act.wait_ge(sem("gk_turned"), 1)
                act.activation(gk_t, PS[0:16, 1, 0:TOK], ACT.Copy).then_inc(sem("gk_copied"), 1)
                log_sigmoid(la[:, :, 2, :], 1)

            def log_sigmoid(dst, k):
                act.wait_ge(sem("logits_z"), k)
                s = sq[:, (k - 1) * 512:(k - 1) * 512 + dst.shape[1] * dst.shape[2]].rearrange("p (t n) -> p t n", t=TT)
                link(act.activation(s, dst, ACT.Abs))
                link(act.activation(s, s, ACT.Exp, scale=-1.0))
                act.activation(s, s, ACT.Ln, bias=1.0).then_inc(sem("logits_ln"), 1)

            def gdn_tokens():
                act.wait_ge(sem("gdn_taps"), 1)
                v = chm[:, 0:6, :].rearrange("p f n -> p (f n)")
                act.activation(v, v, ACT.Silu).then_inc(sem("gdn_convolved"), 1)
                act.preload_act_table_set(TABLES)
                act.wait_ge(sem("gdn_token_major"), 1)
                act.wait_ge(sem("sq_free"), 1)
                act.activation(sq, PS[:, 0:2, :].rearrange("p b n -> p (b n)"), ACT.Square).then_inc(sem("gdn_squares"), 1)
                rstd16("gdn_sums", "gdn_rstd", 1.0)

            def rstd16(ready, done, scale, n=16):
                act.wait_ge(sem(ready), 1)
                s = stat[:, 8:8 + n]
                link(act.activation(s, s, ACT.Ln, scale=scale, bias=eps[:, :]))
                act.activation(s, s, ACT.Exp, scale=-0.5).then_inc(sem(done), 1)

            def gdn_channels():
                act.wait_ge(sem("gdn_channel_major"), 1)
                act.activation(chm[:, 0:6, :].rearrange("p f n -> p (f n)"),
                               PS[:, 0:3, :].rearrange("p b n -> p (b n)"), ACT.Copy).then_inc(sem("gdn_copied"), 1)

            bank2 = lambda b: PS[:, b:b + 2, :].rearrange("p b n -> p (b n)")
            flat = lambda v: v.rearrange("p u n -> p (u n)")

            def gdn_grams():
                act.wait_ge(sem("decay_logs"), 1)
                act.activation(flat(dec), bank2(2), ACT.Exp).then_inc(sem("decay"), 1)
                act.wait_ge(sem("decay_turned"), 1)
                act.activation(flat(dec_t), bank2(2), ACT.Copy).then_inc(sem("decay_t"), 1)
                act.wait_ge(sem("m_turned"), 1)
                act.activation(flat(mt_gd), bank2(0), ACT.Copy).then_inc(sem("mt_ready"), 1)

            def gdn_invert(lv):
                act.wait_ge(sem("cx"), lv + 1)
                act.activation(flat(y_gd), bank2(2), ACT.Copy).then_inc(sem("cx_copied"), 1)

            def gdn_solve():
                act.wait_ge(sem("solved"), 1)
                act.activation(flat(u_gd), PS[:, 2, :], ACT.Copy)
                act.activation(flat(w_t), PS[:, 3, :], ACT.Copy).then_inc(sem("solution"), 1)

            def head_post(k, grp):
                act.wait_ge(sem("group_out"), k + 1)
                act.activation(sq[:, 0:512].rearrange("p (t n) -> p t n", t=TT), group_view(grp), ACT.Square) \
                    .then_inc(sem("group_squares"), 1)
                act.wait_ge(sem("group_sums"), k + 1)
                s = stat[:, 8:16]
                link(act.activation(s, s, ACT.Ln, scale=1.0 / DH, bias=eps[:, :]))
                act.activation(s, s, ACT.Exp, scale=-0.5).then_inc(sem("group_rstd"), 1)

            def silu_gates():
                act.wait_ge(sem("proj_bank_read0"), 8)
                act.wait_ge(sem("proj_bank_read1"), 7)
                act.activation(tokm[:, :, 6:9, :], tokm[:, :, 6:9, :], ACT.Silu)
                act.activation(chm[:, 6:8, :], chm[:, 6:8, :], ACT.Silu).then_inc(sem("gates_silu"), 1)
                act.preload_act_table_set(TABLES)

            def fox():
                act.wait_ge(sem("sq_free"), 3)
                act.activation(sq.rearrange("p (t s n) -> p t s n", t=TT, s=2), tokm[:, :, 0:2, :], ACT.Square) \
                    .then_inc(sem("fox_squares"), 1)
                rstd16("fox_sums", "fox_rstd", 1.0 / DH)
                act.wait_ge(sem("fox_turned"), 1)
                act.activation(flat(fq_t), PS[:, 0, :], ACT.Copy)
                act.activation(flat(fk_t), PS[:, 1, :], ACT.Copy).then_inc(sem("fox_copied"), 1)
                act.wait_ge(sem("fox_max"), 2)
                for h in range(HEADS):
                    m = (h % 2) * 2 + h // 2
                    act.activation(probs0[:, h, :], PS[:, 2 + h % 2, h // 2 * P:(h // 2 + 1) * P], ACT.Exp,
                                   bias=stat[:, 24 + m:25 + m],
                                   accum_out=stat[:, 32 + h:33 + h]).then_inc(sem("fox_probs"), 1)
                    act.activation(probs1[:, h, :], PS[:, h % 2, h // 2 * TOK:(h // 2 + 1) * TOK], ACT.Exp,
                                   bias=stat[:, 28 + m:29 + m], accum_out=stat[:, 36 + h:37 + h]) \
                        .then_inc(sem("fox_probs"), 1)
                act.wait_ge(sem("fox_probs_turned"), 1)
                act.activation(flat(probs_t[:, 0:4, :]), PS[:, 3, :], ACT.Copy).then_inc(sem("fox_probs_copied"), 1)
                act.activation(flat(probs_t[:, 4:12, :]), bank2(6), ACT.Copy).then_inc(sem("fox_probs_copied"), 1)

            def la_keys():
                log_sigmoid(tokm[:, :, TOKM["hg_f"], :], 2)
                act.wait_ge(sem("hg_keys_log"), 1)
                z = tokm[:, :, TOKM["hg_f"], :]
                act.activation(z, z, ACT.Exp).then_inc(sem("hg_keys"), 1)
                act.wait_ge(sem("hg_keys_turned"), 1)
                act.activation(chm[:, 9:11, :].rearrange("p f n -> p (f n)"), PS[:, 6, :], ACT.Copy) \
                    .then_inc(sem("la_keys"), 1)

            def la_all():
                for lv in range(8):
                    act.wait_ge(sem("exps"), lv + 1)
                    if lv >= 2:
                        act.wait_ge(sem("level_operand"), lv - 1)
                    act.activation(w_lv[:, lv % 2, :], bank2(6)[:, 0:768], ACT.Exp).then_inc(sem("level_exp"), 1)

            between = {0: [gates], 3: [gdn_tokens, gdn_channels], 4: [gdn_grams],
                       5: [lambda: gdn_invert(0)], 6: [lambda: gdn_invert(1)], 7: [lambda: gdn_invert(2)],
                       8: [lambda: gdn_invert(3)], 9: [lambda: gdn_invert(4)], 10: [gdn_solve],
                       14: [silu_gates, lambda: head_post(0, 1), fox, lambda: head_post(1, 0), la_keys, la_all,
                            lambda: head_post(2, 2), lambda: head_post(3, 3)]}
            for n, what in enumerate(MIX_ORDER):
                ahead(n)
                act.wait_ge(block_used, n + 1)
                bank = PS[:, 4 + n % 2, :]
                read = sem(f"proj_bank_read{n % 2}")
                if what == "small":
                    act.activation(small, bank.rearrange("p (t n) -> p t n", t=TT)[:, :, 0:SMALL], ACT.Copy) \
                        .then_inc(read, 1)
                elif what.startswith("gdn_") and what in CHANNEL_MAJOR:
                    s = ("gdn_q", "gdn_k", "gdn_v").index(what)
                    for f in range(2):
                        ins = act.activation(chm[:, 2 * s + f, :], bank[:, f * TOK:(f + 1) * TOK], ACT.Identity,
                                             scale=ch("gdn_conv", 3 * 6 + 2 * s + f))
                    ins.then_inc(sem("gdn_last_tap"), 1)
                elif what == "hg_q":
                    act.activation(chm[:, 6:8, :].rearrange("p f n -> p (f n)"), bank, ACT.Copy).then_inc(read, 1)
                elif what == "gla_qk":
                    act.activation(chm[:, 8, :], bank[:, 0:TOK], ACT.Copy, scale=32.0 ** -0.5)
                    act.activation(chm[:, 11, :], bank[:, TOK:512], ACT.Copy).then_inc(read, 1)
                else:
                    act.activation(tokm[:, :, TOKM[what], :], bank.rearrange("p (t n) -> p t n", t=TT), ACT.Copy) \
                        .then_inc(read, 1)
                for piece in between.get(n, ()):
                    piece()

            turned("mixed", 8, [(None, act_hi, act_lo)])

            def ahead_4(name):
                for j in range(4):
                    ahead(STEP[name] + j)

            ahead_4("mix_out")

            def residual_norm(k):
                act.wait_ge(sem("x_ready"), k)
                norm_stats(k, x[:, 1, :])

            residual_norm(1)
            turned("norm2", 8, [(lambda j: ch("norm2", j), h_hi, h_lo)])

            def ffn(f):
                n0 = STEP[f"ffn{f}"]
                conv = PC[f"ffn_conv{f}"]

                def last_tap(dst, bank, i, half, ready):
                    for c in range(2):
                        col = i * 2 + (half * FT + c)
                        w = channel[:, bass.ds(col + (conv + 2 * 2 * FT), 1)]
                        b = channel[:, bass.ds(col + PC["ffn_bias"], 1)] if f == 0 else 0.0
                        ins = act.activation(dst[:, c, :], PS[:, bank, c * TOK:(c + 1) * TOK], ACT.Identity,
                                             scale=w, bias=b)
                    ins.then_inc(ready, 1)

                def gate(i, n_used):
                    act.wait_ge(block_used, n_used)
                    last_tap(y_gate, 4, i, 0, sem("gate_last_tap"))

                def up(i, n_used):
                    act.wait_ge(sem("gate_convolved"), i + (PAIRS * f + 1))
                    act.activation(s_gate, y_gate, ACT.Silu).then_inc(sem("gate_silu"), 1)
                    act.wait_ge(block_used, n_used)
                    last_tap(y_up, 5, i, 1, sem("up_last_tap"))

                def hid(i):
                    act.wait_ge(sem("hidden_ready"), i + (PAIRS * f + 1))
                    act.activation(hid_hi, hidden, ACT.Copy).then_inc(sem("hidden_hi"), 1)

                ahead(n0)
                gate(0, n0 + 1)
                ahead(n0 + 1)
                up(0, n0 + 2)
                hid(0)
                with act.Fori(1, PAIRS) as i:
                    n = n0 - 1
                    ahead_in_loop(n, i)
                    gate(i, n + 1 + 3 * i)
                    ahead_in_loop(n + 1, i)
                    up(i, n + 2 + 3 * i)
                    ahead_in_loop(n + 2, i)
                    act.wait_ge(block_used, n + 3 + 3 * i)
                    hid(i)
                ahead(n0 + 3 * PAIRS - 1)
                act.preload_act_table_set(TABLES)

            ffn(0)

            residual_norm(2)
            turned("pre_mix0", 8, [(lambda j: ch("pre_mix0", j), h_hi, h_lo)])
            act.wait_ge(sem("bias_by_head"), 1)
            act.activation(bias_row, PS[0:N_HEADS, 7, 0:N_DIST], ACT.Copy).then_inc(sem("bias_rows"), 1)
            n0 = STEP["sc_in"]
            with act.Fori(0, 4) as i:
                ahead_in_loop(n0, i)
                act.wait_ge(block_used, n0 + 1 + 3 * i)
                act.activation(flat(s_gate), PS[:, 4, :], ACT.Copy).then_inc(sem("sc_gc"), 1)
                ahead_in_loop(n0 + 1, i)
                act.wait_ge(sem("sc_product"), i + 1)
                for c in range(2):
                    ins = act.activation(y_gate[:, c, :], y_up[:, c, :], ACT.Identity,
                                         scale=channel[:, bass.ds(2 * i + (PC["sc_conv"] + 16 + c), 1)])
                ins.then_inc(sem("sc_last_tap"), 1)
                ahead_in_loop(n0 + 2, i)
                act.wait_ge(sem("sc_gated"), i + 1)
                act.activation(act_hi[:, bass.ds(2 * i, 2), :], hidden, ACT.Copy).then_inc(sem("sc_hi"), 1)
            ahead_4("sc_out")

            posts = [0]

            def post_norm(n_used, acc):
                q = posts[0]
                posts[0] += 1
                if n_used is not None:
                    act.wait_ge(block_used, n_used)
                s = stat[:, 4:6]
                for t in range(TT):
                    mark(act.activation(junk[:, t, :], acc[:, t, :], ACT.Square, accum_out=s[:, t:t + 1]))
                act.wait_ge(own, count[0])
                link(act.activation(s, s, ACT.Ln, scale=1.0 / D, bias=eps[:, :]))
                act.activation(s, s, ACT.Exp, scale=-0.5).then_inc(sem("post_rstd"), 1)

            post_norm(STEP["sc_out"] + 4, low4)
            residual_norm(3)
            turned("pre_ffn0", 8, [(lambda j: ch("pre_ffn0", j), h_hi, h_lo)])

            def ffn_and_ple(layer, k):
                ffn(1 + layer)
                turned(f"p{layer}", 2, [(None, p_hi, p_lo)])
                post_norm(STEP[f"ffn{1 + layer}"] + 3 * PAIRS, low4)
                residual_norm(k)
                turned(f"pre_ple{layer}", 8, [(lambda j: ch(f"pre_ple{layer}", j), h_hi, h_lo)])
                ahead(STEP[f"ple_proj{layer}"])
                for j in range(4):
                    ahead(STEP[f"ple_gate{layer}"] + j)
                act.wait_ge(block_used, STEP[f"ple_gate{layer}"] + 4)
                act.activation(gate_s, high4, ACT.Sigmoid).then_inc(sem("ple_gate"), 1)
                act.preload_act_table_set(TABLES)
                act.wait_ge(sem("ple_product"), layer + 1)
                post_norm(None, gate_s)

            ffn_and_ple(0, 4)
            residual_norm(5)
            turned("pre_mix1", 8, [(lambda j: ch("pre_mix1", j), h_hi, h_lo), (lambda j: ch("kv", j), act_hi, act_lo)])
            act.wait_ge(sem("bias_flipped"), 1)
            act.activation(flat(bias_t), PS[:, 0:4, :].rearrange("p b n -> p (b n)"), ACT.Copy) \
                .then_inc(sem("bias_copied"), 1)
            act.wait_ge(sem("lambda_sums"), 1)
            act.activation(lam[:, 0:2], lam[:, 0:2], ACT.Exp).then_inc(sem("lambda_exps"), 1)
            for j in range(4):
                n = STEP["att_k"] + j
                ahead(n)
                act.wait_ge(block_used, n + 1)
                act.activation(flat(k_t[:, 2 * j:2 * j + 2, :]), PS[:, 4 + j % 2, :], ACT.Copy) \
                    .then_inc(sem(f"att_bank_read{j % 2}"), 1)
            for j in range(4):
                ahead(STEP["att_v"] + j)
            act.wait_ge(block_used, STEP["att_v"] + 4)
            act.activation(v_tok, low4, ACT.Copy)
            for j in range(4):
                n = STEP["att_q"] + j
                ahead(n)
                act.wait_ge(block_used, n + 1)
                ins = act.activation(flat(q_t[:, 2 * j:2 * j + 2, :]), PS[:, 4 + j % 2, :], ACT.Copy, scale=DH ** -0.5)
                ins.then_inc(sem(f"att_bank_read{j % 2}" if j < 3 else "heads_ready"), 1)
            for h in range(N_HEADS):
                act.wait_ge(sem("att_max"), 2 * (h + 1))
                a = att_stat
                for m in range(2):
                    act.activation(lg1[:, m, :], lg1[:, m, :], ACT.Exp, bias=a[:, m:m + 1], accum_out=a[:, 4 + m:5 + m])
                    ins = act.activation(lg0[:, m, :], lg0[:, m, :], ACT.Exp, bias=a[:, 2 + m:3 + m],
                                         accum_out=a[:, 6 + m:7 + m])
                ins.then_inc(sem("att_exp"), 1)
                act.wait_ge(sem("att_turned"), h + 1)
                act.activation(flat(at_wt), PS[:, 4, 0:384], ACT.Copy).then_inc(sem("att_copied"), 1)
            act.wait_ge(sem("subln_sums"), 1)
            s = stat[:, 8:24]
            link(act.activation(s, s, ACT.Ln, scale=1.0 / P, bias=eps[:, :]))
            act.activation(s, s, ACT.Exp, scale=-0.5).then_inc(sem("subln_rstd"), 1)
            turned("att", 8, [(lambda j: ch("subln"), act_hi, act_lo)])
            ahead_4("att_out")
            post_norm(STEP["att_out"] + 4, low4)
            residual_norm(6)
            turned("pre_ffn1", 8, [(lambda j: ch("pre_ffn1", j), h_hi, h_lo)])
            ffn_and_ple(1, 7)

        @block.vector
        def _(dve):
            own, count = sem("dve_own"), [0]

            def mark(ins):
                count[0] += 1
                ins.then_inc(own, 1)

            def settle():
                dve.wait_ge(own, count[0])

            def link(ins):
                mark(ins)
                settle()

            def signal(which, n=1):
                settle()
                dve.sem_inc(which, n)

            tt, ts, stt = dve.tensor_tensor, dve.tensor_scalar, dve.scalar_tensor_tensor

            def split(n, slot):
                dve.wait_ge(hi_ready, n + 1)
                tt(w_lo[:, slot, :], raw[:, slot, :], w_hi[:, slot, :].bitcast(F), ALU.subtract).then_inc(lo_ready, 1)

            def ahead(n):
                if n + 2 < N_BLOCKS:
                    split(n + 2, (n + 2) % RING)

            def norm_rest(k, junk0):
                s = stat[:, 2 * (k % 2):2 * (k % 2) + 2]
                dve.tensor_tensor_reduce(junk0, x[:, 0, :], x[:, 0, :], 1.0, 0.0, ALU.mult, ALU.add, s[:, 0:1]) \
                    .then_inc(sem("squares0"), 1)
                dve.wait_ge(sem("rstd"), k + 1)
                mark(ts(xn[:, 0, :], x[:, 0, :], s[:, 0:1], None, ALU.mult))
                ts(xn[:, 1, :], x[:, 1, :], s[:, 1:2], None, ALU.mult).then_inc(sem("tokens_ready"), 1)

            def turned(name, chunks, operands):
                c0, p0, _ = TURN[name]
                for b in range(chunks // 2):
                    dve.wait_ge(part_hi, p0 + b + 1)
                    for gain, hi, lo in operands:
                        for j in (2 * b, 2 * b + 1):
                            src = PS[:, 4 + b, (j % 2) * TOK:(j % 2 + 1) * TOK]
                            if gain is None:
                                ins = tt(lo[:, j, :], src, hi[:, j, :].bitcast(F), ALU.subtract)
                            else:
                                ins = stt(lo[:, j, :], src, gain(j), hi[:, j, :].bitcast(F), ALU.mult, ALU.subtract)
                    ins.then_inc(part_ready, 1)

            dve.wait_ge(inputs, N_INPUTS)
            norm_rest(0, z_lv.rearrange("p a n -> p (a n)")[:, 0:D])
            split(0, 0)
            split(1, 1)
            turned("norm1", 8, [(lambda j: ch("norm1", j), h_hi, h_lo)])

            def sigmoid_rest(v):
                link(ts(v, v, 1.0, None, ALU.add))
                dve.reciprocal(v, v)

            def gates():
                dve.wait_ge(sem("proj_bank_read0"), 1)
                dve.wait_ge(sem("mix_inputs"), 48)
                tt(gate_z, small[:, :, 0:8], row[:, 0:8].rearrange("p (o n) -> p o n", o=1).to_broadcast([P, TT, 8]),
                   ALU.add).then_inc(sem("gates_z"), 1)
                dve.wait_ge(sem("gates_exp"), 1)
                mark(stt(lf, gate_z[:, :, 0:4], 0.0, gate_l[:, :, 0:4], ALU.min, ALU.subtract))
                mark(stt(gd, gate_z[:, :, 4:8], 0.0, gate_l[:, :, 4:8], ALU.max, ALU.add))
                mark(ts(beta, beta, 1.0, None, ALU.add))
                settle()
                mark(ts(nlf, lf, -1.0, None, ALU.mult))
                mark(dve.reciprocal(beta, beta))
                mark(tt(ngd, gd, ea.rearrange("p (o n) -> p o n", o=1).to_broadcast([P, TT, 4]), ALU.mult))
                settle()
                ts(gd, ngd, -1.0, None, ALU.mult).then_inc(sem("gates_ready"), 1)
                dve.wait_ge(sem("gate_exps"), 1)
                mark(tt(be_g, beta, e_g, ALU.mult))
                dve.wait_ge(sem("gk_projected"), 1)
                b = rows("b_gk", P).rearrange("p (o n) -> p o n", o=1).to_broadcast([P, TT, P])
                ins = tt(la[:, :, 2, :], PS[:, 1, 256:512].rearrange("p (t n) -> p t n", t=TT), b, ALU.add)
                ins.then_inc(sem("logits_z"), 1)
                dve.wait_ge(sem("logits_z"), 1)
                dve.wait_ge(sem("logits_ln"), 1)
                s = sq[:, 0:256].rearrange("p (t n) -> p t n", t=TT)
                link(stt(la[:, :, 2, :], la[:, :, 2, :], 0.0, s, ALU.min, ALU.subtract))
                mark(ts(la[:, :, 2, :], la[:, :, 2, :], 1.0 / 16.0, None, ALU.mult))
                settle()
                signal(sem("gk_read"), 1)

            def gdn_taps(s, n):
                dve.wait_ge(sem("gdn_last_tap"), s + 1)
                for d in range(1, 4):
                    for f in range(2):
                        dst = chm[:, 2 * s + f, d:TOK]
                        mark(stt(dst, PS[:, 4 + n % 2, f * TOK:(f + 1) * TOK - d], ch("gdn_conv", (3 - d) * 6 + 2 * s + f),
                                 dst, ALU.mult, ALU.add))
                    settle()
                signal(sem(f"proj_bank_read{n % 2}"), 1)

            def gdn_tokens():
                signal(sem("gdn_taps"), 1)
                signal(sem("sq_free"), 1)
                dve.wait_ge(sem("gdn_squares"), 1)
                dve.tensor_reduce(stat[:, 8:24], sq.rearrange("p (u d) -> p u d", d=DH), AX, ALU.add) \
                    .then_inc(sem("gdn_sums"), 1)
                dve.wait_ge(sem("gdn_rstd"), 1)
                link(ts(stat[:, 8:16], stat[:, 8:16], DH ** -0.5, None, ALU.mult))
                psu = lambda b: PS[:, b, :].rearrange("p (u d) -> p u d", d=DH)
                mark(tt(qn, psu(0), unit(stat[:, 8:16], DH), ALU.mult))
                mark(tt(kn, psu(1), unit(stat[:, 16:24], DH), ALU.mult))
                mark(tt(vb, psu(2), unit(th(beta), DH), ALU.mult))
                settle()
                mark(tt(qi, qn, unit(th(e_g), DH), ALU.mult))
                mark(tt(kbg, kn, unit(th(be_g), DH), ALU.mult))
                settle()
                tt(ko, kn, unit(th(e_rest), DH), ALU.mult).then_inc(sem("gdn_normed"), 1)

            bank2 = lambda b: PS[:, b:b + 2, :].rearrange("p b n -> p (b n)").rearrange("p (u n) -> p u n", n=P)

            def gdn_grams():
                dve.wait_ge(sem("decay"), 1)
                for t, h in ALL_UNITS:
                    u = u_of(t, h)
                    ins = stt(m_gd[:, u, :], bank2(0)[:, u, :], beta[:, t, h:h + 1], dec[:, u, :], ALU.mult, ALU.mult)
                ins.then_inc(sem("m_ready"), 1)
                dve.wait_ge(sem("m_ready"), 1)
                dve.wait_ge(sem("decay_t"), 1)
                dve.wait_ge(sem("qk_gram"), 1)
                mark(tt(a_qk, bank2(6), dec_t, ALU.mult))
                dve.wait_ge(sem("mt_ready"), 1)
                mark(tt(inv, m_gd, units(mask("m1"), 8), ALU.mult))
                settle()
                mark(tt(inv_t, mt_gd, units(mask("t1"), 8), ALU.mult))
                mark(tt(inv, units(ident[:, :], 8), inv, ALU.subtract))
                settle()
                tt(inv_t, units(ident[:, :], 8), inv_t, ALU.subtract).then_inc(sem("inv_ready"), 1)
                tt(c_t, mt_gd, units(mask("t2"), 8), ALU.mult).then_inc(sem("ct_ready"), 1)

            def gdn_invert(lv):
                dve.wait_ge(sem("xcx"), lv + 1)
                if lv < 4:
                    tt(c_t, mt_gd, units(mask(f"t{4 << lv}"), 8), ALU.mult).then_inc(sem("ct_ready"), 1)
                    mark(tt(inv, inv, bank2(6), ALU.subtract))
                    settle()
                tt(inv_t, inv_t, bank2(0), ALU.subtract).then_inc(sem("inv_ready"), 1)

            def gdn_solve():
                dve.memset(state, 0.0).then_inc(sem("state_ready"), 1)
                dve.wait_ge(sem("solution"), 1)

            def gdn_chunk(c):
                t, half = divmod(c, 2)
                r = slice(64 * half, 64 * half + 64)
                dve.wait_ge(sem("w_state"), c + 1)
                for hh in range(2):
                    us = slice(t * 4 + hh, t * 4 + hh + 3, 2)
                    ins = tt(v_new[r, us, :], u_gd[r, us, :], PS[r, 3 * hh, 0:P].rearrange("p (h d) -> p h d", d=DH),
                             ALU.subtract)
                ins.then_inc(sem("v_new"), 1)
                dve.wait_ge(sem("chunk_done"), c + 1)
                if c == 3:
                    return
                for h in range(HEADS):
                    a = slice(64 * (h % 2), 64 * (h % 2) + 64)
                    s = state[a, h // 2, :]
                    ins = stt(s, s, e_last[a, t, half, h:h + 1], PS[a, 2, (h // 2) * DH:(h // 2 + 1) * DH],
                              ALU.mult, ALU.add)
                ins.then_inc(sem("state_ready"), 1)

            def head_out(grp, src, scale=None):
                dst = group_view(grp)
                ps = src.rearrange("p (t n) -> p t n", t=TT)
                if scale is None:
                    ins = dve.tensor_copy(dst, ps)
                else:
                    ins = tt(dst.rearrange("p t (h d) -> p t h d", d=DH), ps.rearrange("p t (h d) -> p t h d", d=DH), scale,
                             ALU.mult)
                return ins

            def head_post(k, grp, gain):
                dve.wait_ge(sem("group_squares"), k + 1)
                dve.tensor_reduce(stat[:, 8:16], sq[:, 0:512].rearrange("p (u d) -> p u d", d=DH), AX, ALU.add) \
                    .then_inc(sem("group_sums"), 1)
                dve.wait_ge(sem("group_rstd"), k + 1)
                for t in range(TT):
                    v = group_view(grp)[:, t, :].rearrange("p (h d) -> p h d", d=DH)
                    mark(tt(v, v, unit(stat[:, 8 + 4 * t:12 + 4 * t], DH), ALU.mult))
                settle()
                for t in range(TT):
                    v = group_view(grp)[:, t, :].rearrange("p (h d) -> p h d", d=DH)
                    g = gain if gain is not None else tokm[:, t, 5 + grp, :].rearrange("p (h d) -> p h d", d=DH)
                    mark(tt(v, v, g, ALU.mult))
                settle()

            def silu_gates():
                dve.wait_ge(sem("gates_silu"), 1)
                for i, name in enumerate(("gdn_on", "hg_on", "gla_on")):
                    for t in range(TT):
                        v = tokm[:, t, 6 + i, :].rearrange("p (h d) -> p h d", d=DH)
                        mark(tt(v, v, units(rows(name, DH), HEADS), ALU.mult))
                mark(ts(chm[:, 6:8, :], chm[:, 6:8, :], DH ** -0.5, None, ALU.mult))
                settle()

            def gdn_post():
                mark(head_out(1, PS[:, 1, :]))
                settle()
                for t in range(TT):
                    for hh in range(2):
                        v = group_view(1)[:, t, :].rearrange("p (h d) -> p h d", d=DH)[:, hh:hh + 3:2, :]
                        at = P * (1 + t)
                        ins = tt(v, v, PS[:, 3 * hh, at:at + P].rearrange("p (h d) -> p h d", d=DH), ALU.add)
                ins.then_inc(sem("group_out"), 1)
                head_post(0, 1, None)

            def fox():
                signal(sem("sq_free"), 2)
                dve.wait_ge(sem("fox_squares"), 1)
                dve.tensor_reduce(stat[:, 8:24], sq.rearrange("p (u d) -> p u d", d=DH), AX, ALU.add) \
                    .then_inc(sem("fox_sums"), 1)
                dve.wait_ge(sem("fox_rstd"), 1)
                st = stat[:, 8:24].rearrange("p (t s h) -> p t s h", t=TT, s=2)
                for t in range(TT):
                    for s in range(2):
                        v = tokm[:, t, s, :].rearrange("p (h d) -> p h d", d=DH)
                        mark(tt(v, v, unit(st[:, t, s, :], DH), ALU.mult))
                settle()
                for t in range(TT):
                    for s, name in enumerate(("fox_qn", "fox_kn")):
                        v = tokm[:, t, s, :].rearrange("p (h d) -> p h d", d=DH)
                        mark(tt(v, v, units(rows(name, DH), HEADS), ALU.mult))
                settle()
                ts(tokm[:, :, 0, :], tokm[:, :, 0, :], DH ** -0.5, None, ALU.mult).then_inc(sem("fox_normed"), 1)
                dve.wait_ge(sem("fox_logits"), 1)
                dve.tensor_reduce(stat[:, 24:28], PS[:, 2:4, 0:2 * P].rearrange("p b (h n) -> p b h n", n=P), AX, ALU.max,
                                  negate=True).then_inc(sem("fox_max"), 1)
                dve.tensor_reduce(stat[:, 28:32], PS[:, 0:2, :].rearrange("p b n -> p (b n)")
                                  .rearrange("p (h n) -> p h n", n=TOK), AX, ALU.max, negate=True) \
                    .then_inc(sem("fox_max"), 1)
                dve.wait_ge(sem("fox_probs"), 8)
                link(dve.reciprocal(stat[:, 32:40], stat[:, 32:40]))
                dve.wait_ge(sem("fox_out"), 1)
                for t in range(TT):
                    v = group_view(0)[:, t, :].rearrange("p (h d) -> p h d", d=DH)
                    ins = tt(v, PS[:, 2, t * 256:(t + 1) * 256].rearrange("p (h d) -> p h d", d=DH),
                             unit(stat[:, 32 + 4 * t:36 + 4 * t], DH), ALU.mult)
                ins.then_inc(sem("group_out"), 1)
                head_post(1, 0, units(rows("fox_on", DH), HEADS))

            def la_keys():
                z = tokm[:, :, TOKM["hg_f"], :]
                signal(sem("logits_z"), 1)
                dve.wait_ge(sem("logits_ln"), 2)
                s = sq[:, 512:1024].rearrange("p (t n) -> p t n", t=TT)
                mark(stt(la[:, :, 0:2, :].rearrange("p t f n -> p t (f n)"), z, 0.0, s, ALU.min, ALU.subtract))
                link(stt(z, z, 0.0, s, ALU.max, ALU.add))
                ts(z, z, -1.0, None, ALU.mult).then_inc(sem("hg_keys_log"), 1)
                signal(sem("la_ready"), 1)

            def la_all():
                mark(dve.memset(a_la, 0.0))
                signal(sem("pairs_free"), 1)
                three = lambda v, b: v.rearrange("p (m two n) -> p m two n", two=2, n=b)
                hg_pairs = PS[:, 0:2, :].rearrange("p b n -> p (b n)").rearrange("p (u n) -> p u n", n=P)
                gla_pairs = PS[:, 2:6, 0:2 * P].rearrange("p b (t n) -> p b t n", t=TT)
                gla_a = a_la[:, 8:16, :].rearrange("p (b t) n -> p b t n", t=TT)
                q3 = chm[:, 6:9, :].rearrange("p f n -> p (f n)")
                k3 = chm[:, 9:12, :].rearrange("p f n -> p (f n)")

                def operand(lv):
                    b = 1 << lv
                    dve.wait_ge(sem("level_exp"), lv + 1)
                    if lv == 0:
                        dve.wait_ge(sem("la_keys"), 1)
                    w, z = three(w_lv[:, lv % 2, :], b), three(z_lv[:, lv % 2, :], b)
                    if lv >= 2:
                        dve.wait_ge(sem("pairs"), lv)
                    mark(tt(z[:, :, 0, :], w[:, :, 0, :], three(k3, b)[:, :, 0, :], ALU.mult))
                    tt(z[:, :, 1, :], w[:, :, 1, :], three(q3, b)[:, :, 1, :], ALU.mult).then_inc(sem("level_operand"), 1)

                def select(lv):
                    dve.wait_ge(sem("pairs"), lv + 2)
                    if lv < 0:
                        m = ident[:, :]
                    elif lv < 6:
                        m = mask(f"t{1 << lv}")
                    if lv < 6:
                        m = m.bitcast(I32)
                        mark(dve.copy_predicated(a_la[:, 0:8, :], units(m, 8), hg_pairs))
                        m4 = m.rearrange("p (a b n) -> p a b n", a=1, b=1).to_broadcast([P, 4, TT, P])
                        ins = dve.copy_predicated(gla_a, m4, gla_pairs)
                    elif lv == 6:
                        mark(dve.tensor_copy(a_la[0:64, 0:8, 64:P], hg_pairs[0:64, :, 64:P]))
                        ins = dve.tensor_copy(gla_a[0:64, :, :, 64:P], gla_pairs[0:64, :, :, 64:P])
                    else:
                        top = a_top.rearrange("p (b u) n -> p b (u n)", b=4)
                        mark(dve.tensor_copy(top[:, 0:2, :], PS[:, 0:2, 0:2 * P]))
                        ins = dve.tensor_copy(a_top[:, 4:8, :], PS[:, 2:6, 0:P])
                    ins.then_inc(sem("pairs_read"), 1)
                    dve.wait_ge(sem("pairs_read"), lv + 2)

                operand(0)
                select(-1)
                for lv in range(8):
                    if lv < 7:
                        operand(lv + 1)
                    select(lv)
                dve.wait_ge(sem("la_out"), 1)
                mark(head_out(2, PS[:, 6, :]))
                head_out(3, PS[:, 7, :]).then_inc(sem("group_out"), 2)
                head_post(2, 2, None)
                head_post(3, 3, None)

            between = {0: [gates], 3: [gdn_tokens], 4: [gdn_grams],
                       5: [lambda: gdn_invert(0)], 6: [lambda: gdn_invert(1)], 7: [lambda: gdn_invert(2)],
                       8: [lambda: gdn_invert(3)], 9: [lambda: gdn_invert(4)], 10: [gdn_solve],
                       11: [lambda: gdn_chunk(0)], 12: [lambda: gdn_chunk(1)], 13: [lambda: gdn_chunk(2)],
                       14: [lambda: gdn_chunk(3), silu_gates, gdn_post, fox, la_keys, la_all]}
            for n, what in enumerate(MIX_ORDER):
                ahead(n)
                if 1 <= n <= 3:
                    gdn_taps(n - 1, n)
                for piece in between.get(n, ()):
                    piece()
            settle()
            signal(sem("tokens_ready"), 1)
            signal(sem("mix_done"), 1)
            turned("mixed", 8, [(None, act_hi, act_lo)])

            def ahead_4(name):
                for j in range(4):
                    ahead(STEP[name] + j)

            def residual(n_used):
                dve.wait_ge(block_used, n_used)
                tt(x[:, :, :], x[:, :, :], low4, ALU.add).then_inc(sem("x_ready"), 1)

            def next_norm(k):
                dve.wait_ge(sem("x_ready"), k)
                norm_rest(k, junk[:, 0, :])

            ahead_4("mix_out")
            residual(STEP["mix_out"] + 4)
            next_norm(1)
            turned("norm2", 8, [(lambda j: ch("norm2", j), h_hi, h_lo)])

            def older_taps(y, src, col, two_ft, ready):
                for c in range(2):
                    stt(y[:, c, 1:TOK], src[:, c, 0:TOK - 1], channel[:, bass.ds(col(1) + c, 1)], y[:, c, 1:TOK],
                        ALU.mult, ALU.add).then_inc(ready[0], 1)
                dve.wait_ge(ready[0], ready[1])
                for c in range(2):
                    ins = stt(y[:, c, 2:TOK], src[:, c, 0:TOK - 2], channel[:, bass.ds(col(0) + c, 1)], y[:, c, 2:TOK],
                              ALU.mult, ALU.add)
                return ins

            def ffn(f):
                n0 = STEP[f"ffn{f}"]
                conv = PC[f"ffn_conv{f}"]
                bank = lambda b: PS[:, b, :].rearrange("p (c n) -> p c n", c=2)

                def gate(i):
                    dve.wait_ge(sem("gate_last_tap"), i + (PAIRS * f + 1))
                    ins = older_taps(y_gate, bank(4), lambda tap: 2 * i + (conv + tap * 2 * FT), 0,
                                     (sem("gate_tap1"), 2 * i + (2 * PAIRS * f + 2)))
                    ins.then_inc(sem("gate_convolved"), 1)
                    dve.wait_ge(sem("gate_convolved"), i + (PAIRS * f + 1))

                def up(i):
                    dve.wait_ge(sem("up_last_tap"), i + (PAIRS * f + 1))
                    ins = older_taps(y_up, bank(5), lambda tap: 2 * i + (conv + tap * 2 * FT + FT), 0,
                                     (sem("up_tap1"), 2 * i + (2 * PAIRS * f + 2)))
                    ins.then_inc(sem("up_read"), 1)
                    dve.wait_ge(sem("up_read"), i + (PAIRS * f + 1))
                    dve.wait_ge(sem("gate_silu"), i + (PAIRS * f + 1))
                    tt(hidden, s_gate, y_up, ALU.mult).then_inc(sem("hidden_ready"), 1)

                def hid(i):
                    dve.wait_ge(sem("hidden_hi"), i + (PAIRS * f + 1))
                    tt(hid_lo, hidden, hid_hi.bitcast(F), ALU.subtract).then_inc(sem("hidden_split"), 1)

                ahead(n0)
                gate(0)
                ahead(n0 + 1)
                up(0)
                hid(0)
                with dve.Fori(1, PAIRS) as i:
                    n = n0 - 1
                    split(n + 2 + 3 * i, (n + 2) % RING)
                    gate(i)
                    split(n + 3 + 3 * i, (n + 3) % RING)
                    up(i)
                    split(n + 4 + 3 * i, (n + 4) % RING)
                    hid(i)
                ahead(n0 + 3 * PAIRS - 1)

            ffn(0)
            residual(STEP["ffn0"] + 3 * PAIRS)
            next_norm(2)
            turned("pre_mix0", 8, [(lambda j: ch("pre_mix0", j), h_hi, h_lo)])

            n0 = STEP["sc_in"]
            signal(sem("sc_bank_read"), 3)
            with dve.Fori(0, 4) as i:
                split(n0 + 2 + 3 * i, (n0 + 2) % RING)
                split(n0 + 3 + 3 * i, (n0 + 3) % RING)
                dve.wait_ge(sem("sc_gc"), i + 1)
                dve.wait_ge(block_used, n0 + 2 + 3 * i)
                tt(y_up, s_gate, PS[:, 5, :].rearrange("p (c n) -> p c n", c=2), ALU.mult).then_inc(sem("sc_product"), 1)
                dve.wait_ge(sem("sc_product"), i + 1)
                dve.sem_inc(sem("sc_bank_read"), 2)
                dve.wait_ge(sem("sc_last_tap"), i + 1)
                ins = older_taps(y_gate, y_up, lambda tap: 2 * i + (PC["sc_conv"] + tap * 8), 0, (sem("sc_tap1"), 2 * i + 2))
                ins.then_inc(sem("sc_convolved"), 1)
                dve.wait_ge(sem("sc_convolved"), i + 1)
                split(n0 + 4 + 3 * i, (n0 + 4) % RING)
                dve.wait_ge(block_used, n0 + 3 + 3 * i)
                tt(hidden, y_gate, PS[:, 6, :].rearrange("p (c n) -> p c n", c=2), ALU.mult).then_inc(sem("sc_gated"), 1)
                dve.wait_ge(sem("sc_gated"), i + 1)
                dve.sem_inc(sem("sc_bank_read"), 1)
                dve.wait_ge(sem("sc_hi"), i + 1)
                tt(act_lo[:, bass.ds(2 * i, 2), :], hidden, act_hi[:, bass.ds(2 * i, 2), :].bitcast(F), ALU.subtract) \
                    .then_inc(sem("sc_hidden"), 1)
            ahead_4("sc_out")

            posts = [0]

            def post(acc):
                q = posts[0]
                posts[0] += 1
                s = stat[:, 4:6]
                dve.wait_ge(sem("post_rstd"), q + 1)
                dve.wait_ge(sem("post_loaded"), 16 * (q + 1))
                for t in range(TT):
                    mark(stt(junk[:, t, :], acc[:, t, :], s[:, t:t + 1], post_g, ALU.mult, ALU.mult))
                settle()
                dve.sem_inc(sem("post_used"), 1)
                tt(x[:, :, :], x[:, :, :], junk, ALU.add).then_inc(sem("x_ready"), 1)

            post(low4)
            next_norm(3)
            turned("pre_ffn0", 8, [(lambda j: ch("pre_ffn0", j), h_hi, h_lo)])

            def ffn_and_ple(layer, k):
                ffn(1 + layer)
                turned(f"p{layer}", 2, [(None, p_hi, p_lo)])
                post(low4)
                dve.sem_inc(sem("low4_read"), 1)
                next_norm(k)
                turned(f"pre_ple{layer}", 8, [(lambda j: ch(f"pre_ple{layer}", j), h_hi, h_lo)])
                ahead(STEP[f"ple_proj{layer}"])
                for j in range(4):
                    ahead(STEP[f"ple_gate{layer}"] + j)
                dve.wait_ge(sem("ple_gate"), layer + 1)
                tt(gate_s, gate_s, low4, ALU.mult).then_inc(sem("ple_product"), 1)
                post(gate_s)

            ffn_and_ple(0, 4)
            next_norm(5)
            turned("pre_mix1", 8, [(lambda j: ch("pre_mix1", j), h_hi, h_lo), (lambda j: ch("kv", j), act_hi, act_lo)])

            lv4 = rows("lambda", 256).rearrange("p (a b d) -> p a b d", a=2, b=2)
            lj = gate_s[:, 0, 0:P].rearrange("p (a d) -> p a d", a=2)
            link(tt(lj, lv4[:, :, 0, :], lv4[:, :, 1, :], ALU.mult))
            dve.tensor_reduce(lam[:, 0:2], lj, AX, ALU.add).then_inc(sem("lambda_sums"), 1)
            dve.wait_ge(sem("lambda_exps"), 1)
            link(tt(lam[:, 2:3], lam[:, 1:2], lam[:, 0:1], ALU.subtract))
            link(ts(lam[:, 3:4], lam[:, 2:3], -LAMBDA_INIT, None, ALU.add))
            for name in ("att_k", "att_v", "att_q"):
                ahead_4(name)
            dve.wait_ge(sem("bias_copied"), 1)
            for h in range(N_HEADS):
                a = att_stat
                dve.wait_ge(sem("logits"), h + 1)
                b1 = bias_t[:, h, :].rearrange("p (o n) -> p o n", o=1).to_broadcast([P, 2, TOK])
                b0 = bias_t[:, h, P:TOK].rearrange("p (o n) -> p o n", o=1).to_broadcast([P, 2, P])
                mark(tt(lg1, PS[:, 6:8, 0:TOK], b1, ALU.add))
                mark(tt(lg0, PS[:, 6:8, TOK:TOK + P], b0, ALU.add))
                settle()
                dve.sem_inc(sem("logits_read"), 1)
                dve.tensor_reduce(a[:, 0:2], lg1, AX, ALU.max, negate=True).then_inc(sem("att_max"), 1)
                dve.tensor_reduce(a[:, 2:4], lg0, AX, ALU.max, negate=True).then_inc(sem("att_max"), 1)
                dve.wait_ge(sem("att_exp"), h + 1)
                link(dve.reciprocal(a[:, 8:12], a[:, 4:8]))
                for m in (9, 11):
                    mark(tt(a[:, m:m + 1], a[:, m:m + 1], lam[:, 3:4], ALU.mult))
                settle()
                mark(ts(lg1[:, 0, :], lg1[:, 0, :], a[:, 8:9], None, ALU.mult))
                mark(ts(lg0[:, 0, :], lg0[:, 0, :], a[:, 10:11], None, ALU.mult))
                settle()
                w1 = at_w[:, 0:2, :].rearrange("p a n -> p (a n)")
                mark(stt(w1, lg1[:, 1, :], a[:, 9:10], lg1[:, 0, :], ALU.mult, ALU.add))
                stt(at_w[:, 2, :], lg0[:, 1, :], a[:, 11:12], lg0[:, 0, :], ALU.mult, ALU.add) \
                    .then_inc(sem("att_weights"), 1)
                dve.wait_ge(sem("att_weights"), h + 1)
                dve.wait_ge(sem("head_out"), h + 1)
                mark(dve.tensor_copy(xn[:, :, h * P:(h + 1) * P], PS[:, 5, 0:TOK].rearrange("p (t n) -> p t n", t=TT)))
                settle()
                dve.sem_inc(sem("head_read"), 1)
            link(tt(junk, xn[:, :, :], xn[:, :, :], ALU.mult))
            dve.tensor_reduce(stat[:, 8:24], junk.rearrange("p t n -> p (t n)").rearrange("p (u d) -> p u d", d=P), AX,
                              ALU.add).then_inc(sem("subln_sums"), 1)
            dve.wait_ge(sem("subln_rstd"), 1)
            link(ts(stat[:, 8:24], stat[:, 8:24], 1.0 - LAMBDA_INIT, None, ALU.mult))
            v = xn[:, :, :].rearrange("p t n -> p (t n)").rearrange("p (u d) -> p u d", d=P)
            tt(v, v, unit(stat[:, 8:24], P), ALU.mult).then_inc(sem("tokens_ready"), 1)
            turned("att", 8, [(lambda j: ch("subln"), act_hi, act_lo)])
            ahead_4("att_out")
            post(low4)
            next_norm(6)
            turned("pre_ffn1", 8, [(lambda j: ch("pre_ffn1", j), h_hi, h_lo)])
            ffn_and_ple(1, 7)
            dve.wait_ge(sem("x_ready"), 8)
            dve.sem_inc(sem("result"), 1)


def column_block(w, c0, n=256):
    b = np.zeros((P, KC, 256), np.float32)
    b[:, :, 0:n] = w[:, c0:c0 + n].reshape(KC, P, n).transpose(1, 0, 2)
    return b.reshape(P, BLK)


def row_block_of(w, j):
    return w[256 * j:256 * (j + 1)].reshape(2, P, D).transpose(1, 0, 2).reshape(P, BLK)


def weight_stream(a):
    blocks = []
    w = a["w_in"][0]
    small = np.concatenate([w[:, W_IN[n]:W_IN[n] + m] for n, m in
                            (("fox_f", 4), ("gdn_a", 4), ("gdn_b", 4), ("gla_gk", 16))], axis=1)
    for what in MIX_ORDER:
        blocks.append(column_block(small, 0, SMALL) if what == "small" else column_block(w, W_IN[what]))

    def rows_of(w, n=4):
        blocks.extend(row_block_of(w, j) for j in range(n))

    def ffn(up, down):
        for i in range(PAIRS):
            blocks.append(column_block(up, 256 * i))
            blocks.append(column_block(up, D_FF + 256 * i))
            if i:
                blocks.append(row_block_of(down, i - 1))
        blocks.append(row_block_of(down, PAIRS - 1))

    rows_of(a["w_out"][0])
    ffn(a["w_up"][0], a["w_down"][0])
    w = a["w_sc_in_2"][0]
    for i in range(4):
        for part in (1, 2, 0):
            blocks.append(column_block(w, part * D + 256 * i))
    rows_of(a["w_sc_out_2"][0])
    for layer in range(2):
        if layer == 1:
            for i in range(4):
                blocks.append(column_block(a["w_kv_2"], 256 * i))
            rows_of(a["w_kv_2"][:, D:])
            for i in range(4):
                blocks.append(column_block(a["w_q_2"][0], 256 * i))
            rows_of(a["w_o_2"][0])
        ffn(a["w_ffn_up_2"][layer], a["w_ffn_down_2"][layer])
        rows_of(a["w_ple_proj_2"][layer], 1)
        rows_of(a["w_ple_gate_2"][layer])
    assert len(blocks) == N_BLOCKS
    return np.stack(blocks)


def channel_columns(a):
    def cols(v):
        return v.reshape(-1, P).T

    parts = [cols(a["norm1_g"][0]), cols(a["norm2_g"][0]), cols(a["g_pre_mix_2"][0]), cols(a["g_pre_ffn_2"][0]),
             cols(a["g_pre_ple_2"][0]), cols(a["g_pre_mix_2"][1]), cols(a["g_kv_2"]), cols(a["g_pre_ffn_2"][1]),
             cols(a["g_pre_ple_2"][1]), cols(a["g_subln_2"][0]), cols(a["w_sc_conv_2"][0]), cols(a["gdn_conv_w"][0]),
             cols(a["ffn_conv_w"][0]), cols(a["ffn_conv_b"][0]), cols(a["w_ffn_conv_2"][0]), cols(a["w_ffn_conv_2"][1])]
    return np.ascontiguousarray(np.concatenate(parts, axis=1))


def mask_table():
    i = np.arange(P)
    r, c = i[:, None], i[None, :]
    same = r // CHUNK == c // CHUNK
    one = {"tri": r <= c, "ones": r >= 0 * c, "after": r > c, "blk_tri": same & (r <= c), "blk_after": same & (r > c),
           "ind0": (r < CHUNK) & (c >= 0), "ind1": (r >= CHUNK) & (c >= 0),
           "m1": (r // 2 == c // 2) & (c < r)}
    for lv in range(6):
        b = 1 << lv
        one[f"t{b}"] = (r // (2 * b) == c // (2 * b)) & (r % (2 * b) < b) & (c % (2 * b) >= b)
    for lv in range(7):
        b = 1 << lv
        mid = c // (2 * b) * (2 * b) + b - 1
        right = c % (2 * b) >= b
        one[f"e{b}"] = np.where(right, (r > mid) & (r <= c), (r > c) & (r <= mid))
    add = {"fox_add": c <= r, "gdn_add": same & (c <= r)}
    rows = [np.where(add[n], 0.0, NEG) if n in add else one[n] + np.zeros((P, P)) for n in MASKS]
    return np.stack(rows, axis=1).astype(np.float32)


def distance_one_hot():
    dist = 255 - np.arange(N_DIST)
    n, exact, far = 32, 16, 128
    safe = np.maximum(dist, 1).astype(np.float32)
    large = exact + (np.log(safe / np.float32(exact)) / np.float32(math.log(far / exact)) * (n - exact)).astype(np.int32)
    bucket = np.where(dist < 0, n, np.where(dist < exact, dist, np.minimum(large, n - 1)))
    return (np.arange(BIAS_ROWS)[:, None] == bucket[None, :]).astype(np.float32)


def kernel(**inputs):
    import concourse.bacc as bacc
    from concourse.bass_utils import run_bass_kernel_spmd

    a = {k: np.asarray(v) for k, v in inputs.items()}
    row = np.concatenate([a["fox_b_f"][0], a["gdn_dt_bias"][0], a["gdn_a_log"][0], a["fox_qn_g"][0], a["fox_kn_g"][0],
                          a["fox_on_g"][0], a["gdn_on_g"][0], a["hg_on_g"][0], a["gla_on_g"][0], a["gla_b_gk"][0],
                          a["diff_lambda_2"][0].reshape(-1)])
    post = np.stack([a["g_post_mix_2"][0], a["g_post_ffn_2"][0], a["g_post_ple_2"][0],
                     a["g_post_mix_2"][1], a["g_post_ffn_2"][1], a["g_post_ple_2"][1]])
    arrays = {
        "weights": weight_stream(a), "x_in": a["x"][0], "masks_in": mask_table(), "ident_in": np.eye(P, dtype=np.float32),
        "channel_in": channel_columns(a), "row_in": row, "w_gk_in": a["gla_w_gk"][0], "post_in": post,
        "p_in": a["p_2"][:, 0], "table_in": a["rel_bias_2"], "onehot_in": distance_one_hot(),
        "flip_in": np.eye(P, dtype=np.float32)[::-1],
    }
    arrays = {k: np.ascontiguousarray(v) for k, v in arrays.items()}
    nc = bacc.Bacc("TRN2", target_bir_lowering=False, num_devices=1)
    args = [nc.dram_tensor(k, v.shape, mybir.dt.from_np(v.dtype), kind="ExternalInput").ap() for k, v in arrays.items()]
    result = nc.dram_tensor("result", (TOK, D), F, kind="ExternalOutput").ap()
    build(nc, *args, result)
    r = run_bass_kernel_spmd(nc, [arrays], core_ids=[0])
    return r.results[0]["result"].reshape(1, TOK, D)
```

```python
import math
from contextlib import ExitStack

import numpy as np

import concourse.bass as bass
from concourse import mybir

F = mybir.dt.float32
R = mybir.dt.float32r
I32 = mybir.dt.int32
ALU = mybir.AluOpType
ACT = mybir.ActivationFunctionType
AX = mybir.AxisListType.X

P = 128
TOK = 256
TT = TOK // P
D = 1024
KC = D // P
BLK = 2048
RING = 3
EPS = 1e-6
ARENA = 24496
NEG = -1e30
D_FF = 2816
FT = D_FF // P
PAIRS = FT // 2
HEADS = 4
DH = 64
CHUNK = 64
GROUP = 256
TABLES = "natural_log_exp_and_others"

STEP = {}
N_BLOCKS = 0
for _name, _n in (("mix_in", 15), ("mix_out", 4), ("ffn0", 3 * PAIRS), ("sc_in", 12), ("sc_out", 4),
                  ("ffn1", 3 * PAIRS), ("ple_proj0", 1), ("ple_gate0", 4), ("att_k", 4), ("att_q", 4),
                  ("att_v", 4), ("att_out", 4), ("ffn2", 3 * PAIRS), ("ple_proj1", 1), ("ple_gate1", 4)):
    STEP[_name] = N_BLOCKS
    N_BLOCKS += _n

W_IN = {"fox_q": 0, "fox_k": 256, "fox_v": 512, "fox_f": 768, "gdn_q": 772, "gdn_k": 1028, "gdn_v": 1284,
        "gdn_b": 1540, "gdn_a": 1544, "gdn_z": 1548, "hg_q": 1804, "hg_f": 2060, "hg_i": 2316,
        "hg_g": 2572, "gla_qk": 2828, "gla_v": 3084, "gla_gk": 3340, "gla_g": 3356}
MIX_ORDER = ("small", "gdn_q", "gdn_k", "gdn_v", "hg_f", "hg_q", "fox_q", "fox_k", "fox_v", "gla_qk",
             "gla_v", "hg_i", "gdn_z", "hg_g", "gla_g")
CHANNEL_MAJOR = ("gdn_q", "gdn_k", "gdn_v", "hg_q", "gla_qk")
TOKM = {n: i for i, n in enumerate(("fox_q", "fox_k", "fox_v", "hg_f", "hg_i", "gla_v", "gdn_z", "hg_g", "gla_g"))}
SMALL = 28

MASKS = ("tri", "ones", "after", "fox_add", "blk_tri", "blk_after", "ind0", "ind1", "gdn_add", "m1",
         "t1", "t2", "t4", "t8", "t16", "t32", "e1", "e2", "e4", "e8", "e16", "e32", "e64")
MASK = {n: i for i, n in enumerate(MASKS)}

PC, N_PC = {}, 0
for _name, _n in (("norm1", 8), ("norm2", 8), ("pre_mix0", 8), ("pre_ffn0", 8), ("pre_ple0", 8),
                  ("pre_mix1", 8), ("kv", 8), ("pre_ffn1", 8), ("pre_ple1", 8), ("subln", 1),
                  ("sc_conv", 24), ("gdn_conv", 24), ("ffn_conv0", 3 * 2 * FT), ("ffn_bias", 2 * FT),
                  ("ffn_conv1", 3 * 2 * FT), ("ffn_conv2", 3 * 2 * FT)):
    PC[_name] = N_PC
    N_PC += _n

ROW, N_ROW = {}, 0
for _name, _n in (("fox_b_f", 4), ("gdn_dt", 4), ("gdn_a_log", 4), ("fox_qn", 64), ("fox_kn", 64), ("fox_on", 64),
                  ("gdn_on", 64), ("hg_on", 64), ("gla_on", 64), ("b_gk", 128), ("lambda", 256)):
    ROW[_name] = N_ROW
    N_ROW += _n

TURN = {}
_chunks = 0
for _name, _n in (("norm1", 8), ("mixed", 8), ("norm2", 8), ("pre_mix0", 8), ("pre_ffn0", 8), ("p0", 2), ("pre_ple0", 8),
                  ("pre_mix1", 8), ("att", 8), ("pre_ffn1", 8), ("p1", 2), ("pre_ple1", 8)):
    TURN[_name] = (_chunks, _chunks // 2, _n)
    _chunks += _n

N_HEADS = 8
LAMBDA_INIT = 0.8 - 0.6 * math.exp(-0.3)
N_DIST = 384
BIAS_ROWS = 33


def build(nc, weights, x_in, masks_in, ident_in, channel_in, row_in, w_gk_in, post_in, p_in, table_in,
          onehot_in, flip_in, out):
    bias_dram = nc.dram_tensor("bias_by_distance", (N_HEADS, N_DIST), F, kind="Internal").ap()
    with ExitStack() as ctx:
        sems = {}

        def sem(name):
            if name not in sems:
                sems[name] = ctx.enter_context(nc.semaphore(name))
            return sems[name]

        def sb(name, shape, dt=F):
            return ctx.enter_context(nc.sbuf_tensor(name, shape, dt))

        raw = sb("raw", [P, RING, BLK])
        w_hi = sb("w_hi", [P, RING, BLK], R)
        w_lo = sb("w_lo", [P, RING, BLK], R)
        x = sb("x", [P, TT, D])
        xn = sb("xn", [P, TT, D])
        h_hi = sb("h_hi", [P, KC, TOK], R)
        h_lo = sb("h_lo", [P, KC, TOK], R)
        channel = sb("channel", [P, N_PC])
        row = sb("row", [P, N_ROW])
        ident = sb("ident", [P, P])
        stat = sb("stat", [P, 64])
        eps = sb("eps", [P, 1])
        zeros_r = sb("zeros_r", [P, 512], R)
        arena_offset = -(-nc.sbuf_base // 32) * 32
        fence = sb("arena", [P, ARENA])

        arena = {"at": 0, "n": 0}

        def place(shape):
            n = int(np.prod(shape[1:]))
            at = arena["at"]
            arena["at"] += n
            assert arena["at"] <= ARENA, arena
            v = fence[0:shape[0], at:at + n]
            if len(shape) == 3:
                v = v.rearrange("p (a b) -> p a b", a=shape[1])
            elif len(shape) == 4:
                v = v.rearrange("p (a b c) -> p a b c", a=shape[1], b=shape[2])
            return v

        masks = place([P, len(MASKS), P])
        tokm = place([P, TT, len(TOKM), GROUP])
        small = place([P, TT, SMALL])
        chm = place([P, 12, TOK])
        gate_z = place([P, TT, 8])
        gate_l = place([P, TT, 8])
        lf = place([P, TT, HEADS])
        nlf = place([P, TT, HEADS])
        gd = place([P, TT, HEADS])
        ngd = place([P, TT, HEADS])
        beta = place([P, TT, HEADS])
        ea = place([P, HEADS])
        e_g = place([P, TT, HEADS])
        e_rest = place([P, TT, HEADS])
        e_last = place([P, TT, 2, HEADS])
        be_g = place([P, TT, HEADS])
        la = place([P, TT, 3, P])
        gk_t = place([16, TOK])
        w_gk = place([16, P])
        sq = place([P, 1024])
        mix_at = arena["at"]
        qn = place([P, 8, DH])
        kn = place([P, 8, DH])
        kbg = place([P, 8, DH])
        vb = place([P, 8, DH])
        ko = place([P, 8, DH])
        qi = place([P, 8, DH])
        w_t = place([P, 2, TOK])
        u_gd = place([P, 8, DH])
        v_new = place([P, 8, DH])
        state = place([P, 2, DH])
        dec = place([P, 8, P])
        dec_t = place([P, 8, P])
        m_gd = place([P, 8, P])
        mt_gd = place([P, 8, P])
        a_qk = place([P, 8, P])
        c_t = place([P, 8, P])
        inv, inv_t, y_gd = dec, dec_t, m_gd
        gdn_at = arena["at"]
        arena["at"] = mix_at
        fq_t = place([P, 2, TOK])
        fk_t = place([P, 2, TOK])
        probs0 = place([P, HEADS, P])
        probs1 = place([P, HEADS, TOK])
        probs_t = place([P, 12, P])
        arena["at"] = mix_at
        w_lv = place([P, 2, 768])
        z_lv = place([P, 2, 768])
        a_la = place([P, 16, P])
        a_top = place([P, 8, P])

        PS = ctx.enter_context(nc.psum_tensor("PS", [P, 8, 512], F))
        low4 = PS[:, 0:4, :].rearrange("p b n -> p (b n)").rearrange("p (t n) -> p t n", t=TT)
        high4 = PS[:, 4:8, :].rearrange("p b n -> p (b n)").rearrange("p (t n) -> p t n", t=TT)

        operand_offset = arena_offset + 4 * (ARENA - 2 * KC * TOK)
        act_hi = nc.alloc_sbuf_tensor_at("act_hi", [P, KC, TOK], R, offset=operand_offset)
        act_lo = nc.alloc_sbuf_tensor_at("act_lo", [P, KC, TOK], R, offset=operand_offset + 4 * KC * TOK)
        arena["at"] = 0
        hid_hi = act_hi[:, 0:2, :]
        hid_lo = act_lo[:, 0:2, :]
        p_hi = act_hi[:, 2:4, :]
        p_lo = act_lo[:, 2:4, :]
        y_gate = place([P, 2, TOK])
        y_up = place([P, 2, TOK])
        s_gate = place([P, 2, TOK])
        hidden = place([P, 2, TOK])
        wt_at = arena["at"]
        junk = place([P, TT, D])
        gate_s = place([P, TT, D])
        post_g = place([P, D])
        p_tok = place([P, TT, TOK])
        q_t = place([P, N_HEADS, TOK])
        k_t = place([P, N_HEADS, TOK])
        v_tok = place([P, TT, D])
        bias_t = place([P, N_HEADS, TOK])
        bias_rev = junk.rearrange("p t (h n) -> p (t h) n", n=TOK)
        flip = place([P, P])
        lg1 = place([P, 2, TOK])
        lg0 = place([P, 2, P])
        at_w = place([P, 3, P])
        at_wt = fence[:, wt_at:wt_at + N_HEADS * 3 * P].rearrange("p (h j n) -> p h j n", h=N_HEADS, j=3)
        table = place([BIAS_ROWS, N_HEADS])
        onehot = place([BIAS_ROWS, N_DIST])
        bias_row = place([N_HEADS, N_DIST])
        lam = place([P, 8])
        att_stat = place([P, 16])
        assert arena["at"] <= ARENA - 2 * KC * TOK

        def mask(name):
            return masks[:, MASK[name], :]

        def ch(name, j=0):
            return channel[:, PC[name] + j:PC[name] + j + 1]

        def rows(name, n):
            return row[:, ROW[name]:ROW[name] + n]

        def unit(v, n):
            return v.rearrange("p (u o) -> p u o", o=1).to_broadcast([P, v.shape[1], n])

        def units(v, n):
            return v.rearrange("p (o m) -> p o m", o=1).to_broadcast([P, n, v.shape[1]])

        def group_view(grp):
            return xn[:, :, grp * GROUP:(grp + 1) * GROUP]

        def u_of(t, h):
            return (h % 2) * 4 + t * 2 + h // 2

        def la_unit(t, h):
            return u_of(t, h) if h < 4 else 8 + (h - 4) * 2 + t

        def pair_bank(t, h):
            bank, at = (h % 2, (t * 2 + h // 2) * P) if h < 4 else (h - 2, t * P)
            return PS[:, bank, at:at + P]

        def la_top_unit(h):
            return (h % 2) * 2 + h // 2 if h < 4 else h

        ALL_UNITS = [(t, h) for t in range(TT) for h in range(HEADS)]

        def th(v):
            return v.rearrange("p t h -> p (t h)")

        raw_loaded = [sem(f"raw_loaded{s}") for s in range(RING)]
        hi_ready, lo_ready, block_used = sem("hi_ready"), sem("lo_ready"), sem("block_used")
        chunks_turned, part_hi, part_ready = sem("chunks_turned"), sem("part_hi"), sem("part_ready")
        inputs = sem("inputs_loaded")
        N_INPUTS = 3 * 16

        block = ctx.enter_context(nc.Block())

        @block.sync
        def _(sp):
            sp.dma_start(x[:, :, :], x_in.rearrange("(t p) n -> p t n", p=P)).then_inc(inputs, 16)
            sp.dma_start(ident[:, :], ident_in).then_inc(inputs, 16)
            sp.dma_start(channel[:, :], channel_in).then_inc(inputs, 16)
            for s in range(RING):
                sp.dma_start(raw[:, s, :], weights[s]).then_inc(raw_loaded[s], 16)
            sp.dma_start(row[:, :], row_in.partition_broadcast(P)).then_inc(sem("mix_inputs"), 16)
            sp.dma_start(w_gk, w_gk_in).then_inc(sem("mix_inputs"), 16)
            sp.dma_start(masks, masks_in).then_inc(sem("mix_inputs"), 16)
            whole = (N_BLOCKS - RING) // RING
            with sp.Fori(1, 1 + whole) as i:
                for s in range(RING):
                    sp.wait_ge(lo_ready, RING * i + (s - RING + 1))
                    sp.dma_start(raw[:, s, :], weights[bass.ds(RING * i + s, 1)].rearrange("a p n -> (a p) n")) \
                        .then_inc(raw_loaded[s], 16)
            for n in range(RING + whole * RING, N_BLOCKS):
                sp.wait_ge(lo_ready, n - RING + 1)
                sp.dma_start(raw[:, n % RING, :], weights[n]).then_inc(raw_loaded[n % RING], 16)
            for t in range(TT):
                sp.wait_ge(sem("x_tile"), 15 + t)
                sp.dma_start(out[t * P:(t + 1) * P, :], x[:, t, :]).then_inc(sem("stored"), 16)
            sp.wait_ge(sem("stored"), 16 * TT)

        @block.gpsimd
        def _(pool):
            pool.memset(zeros_r[:, :].bitcast(F), 0.0).then_inc(sem("zeros"), 1)
            pool.memset(eps[:, :], EPS).then_inc(sem("eps_set"), 1)
            pool.wait_ge(sem("mix_done"), 1)
            pool.dma_start(flip, flip_in).then_inc(sem("flip_loaded"), 16)
            pool.memset(table, NEG).then_inc(sem("table_row"), 1)
            pool.wait_ge(sem("table_row"), 1)
            pool.dma_start(table[0:BIAS_ROWS - 1, :], table_in).then_inc(sem("table_loaded"), 16)
            pool.dma_start(onehot, onehot_in).then_inc(sem("table_loaded"), 16)
            pool.wait_ge(sem("bias_rows"), 1)
            pool.dma_start(bias_dram, bias_row).then_inc(sem("bias_stored"), 16)
            pool.wait_ge(sem("bias_stored"), 16)
            toeplitz = bass.AP(tensor=bias_dram.tensor, offset=0, ap=[[1, P], [N_DIST, N_HEADS], [1, TOK]])
            for n in range(6):
                if n:
                    pool.wait_ge(sem("post_used"), n)
                pool.dma_start(post_g, post_in[n].partition_broadcast(P)).then_inc(sem("post_loaded"), 16)
                if n == 3:
                    pool.wait_ge(sem("tokens1_ready"), 6)
                    pool.dma_start(bias_rev, toeplitz).then_inc(sem("bias_loaded"), 16)
                if n in (0, 3):
                    if n == 3:
                        pool.wait_ge(chunks_turned, TURN["p0"][1] + 1)
                    pool.dma_start(p_tok, p_in[n // 3].rearrange("(t p) n -> p t n", p=P)).then_inc(sem("p_loaded"), 16)

        @block.tensor
        def _(pe):
            def mm(o, lhs, rhs, start=True, stop=True):
                return pe.matmul(o, lhs, rhs, start=start, stop=stop)

            def block_ready(n):
                pe.wait_ge(hi_ready, n + 1)
                pe.wait_ge(lo_ready, n + 1)

            def chunks_ready(name, k):
                pe.wait_ge(part_ready, TURN[name][1] + k // 2 + 1)

            def columns(n0, slot, bank, operand, channel_major=True, n=TOK, fresh=None):
                block_ready(n0)
                a_hi, a_lo = operand
                for f in range(2):
                    for k in range(KC):
                        if fresh and f == 0 and k % 2 == 0:
                            chunks_ready(fresh, k)
                        if channel_major:
                            at = k * 256 + f * P
                            ws_hi, ws_lo = w_hi[:, slot, at:at + P], w_lo[:, slot, at:at + P]
                            o = PS[:, bank, f * TOK:(f + 1) * TOK]
                            mm(o, ws_hi, a_hi[:, k, :], k == 0, False)
                            mm(o, ws_hi, a_lo[:, k, :], False, False)
                            last = mm(o, ws_lo, a_hi[:, k, :], False, k == KC - 1)
                        else:
                            tok = slice(f * P, (f + 1) * P)
                            ws_hi, ws_lo = w_hi[:, slot, k * 256:k * 256 + n], w_lo[:, slot, k * 256:k * 256 + n]
                            o = PS[:, bank, f * TOK:f * TOK + n]
                            mm(o, a_hi[:, k, tok], ws_hi, k == 0, False)
                            mm(o, a_hi[:, k, tok], ws_lo, False, False)
                            last = mm(o, a_lo[:, k, tok], ws_hi, False, k == KC - 1)
                last.then_inc(block_used, 1)

            def row_block(n0, slot, acc, operand, k0, first, final, tiles=False):
                block_ready(n0)
                a_hi, a_lo = operand
                parts = ((a_hi, w_hi), (a_hi, w_lo), (a_lo, w_hi))
                order = [(kk, t) for t in range(TT) for kk in range(2)] if final else \
                    [(kk, t) for kk in range(2) for t in range(TT)]
                for kk, t in order:
                    tok = slice(t * P, (t + 1) * P)
                    for j, (a, w) in enumerate(parts):
                        for half in range(2):
                            at = kk * D + half * 512
                            last = pe.matmul(acc[:, t, half * 512:(half + 1) * 512], a[:, k0 + kk, tok],
                                             w[:, slot, at:at + 512], start=first and kk == 0 and j == 0,
                                             stop=final and kk == 1 and j == 2, skip_group_check=True)
                    if tiles and (kk, t) == (1, 0):
                        last.then_inc(sem("tile_summed"), 1)
                last.then_inc(block_used, 1)

            def turn(name, src, bank=4, tile_ready=None):
                for t in range(TT):
                    if tile_ready:
                        pe.wait_ge(sem(f"tokens{t}_ready"), tile_ready)
                    for j in range(TURN[name][2]):
                        at = (j % 2) * TOK + t * P
                        last = pe.transpose(PS[:, bank + j // 2, at:at + P], src[:, t, j * P:(j + 1) * P], ident[:, :])
                        if t == TT - 1 and j % 2:
                            last.then_inc(chunks_turned, 1)

            pe.wait_ge(inputs, N_INPUTS)
            turn("norm1", xn, tile_ready=1)

            def gates():
                pe.wait_ge(sem("gates_ready"), 1)
                pe.wait_ge(sem("mix_inputs"), 48)
                o = PS[:, 0, :]
                for t in range(TT):
                    mm(o[:, t * 4:t * 4 + 4], mask("blk_tri"), gd[:, t, :])
                    mm(o[:, 8 + t * 4:12 + t * 4], mask("blk_after"), gd[:, t, :])
                    for c in range(2):
                        at = 16 + (t * 2 + c) * 4
                        last = mm(o[:, at:at + 4], mask(f"ind{c}"), gd[:, t, :])
                last.then_inc(sem("gate_sums"), 1)
                for t in range(TT):
                    last = pe.transpose(PS[0:16, 1, t * P:(t + 1) * P], small[:, t, 12:28], ident[:, :])
                last.then_inc(sem("gk_turned"), 1)
                pe.wait_ge(sem("gk_copied"), 1)
                for t in range(TT):
                    last = mm(PS[:, 1, 256 + t * P:256 + (t + 1) * P], gk_t[:, t * P:(t + 1) * P], w_gk)
                last.then_inc(sem("gk_projected"), 1)

            def gdn_tokens():
                pe.wait_ge(sem("gdn_convolved"), 1)
                pe.wait_ge(sem("gk_read"), 1)
                for s in range(3):
                    for t in range(TT):
                        for f in range(2):
                            last = pe.transpose(PS[:, s, t * TOK + f * P:t * TOK + (f + 1) * P],
                                                chm[:, 2 * s + f, t * P:(t + 1) * P], ident[:, :])
                last.then_inc(sem("gdn_token_major"), 1)

            def gdn_channels():
                pe.wait_ge(sem("gdn_normed"), 1)
                for s, v in enumerate((qn, kn, qi)):
                    w = v.rearrange("p (t c) d -> p t (c d)", t=TT)
                    for pair in range(2):
                        for t in range(TT):
                            last = pe.transpose(PS[:, s, pair * TOK + t * P:pair * TOK + (t + 1) * P],
                                                w[:, t, pair * P:(pair + 1) * P], ident[:, :])
                last.then_inc(sem("gdn_channel_major"), 1)

            def unit_of(v, t, h):
                return v[64 * (h % 2):64 * (h % 2) + 64, h // 2, t * P:(t + 1) * P]

            qn_t, kn_t, qi_t = chm[:, 0:2, :], chm[:, 2:4, :], chm[:, 4:6, :]
            bank2 = lambda b: PS[:, b:b + 2, :].rearrange("p b n -> p (b n)").rearrange("p (u n) -> p u n", n=P)

            def gdn_grams():
                pe.wait_ge(sem("gdn_copied"), 1)
                for t, h in ALL_UNITS:
                    u = u_of(t, h)
                    mm(bank2(0)[:, u, :], unit_of(kn_t, t, h), unit_of(kn_t, t, h))
                    g_b = gd[:, t, h:h + 1].to_broadcast([P, P])
                    ng_b = ngd[:, t, h:h + 1].to_broadcast([P, P])
                    o = bank2(2)[:, u, :]
                    mm(o, mask("blk_tri"), g_b, True, False)
                    mm(o, ng_b, mask("blk_tri"), False, False)
                    last = mm(o, ident[:, :], mask("gdn_add"), False, True)
                last.then_inc(sem("decay_logs"), 1)
                for t, h in ALL_UNITS:
                    last = mm(bank2(6)[:, u_of(t, h), :], unit_of(kn_t, t, h), unit_of(qn_t, t, h))
                last.then_inc(sem("qk_gram"), 1)
                pe.wait_ge(sem("decay"), 1)
                for u in range(8):
                    last = pe.transpose(bank2(2)[:, u, :], dec[:, u, :], ident[:, :])
                last.then_inc(sem("decay_turned"), 1)
                pe.wait_ge(sem("m_ready"), 1)
                for u in range(8):
                    last = pe.transpose(bank2(0)[:, u, :], m_gd[:, u, :], ident[:, :])
                last.then_inc(sem("m_turned"), 1)

            def gdn_invert(lv):
                pe.wait_ge(sem("inv_ready"), lv + 1)
                pe.wait_ge(sem("ct_ready"), lv + 1)
                for u in range(8):
                    last = mm(bank2(2)[:, u, :], c_t[:, u, :], inv[:, u, :])
                last.then_inc(sem("cx"), 1)
                pe.wait_ge(sem("cx_copied"), lv + 1)
                for u in range(8):
                    if lv < 4:
                        mm(bank2(6)[:, u, :], inv_t[:, u, :], y_gd[:, u, :])
                    last = mm(bank2(0)[:, u, :], y_gd[:, u, :], inv_t[:, u, :])
                last.then_inc(sem("xcx"), 1)

            def gdn_solve():
                pe.wait_ge(sem("inv_ready"), 6)
                for t, h in ALL_UNITS:
                    m, u = u_of(t, h), t * HEADS + h
                    mm(PS[:, 2, u * DH:(u + 1) * DH], inv_t[:, m, :], vb[:, u, :])
                    a = 64 * (h % 2)
                    at = (h // 2) * TOK + t * P
                    last = mm(PS[a:a + 64, 3, at:at + P], kbg[:, u, :], inv_t[:, m, :])
                last.then_inc(sem("solved"), 1)

            def gdn_chunk(c):
                t, half = divmod(c, 2)
                r = slice(64 * half, 64 * half + 64)
                tok = slice(c * CHUNK, (c + 1) * CHUNK)
                pe.wait_ge(sem("state_ready"), c + 1)
                if c == 0:
                    pe.wait_ge(sem("solution"), 1)
                for h in range(HEADS):
                    a = slice(64 * (h % 2), 64 * (h % 2) + 64)
                    bank, at = 3 * (h % 2), (h // 2) * DH
                    mm(PS[r, bank, at:at + DH], w_t[a, h // 2, tok], state[a, h // 2, :])
                    at += P * (1 + t)
                    last = mm(PS[r, bank, at:at + DH], qi_t[a, h // 2, tok], state[a, h // 2, :])
                last.then_inc(sem("w_state"), 1)
                pe.wait_ge(sem("v_new"), c + 1)
                for h in range(HEADS):
                    a = slice(64 * (h % 2), 64 * (h % 2) + 64)
                    u = t * HEADS + h
                    mm(PS[r, 1, u * DH:(u + 1) * DH], a_qk[r, u_of(t, h), 64 * half:64 * half + 64], v_new[r, u, :])
                    last = mm(PS[a, 2, (h // 2) * DH:(h // 2 + 1) * DH], ko[r, u, :], v_new[r, u, :])
                last.then_inc(sem("chunk_done"), 1)

            def fox():
                pe.wait_ge(sem("fox_normed"), 1)
                for s in range(2):
                    for pair in range(2):
                        for t in range(TT):
                            last = pe.transpose(PS[:, s, pair * TOK + t * P:pair * TOK + (t + 1) * P],
                                                tokm[:, t, s, pair * P:(pair + 1) * P], ident[:, :])
                last.then_inc(sem("fox_turned"), 1)
                pe.wait_ge(sem("fox_copied"), 1)
                for h in range(HEADS):
                    a = slice(64 * (h % 2), 64 * (h % 2) + 64)
                    q, k = fq_t[a, h // 2, :], fk_t[a, h // 2, :]
                    n0 = nlf[:, 0, h:h + 1].to_broadcast([P, P])
                    n1 = nlf[:, 1, h:h + 1].to_broadcast([P, P])
                    hh, pair = h % 2, h // 2
                    o = PS[:, 2 + hh, pair * P:(pair + 1) * P]
                    mm(o, q[:, 0:P], k[:, 0:P], True, False)
                    mm(o, n0, mask("tri"), False, False)
                    mm(o, ident[:, :], mask("fox_add"), False, True)
                    o = PS[:, hh, pair * TOK:(pair + 1) * TOK]
                    tri_ones = masks[:, MASK["tri"]:MASK["tri"] + 2, :].rearrange("p a n -> p (a n)")
                    mm(o, q[:, P:TOK], k, True, False)
                    mm(o, n0, tri_ones, False, False)
                    mm(o[:, P:TOK], n1, mask("tri"), False, False)
                    last = mm(o[:, P:TOK], ident[:, :], mask("fox_add"), False, True)
                last.then_inc(sem("fox_logits"), 1)
                pe.wait_ge(sem("fox_probs"), 8)
                for h in range(HEADS):
                    pe.transpose(PS[:, 3, h * P:(h + 1) * P], probs0[:, h, :], ident[:, :])
                    for j in range(2):
                        last = pe.transpose(PS[:, 6 + h // 2, ((h % 2) * 2 + j) * P:((h % 2) * 2 + j + 1) * P],
                                            probs1[:, h, j * P:(j + 1) * P], ident[:, :])
                last.then_inc(sem("fox_probs_turned"), 1)
                pe.wait_ge(sem("fox_probs_copied"), 2)
                for h in range(HEADS):
                    v = lambda t: tokm[:, t, TOKM["fox_v"], h * DH:(h + 1) * DH]
                    mm(PS[:, 2, h * DH:(h + 1) * DH], probs_t[:, h, :], v(0))
                    o = PS[:, 2, 256 + h * DH:256 + (h + 1) * DH]
                    mm(o, probs_t[:, 4 + 2 * h, :], v(0), True, False)
                    last = mm(o, probs_t[:, 5 + 2 * h, :], v(1), False, True)
                last.then_inc(sem("fox_out"), 1)

            def la_keys():
                pe.wait_ge(sem("hg_keys"), 1)
                for f in range(2):
                    for t in range(TT):
                        last = pe.transpose(PS[:, 6, f * TOK + t * P:f * TOK + (t + 1) * P],
                                            tokm[:, t, TOKM["hg_f"], f * P:(f + 1) * P], ident[:, :])
                last.then_inc(sem("hg_keys_turned"), 1)

            exps = PS[:, 6:8, :].rearrange("p b n -> p (b n)")

            def la_exponents(lv):
                if lv:
                    pe.wait_ge(sem("level_exp"), lv)
                else:
                    pe.wait_ge(sem("la_ready"), 1)
                for f in range(3):
                    for t in range(TT):
                        m = mask(f"e{1 << lv}") if lv < 7 else mask("after" if t == 0 else "tri")
                        last = mm(exps[:, f * TOK + t * P:f * TOK + (t + 1) * P], la[:, t, f, :], m)
                last.then_inc(sem("exps"), 1)

            def la_rows(h):
                if h < 4:
                    return slice(64 * (h % 2), 64 * (h % 2) + 64), h // 2
                return slice(32 * (h - 4), 32 * (h - 4) + 32), 2

            def la_pairs(lv):
                if lv >= 0:
                    pe.wait_ge(sem("level_operand"), lv + 1)
                if lv >= 0:
                    pe.wait_ge(sem("pairs_read"), lv + 1)
                for h in range(8):
                    r, f = la_rows(h)
                    k, q = ((chm[r, 9 + f, :], chm[r, 6 + f, :]) if lv < 0 else
                            (z_lv[r, lv % 2, f * TOK:(f + 1) * TOK],) * 2)
                    if lv < 7:
                        for t in range(TT):
                            c = slice(t * P, (t + 1) * P)
                            last = mm(pair_bank(t, h), k[:, c], q[:, c])
                    else:
                        last = mm(pair_bank(0, h), k[:, 0:P], q[:, P:TOK])
                last.then_inc(sem("pairs"), 1)

            def la_all():
                pe.wait_ge(sem("la_keys"), 1)
                la_exponents(0)
                pe.wait_ge(sem("pairs_free"), 1)
                la_pairs(-1)
                for lv in range(8):
                    if lv < 7:
                        la_exponents(lv + 1)
                    la_pairs(lv)
                pe.wait_ge(sem("pairs_read"), 9)
                for h in range(8):
                    src = tokm[:, :, TOKM["hg_i"] if h < 4 else TOKM["gla_v"], (h % 4) * DH:(h % 4 + 1) * DH]
                    o = lambda t: PS[:, 6 + h // 4, t * 256 + (h % 4) * DH:t * 256 + (h % 4 + 1) * DH]
                    mm(o(0), a_la[:, la_unit(0, h), :], src[:, 0, :])
                    mm(o(1), a_top[:, la_top_unit(h), :], src[:, 0, :], True, False)
                    last = mm(o(1), a_la[:, la_unit(1, h), :], src[:, 1, :], False, True)
                last.then_inc(sem("la_out"), 1)

            between = {0: [gates], 3: [gdn_tokens, gdn_channels], 4: [gdn_grams],
                       5: [lambda: gdn_invert(0)], 6: [lambda: gdn_invert(1)], 7: [lambda: gdn_invert(2)],
                       8: [lambda: gdn_invert(3)], 9: [lambda: gdn_invert(4)], 10: [gdn_solve],
                       11: [lambda: gdn_chunk(0)], 12: [lambda: gdn_chunk(1)], 13: [lambda: gdn_chunk(2)],
                       14: [lambda: gdn_chunk(3), fox, la_keys, la_all]}
            for n, what in enumerate(MIX_ORDER):
                if n >= 2:
                    pe.wait_ge(sem(f"proj_bank_read{n % 2}"), n // 2)
                elif n == 0:
                    chunks_ready("norm1", 1)
                else:
                    chunks_ready("norm1", 7)
                columns(n, n % RING, 4 + n % 2, (h_hi, h_lo), what in CHANNEL_MAJOR, SMALL if n == 0 else 256,
                        "norm1" if n == 0 else None)
                for piece in between.get(n, ()):
                    piece()

            pe.wait_ge(sem("mix_done"), 1)
            turn("mixed", xn)

            def rows_4(name, acc, operand, fresh=None, tiles=True):
                for j in range(4):
                    n = STEP[name] + j
                    if fresh:
                        chunks_ready(fresh, 2 * j)
                    row_block(n, n % RING, acc, operand, 2 * j, j == 0, j == 3, tiles and j == 3)

            rows_4("mix_out", low4, (act_hi, act_lo), "mixed")

            def ffn(f, fresh, p_name=None):
                n0 = STEP[f"ffn{f}"]
                slot = lambda j: (n0 + j) % RING
                for t in range(TT):
                    for half in range(2):
                        pe.matmul(low4[:, t, half * 512:(half + 1) * 512], zeros_r[:, 0:P], zeros_r[:, :],
                                  start=True, stop=False, skip_group_check=True)
                chunks_ready(fresh, 1)
                columns(n0, slot(0), 4, (h_hi, h_lo), fresh=fresh)
                columns(n0 + 1, slot(1), 5, (h_hi, h_lo))
                if p_name:
                    pe.wait_ge(sem("p_loaded"), 16 * f)
                    turn(p_name, p_tok, 6)
                with pe.Fori(1, PAIRS) as i:
                    n = n0 - 1 + 3 * i
                    pe.wait_ge(sem("gate_convolved"), PAIRS * f + i)
                    columns(n, slot(2), 4, (h_hi, h_lo))
                    pe.wait_ge(sem("up_read"), PAIRS * f + i)
                    columns(n + 1, slot(0), 5, (h_hi, h_lo))
                    pe.wait_ge(sem("hidden_split"), PAIRS * f + i)
                    row_block(n + 2, slot(1), low4, (hid_hi, hid_lo), 0, False, False)
                pe.wait_ge(sem("hidden_split"), PAIRS * (f + 1))
                n = n0 + 3 * PAIRS - 1
                row_block(n, n % RING, low4, (hid_hi, hid_lo), 0, False, True, True)

            pe.wait_ge(sem("zeros"), 1)
            turn("norm2", xn, tile_ready=2)
            ffn(0, "norm2")

            turn("pre_mix0", xn, tile_ready=3)
            chunks_ready("pre_mix0", 7)
            pe.wait_ge(sem("table_loaded"), 32)
            mm(PS[0:N_HEADS, 7, 0:N_DIST], table, onehot).then_inc(sem("bias_by_head"), 1)
            n0 = STEP["sc_in"]
            with pe.Fori(0, 4) as i:
                for j in range(3):
                    pe.wait_ge(sem("sc_bank_read"), 3 * i + (j + 1))
                    columns(n0 + j + 3 * i, (n0 + j) % RING, 4 + j, (h_hi, h_lo))
            pe.wait_ge(sem("sc_hidden"), 4)
            rows_4("sc_out", low4, (act_hi, act_lo))

            def ffn_and_ple(layer):
                k = 4 if layer == 0 else 7
                turn(f"pre_ffn{layer}", xn, tile_ready=k)
                ffn(1 + layer, f"pre_ffn{layer}", f"p{layer}")
                pe.wait_ge(sem("x_tile"), 2 * k)
                chunks_ready(f"p{layer}", 1)
                n = STEP[f"ple_proj{layer}"]
                row_block(n, n % RING, low4, (p_hi, p_lo), 0, True, True)
                turn(f"pre_ple{layer}", xn, tile_ready=k + 1)
                chunks_ready(f"pre_ple{layer}", 7)
                rows_4(f"ple_gate{layer}", high4, (h_hi, h_lo))

            ffn_and_ple(0)

            turn("pre_mix1", xn, tile_ready=6)
            chunks_ready("pre_mix1", 7)

            def turn_weights(h):
                if h == 2:
                    pe.wait_ge(sem("att_bank_read0"), 4)
                if h >= 1:
                    pe.wait_ge(sem("att_copied"), h)
                pe.wait_ge(sem("att_weights"), h + 1)
                for j in range(3):
                    last = pe.transpose(PS[:, 3 if h < 2 else 4, j * P:(j + 1) * P], at_w[:, j, :], ident[:, :])
                last.then_inc(sem("att_turned"), 1)

            def logits(h):
                if h:
                    pe.wait_ge(sem("logits_read"), h)
                else:
                    pe.wait_ge(sem("att_bank_read0"), 3)
                if h == 2:
                    pe.wait_ge(sem("att_bank_read1"), 3)
                if h == 4:
                    pe.wait_ge(sem("att_bank_read0"), 4)
                if h == 6:
                    pe.wait_ge(sem("att_bank_read1"), 4)
                for m in range(2):
                    r = slice(64 * m, 64 * m + 64)
                    mm(PS[:, 6 + m, 0:TOK], q_t[r, h, P:TOK], k_t[r, h, :])
                    last = mm(PS[:, 6 + m, TOK:TOK + P], q_t[r, h, 0:P], k_t[r, h, 0:P])
                last.then_inc(sem("logits"), 1)

            for j in range(8):
                n = STEP["att_k"] + j
                if j >= 2:
                    pe.wait_ge(sem(f"att_bank_read{j % 2}"), j // 2)
                columns(n, n % RING, 4 + j % 2, (act_hi, act_lo) if j < 4 else (h_hi, h_lo))
                if j == 2:
                    pe.wait_ge(sem("flip_loaded"), 16)
                    pe.wait_ge(sem("bias_loaded"), 16)
                    for b in range(4):
                        last = mm(PS[:, b, :], flip, bias_rev[:, 2 * b:2 * b + 2, :].rearrange("p h n -> p (h n)"))
                    last.then_inc(sem("bias_flipped"), 1)
                if j >= 5:
                    if j == 6:
                        pe.wait_ge(sem("bias_copied"), 1)
                    if j > 5:
                        turn_weights(j - 6)
                    logits(j - 5)
            pe.wait_ge(sem("att_copied"), 2)
            for j in range(4):
                n = STEP["att_v"] + j
                row_block(n, n % RING, low4, (act_hi, act_lo), 2 * j, j == 0, j == 3)
                turn_weights(j + 2)
                logits(j + 3)
            turn_weights(6)
            logits(7)
            turn_weights(7)
            pe.wait_ge(sem("v_copied"), 2)
            for t in range(TT):
                for h in range(N_HEADS):
                    pe.wait_ge(sem("att_copied"), h + 1)
                    v = lambda t: v_tok[:, t, h * P:(h + 1) * P]
                    o = low4[:, t, h * P:(h + 1) * P]
                    if t == 0:
                        last = mm(o, at_wt[:, h, 2, :], v(0))
                    else:
                        mm(o, at_wt[:, h, 0, :], v(0), True, False)
                        last = mm(o, at_wt[:, h, 1, :], v(1), False, True)
                last.then_inc(sem("head_out"), 1)
            for t in range(TT):
                pe.wait_ge(sem("heads_normed"), t + 1)
            turn("att", xn)
            rows_4("att_out", low4, (act_hi, act_lo), "att")
            ffn_and_ple(1)

        @block.scalar
        def _(act):
            own, count = sem("act_own"), [0]

            def mark(ins):
                count[0] += 1
                ins.then_inc(own, 1)

            def link(ins):
                mark(ins)
                act.wait_ge(own, count[0])

            def split(n, slot, lap, steady=True):
                act.wait_ge(raw_loaded[slot], 16 * lap)
                if steady:
                    act.wait_ge(block_used, n - (RING - 1))
                act.activation(w_hi[:, slot, :], raw[:, slot, :], ACT.Copy).then_inc(hi_ready, 1)

            def ahead(n):
                if n + 2 < N_BLOCKS:
                    split(n + 2, (n + 2) % RING, (n + 2) // RING + 1, n + 2 >= RING)

            def ahead_in_loop(n_base, i):
                m = n_base + 2
                split(m + 3 * i, m % RING, i + (m // RING + 1))

            def inverse_rms(s, n, done=None):
                link(act.activation(s, s, ACT.Ln, scale=1.0 / n, bias=eps[:, :]))
                ins = act.activation(s, s, ACT.Exp, scale=-0.5)
                if done is None:
                    link(ins)
                else:
                    ins.then_inc(done, 1)

            def norm(k, squares):
                s = stat[:, 2 * (k % 2):2 * (k % 2) + 2]
                if k > 1:
                    act.wait_ge(sem("x_tile"), 2 * k - 3)
                link(act.activation(squares, x[:, 0, :], ACT.Square, accum_out=s[:, 0:1]))
                inverse_rms(s[:, 0:1], D)
                act.activation(xn[:, 0, :], x[:, 0, :], ACT.Copy, scale=s[:, 0:1]).then_inc(sem("tokens0_ready"), 1)
                act.wait_ge(sem("squares1"), k)
                inverse_rms(s[:, 1:2], D, sem("rstd1"))

            def turned(name, operands, bank=4):
                _, p0, chunks = TURN[name]
                for b in range(chunks // 2):
                    act.wait_ge(chunks_turned, p0 + b + 1)
                    for gain, hi, _ in operands:
                        for j in (2 * b, 2 * b + 1):
                            src = PS[:, bank + b, (j % 2) * TOK:(j % 2 + 1) * TOK]
                            if gain is None:
                                ins = act.activation(hi[:, j, :], src, ACT.Copy)
                            else:
                                ins = act.activation(hi[:, j, :], src, ACT.Identity, scale=gain(j))
                    ins.then_inc(part_hi, 1)

            act.preload_act_table_set(TABLES)
            act.wait_ge(inputs, N_INPUTS)
            act.wait_ge(sem("eps_set"), 1)
            norm(1, sq)
            split(0, 0, 1, False)
            split(1, 1, 1, False)
            turned("norm1", [(lambda j: ch("norm1", j), h_hi, h_lo)])

            def gates():
                act.wait_ge(sem("gates_z"), 1)
                act.wait_ge(sem("mix_inputs"), 48)
                link(act.activation(gate_l, gate_z, ACT.Abs))
                link(act.activation(gate_l, gate_l, ACT.Exp, scale=-1.0))
                act.activation(gate_l, gate_l, ACT.Ln, bias=1.0)
                act.activation(ea, rows("gdn_a_log", 4), ACT.Exp)
                act.activation(beta, small[:, :, 8:12], ACT.Exp, scale=-1.0).then_inc(sem("gates_exp"), 1)
                act.wait_ge(sem("gate_sums"), 1)
                act.activation(th(e_g), PS[:, 0, 0:8], ACT.Exp)
                act.activation(th(e_rest), PS[:, 0, 8:16], ACT.Exp)
                act.activation(e_last.rearrange("p t c h -> p (t c h)"), PS[:, 0, 16:32], ACT.Exp) \
                    .then_inc(sem("gate_exps"), 1)
                act.wait_ge(sem("gk_turned"), 1)
                act.activation(gk_t, PS[0:16, 1, 0:TOK], ACT.Copy).then_inc(sem("gk_copied"), 1)
                log_sigmoid(la[:, :, 2, :], 1)

            def log_sigmoid(dst, k):
                act.wait_ge(sem("logits_z"), k)
                s = sq[:, (k - 1) * 512:(k - 1) * 512 + dst.shape[1] * dst.shape[2]].rearrange("p (t n) -> p t n", t=TT)
                link(act.activation(s, dst, ACT.Abs))
                link(act.activation(s, s, ACT.Exp, scale=-1.0))
                act.activation(s, s, ACT.Ln, bias=1.0).then_inc(sem("logits_ln"), 1)

            def gdn_tokens():
                act.wait_ge(sem("gdn_taps"), 1)
                v = chm[:, 0:6, :].rearrange("p f n -> p (f n)")
                act.activation(v, v, ACT.Silu).then_inc(sem("gdn_convolved"), 1)
                act.preload_act_table_set(TABLES)
                act.wait_ge(sem("gdn_token_major"), 1)
                act.wait_ge(sem("sq_free"), 1)
                act.activation(sq, PS[:, 0:2, :].rearrange("p b n -> p (b n)"), ACT.Square).then_inc(sem("gdn_squares"), 1)
                rstd16("gdn_sums", "gdn_rstd", 1.0)

            def rstd16(ready, done, scale, n=16):
                act.wait_ge(sem(ready), 1)
                s = stat[:, 8:8 + n]
                link(act.activation(s, s, ACT.Ln, scale=scale, bias=eps[:, :]))
                act.activation(s, s, ACT.Exp, scale=-0.5).then_inc(sem(done), 1)

            def gdn_channels():
                act.wait_ge(sem("gdn_channel_major"), 1)
                act.activation(chm[:, 0:6, :].rearrange("p f n -> p (f n)"),
                               PS[:, 0:3, :].rearrange("p b n -> p (b n)"), ACT.Copy).then_inc(sem("gdn_copied"), 1)

            bank2 = lambda b: PS[:, b:b + 2, :].rearrange("p b n -> p (b n)")
            flat = lambda v: v.rearrange("p u n -> p (u n)")

            def gdn_grams():
                act.wait_ge(sem("decay_logs"), 1)
                act.activation(flat(dec), bank2(2), ACT.Exp).then_inc(sem("decay"), 1)
                act.wait_ge(sem("decay_turned"), 1)
                act.activation(flat(dec_t), bank2(2), ACT.Copy).then_inc(sem("decay_t"), 1)
                act.wait_ge(sem("m_turned"), 1)
                act.activation(flat(mt_gd), bank2(0), ACT.Copy).then_inc(sem("mt_ready"), 1)

            def gdn_invert(lv):
                act.wait_ge(sem("cx"), lv + 1)
                act.activation(flat(y_gd), bank2(2), ACT.Copy).then_inc(sem("cx_copied"), 1)

            def gdn_solve():
                act.wait_ge(sem("solved"), 1)
                act.activation(flat(u_gd), PS[:, 2, :], ACT.Copy)
                act.activation(flat(w_t), PS[:, 3, :], ACT.Copy).then_inc(sem("solution"), 1)

            def head_post(k, grp):
                act.wait_ge(sem("group_out"), k + 1)
                act.activation(sq[:, 0:512].rearrange("p (t n) -> p t n", t=TT), group_view(grp), ACT.Square) \
                    .then_inc(sem("group_squares"), 1)
                act.wait_ge(sem("group_sums"), k + 1)
                s = stat[:, 8:16]
                link(act.activation(s, s, ACT.Ln, scale=1.0 / DH, bias=eps[:, :]))
                act.activation(s, s, ACT.Exp, scale=-0.5).then_inc(sem("group_rstd"), 1)

            def silu_gates():
                act.wait_ge(sem("proj_bank_read0"), 8)
                act.wait_ge(sem("proj_bank_read1"), 7)
                act.activation(tokm[:, :, 6:9, :], tokm[:, :, 6:9, :], ACT.Silu)
                act.activation(chm[:, 6:8, :], chm[:, 6:8, :], ACT.Silu).then_inc(sem("gates_silu"), 1)
                act.preload_act_table_set(TABLES)

            def fox():
                act.wait_ge(sem("sq_free"), 3)
                act.activation(sq.rearrange("p (t s n) -> p t s n", t=TT, s=2), tokm[:, :, 0:2, :], ACT.Square) \
                    .then_inc(sem("fox_squares"), 1)
                rstd16("fox_sums", "fox_rstd", 1.0 / DH)
                act.wait_ge(sem("fox_turned"), 1)
                act.activation(flat(fq_t), PS[:, 0, :], ACT.Copy)
                act.activation(flat(fk_t), PS[:, 1, :], ACT.Copy).then_inc(sem("fox_copied"), 1)
                act.wait_ge(sem("fox_max"), 2)
                for h in range(HEADS):
                    m = (h % 2) * 2 + h // 2
                    act.activation(probs0[:, h, :], PS[:, 2 + h % 2, h // 2 * P:(h // 2 + 1) * P], ACT.Exp,
                                   bias=stat[:, 24 + m:25 + m],
                                   accum_out=stat[:, 32 + h:33 + h]).then_inc(sem("fox_probs"), 1)
                    act.activation(probs1[:, h, :], PS[:, h % 2, h // 2 * TOK:(h // 2 + 1) * TOK], ACT.Exp,
                                   bias=stat[:, 28 + m:29 + m], accum_out=stat[:, 36 + h:37 + h]) \
                        .then_inc(sem("fox_probs"), 1)
                act.wait_ge(sem("fox_probs_turned"), 1)
                act.activation(flat(probs_t[:, 0:4, :]), PS[:, 3, :], ACT.Copy).then_inc(sem("fox_probs_copied"), 1)
                act.activation(flat(probs_t[:, 4:12, :]), bank2(6), ACT.Copy).then_inc(sem("fox_probs_copied"), 1)

            def la_keys():
                log_sigmoid(tokm[:, :, TOKM["hg_f"], :], 2)
                act.wait_ge(sem("hg_keys_log"), 1)
                z = tokm[:, :, TOKM["hg_f"], :]
                act.activation(z, z, ACT.Exp).then_inc(sem("hg_keys"), 1)
                act.wait_ge(sem("hg_keys_turned"), 1)
                act.activation(chm[:, 9:11, :].rearrange("p f n -> p (f n)"), PS[:, 6, :], ACT.Copy) \
                    .then_inc(sem("la_keys"), 1)

            def la_all():
                for lv in range(8):
                    act.wait_ge(sem("exps"), lv + 1)
                    if lv >= 2:
                        act.wait_ge(sem("level_operand"), lv - 1)
                    act.activation(w_lv[:, lv % 2, :], bank2(6)[:, 0:768], ACT.Exp).then_inc(sem("level_exp"), 1)

            between = {0: [gates], 3: [gdn_tokens, gdn_channels], 4: [gdn_grams],
                       5: [lambda: gdn_invert(0)], 6: [lambda: gdn_invert(1)], 7: [lambda: gdn_invert(2)],
                       8: [lambda: gdn_invert(3)], 9: [lambda: gdn_invert(4)], 10: [gdn_solve],
                       14: [silu_gates, lambda: head_post(0, 1), fox, lambda: head_post(1, 0), la_keys, la_all,
                            lambda: head_post(2, 2), lambda: head_post(3, 3)]}
            for n, what in enumerate(MIX_ORDER):
                ahead(n)
                act.wait_ge(block_used, n + 1)
                bank = PS[:, 4 + n % 2, :]
                read = sem(f"proj_bank_read{n % 2}")
                if what == "small":
                    act.activation(small, bank.rearrange("p (t n) -> p t n", t=TT)[:, :, 0:SMALL], ACT.Copy) \
                        .then_inc(read, 1)
                elif what.startswith("gdn_") and what in CHANNEL_MAJOR:
                    s = ("gdn_q", "gdn_k", "gdn_v").index(what)
                    for f in range(2):
                        ins = act.activation(chm[:, 2 * s + f, :], bank[:, f * TOK:(f + 1) * TOK], ACT.Identity,
                                             scale=ch("gdn_conv", 3 * 6 + 2 * s + f))
                    ins.then_inc(sem("gdn_last_tap"), 1)
                elif what == "hg_q":
                    act.activation(chm[:, 6:8, :].rearrange("p f n -> p (f n)"), bank, ACT.Copy).then_inc(read, 1)
                elif what == "gla_qk":
                    act.activation(chm[:, 8, :], bank[:, 0:TOK], ACT.Copy, scale=32.0 ** -0.5)
                    act.activation(chm[:, 11, :], bank[:, TOK:512], ACT.Copy).then_inc(read, 1)
                else:
                    act.activation(tokm[:, :, TOKM[what], :], bank.rearrange("p (t n) -> p t n", t=TT), ACT.Copy) \
                        .then_inc(read, 1)
                for piece in between.get(n, ()):
                    piece()

            turned("mixed", [(None, act_hi, act_lo)])

            def ahead_4(name):
                for j in range(4):
                    ahead(STEP[name] + j)

            ahead_4("mix_out")

            norm(2, junk[:, 0, :])
            turned("norm2", [(lambda j: ch("norm2", j), h_hi, h_lo)])

            def ffn(f, p_name=None):
                n0 = STEP[f"ffn{f}"]
                conv = PC[f"ffn_conv{f}"]

                def last_tap(dst, bank, i, half, ready):
                    for c in range(2):
                        col = i * 2 + (half * FT + c)
                        w = channel[:, bass.ds(col + (conv + 2 * 2 * FT), 1)]
                        b = channel[:, bass.ds(col + PC["ffn_bias"], 1)] if f == 0 else 0.0
                        ins = act.activation(dst[:, c, :], PS[:, bank, c * TOK:(c + 1) * TOK], ACT.Identity,
                                             scale=w, bias=b)
                    ins.then_inc(ready, 1)

                def gate(i, n_used):
                    act.wait_ge(block_used, n_used)
                    last_tap(y_gate, 4, i, 0, sem("gate_last_tap"))

                def up(i, n_used):
                    act.wait_ge(sem("gate_convolved"), i + (PAIRS * f + 1))
                    act.activation(s_gate, y_gate, ACT.Silu).then_inc(sem("gate_silu"), 1)
                    act.wait_ge(block_used, n_used)
                    last_tap(y_up, 5, i, 1, sem("up_last_tap"))

                def hid(i):
                    act.wait_ge(sem("hidden_ready"), i + (PAIRS * f + 1))
                    act.activation(hid_hi, hidden, ACT.Copy).then_inc(sem("hidden_hi"), 1)

                ahead(n0)
                gate(0, n0 + 1)
                ahead(n0 + 1)
                up(0, n0 + 2)
                hid(0)
                if p_name:
                    turned(p_name, [(None, p_hi, p_lo)], 6)
                with act.Fori(1, PAIRS) as i:
                    n = n0 - 1
                    ahead_in_loop(n, i)
                    gate(i, n + 1 + 3 * i)
                    ahead_in_loop(n + 1, i)
                    up(i, n + 2 + 3 * i)
                    ahead_in_loop(n + 2, i)
                    act.wait_ge(block_used, n + 3 + 3 * i)
                    hid(i)
                ahead(n0 + 3 * PAIRS - 1)
                act.preload_act_table_set(TABLES)

            ffn(0)

            norm(3, junk[:, 0, :])
            turned("pre_mix0", [(lambda j: ch("pre_mix0", j), h_hi, h_lo)])
            act.wait_ge(sem("bias_by_head"), 1)
            act.activation(bias_row, PS[0:N_HEADS, 7, 0:N_DIST], ACT.Copy).then_inc(sem("bias_rows"), 1)
            n0 = STEP["sc_in"]
            with act.Fori(0, 4) as i:
                ahead_in_loop(n0, i)
                act.wait_ge(block_used, n0 + 1 + 3 * i)
                act.activation(flat(s_gate), PS[:, 4, :], ACT.Copy).then_inc(sem("sc_gc"), 1)
                ahead_in_loop(n0 + 1, i)
                act.wait_ge(sem("sc_product"), i + 1)
                for c in range(2):
                    ins = act.activation(y_gate[:, c, :], y_up[:, c, :], ACT.Identity,
                                         scale=channel[:, bass.ds(2 * i + (PC["sc_conv"] + 16 + c), 1)])
                ins.then_inc(sem("sc_last_tap"), 1)
                ahead_in_loop(n0 + 2, i)
                act.wait_ge(sem("sc_gated"), i + 1)
                act.activation(act_hi[:, bass.ds(2 * i, 2), :], hidden, ACT.Copy).then_inc(sem("sc_hi"), 1)
            ahead_4("sc_out")

            def post(k, n_used):
                for t in range(TT):
                    if t == 0:
                        act.wait_ge(sem("tile_summed"), k)
                    else:
                        act.wait_ge(block_used, n_used)
                    s = stat[:, 4 + t:5 + t]
                    link(act.activation(junk[:, t, :], low4[:, t, :], ACT.Square, accum_out=s))
                    inverse_rms(s, D, sem("post_rstd"))

            post(3, STEP["sc_out"] + 4)
            norm(4, gate_s[:, 0, :])
            turned("pre_ffn0", [(lambda j: ch("pre_ffn0", j), h_hi, h_lo)])

            def ffn_and_ple(layer, k):
                ffn(1 + layer, f"p{layer}")
                post(k, STEP[f"ffn{1 + layer}"] + 3 * PAIRS)
                norm(k + 1, gate_s[:, 0, :])
                turned(f"pre_ple{layer}", [(lambda j: ch(f"pre_ple{layer}", j), h_hi, h_lo)])
                ahead(STEP[f"ple_proj{layer}"])
                for j in range(3):
                    ahead(STEP[f"ple_gate{layer}"] + j)
                act.wait_ge(sem("tile_summed"), k + 1)
                act.activation(gate_s[:, 0, :], high4[:, 0, :], ACT.Sigmoid).then_inc(sem("ple_gate"), 1)
                ahead(STEP[f"ple_gate{layer}"] + 3)
                act.wait_ge(block_used, STEP[f"ple_gate{layer}"] + 4)
                act.activation(gate_s[:, 1, :], high4[:, 1, :], ACT.Sigmoid).then_inc(sem("ple_gate"), 1)
                act.preload_act_table_set(TABLES)
                for t in range(TT):
                    act.wait_ge(sem("ple_product"), 2 * layer + t + 1)
                    s = stat[:, 4 + t:5 + t]
                    link(act.activation(junk[:, t, :], gate_s[:, t, :], ACT.Square, accum_out=s))
                    inverse_rms(s, D, sem("post_rstd"))

            ffn_and_ple(0, 4)
            norm(6, junk[:, 0, :])
            turned("pre_mix1", [(lambda j: ch("pre_mix1", j), h_hi, h_lo), (lambda j: ch("kv", j), act_hi, act_lo)])

            def soften(h):
                act.wait_ge(sem("att_max"), 2 * (h + 1))
                a = att_stat
                for m in range(2):
                    act.activation(lg1[:, m, :], lg1[:, m, :], ACT.Exp, bias=a[:, m:m + 1], accum_out=a[:, 4 + m:5 + m])
                    ins = act.activation(lg0[:, m, :], lg0[:, m, :], ACT.Exp, bias=a[:, 2 + m:3 + m],
                                         accum_out=a[:, 6 + m:7 + m])
                ins.then_inc(sem("att_exp"), 1)

            def copy_weights(h):
                act.wait_ge(sem("att_turned"), h + 1)
                act.activation(flat(at_wt[:, h, :, :]), PS[:, 3 if h < 2 else 4, 0:384], ACT.Copy) \
                    .then_inc(sem("att_copied"), 1)

            for j in range(8):
                n = STEP["att_k"] + j
                ahead(n)
                act.wait_ge(block_used, n + 1)
                dst, scale = (k_t, 1.0) if j < 4 else (q_t, DH ** -0.5)
                i = 2 * (j % 4)
                act.activation(flat(dst[:, i:i + 2, :]), PS[:, 4 + j % 2, :], ACT.Copy, scale=scale) \
                    .then_inc(sem(f"att_bank_read{j % 2}"), 1)
                if j == 0:
                    act.wait_ge(sem("lambda_sums"), 1)
                    act.activation(lam[:, 0:2], lam[:, 0:2], ACT.Exp).then_inc(sem("lambda_exps"), 1)
                if j == 2:
                    act.wait_ge(sem("bias_flipped"), 1)
                    act.activation(flat(bias_t), PS[:, 0:4, :].rearrange("p b n -> p (b n)"), ACT.Copy) \
                        .then_inc(sem("bias_copied"), 1)
                if j >= 6:
                    copy_weights(j - 6)
                if j >= 5:
                    soften(j - 5)
            for j in range(4):
                ahead(STEP["att_v"] + j)
                copy_weights(j + 2)
                soften(j + 3)
            act.wait_ge(block_used, STEP["att_v"] + 4)
            act.activation(v_tok, low4, ACT.Copy).then_inc(sem("v_copied"), 2)
            copy_weights(6)
            soften(7)
            copy_weights(7)
            for t in range(TT):
                act.wait_ge(sem("head_out"), t + 1)
                act.activation(xn[:, t, :], low4[:, t, :], ACT.Square).then_inc(sem("head_squares"), 1)
                act.wait_ge(sem("subln_sums"), t + 1)
                s = stat[:, 8 + 8 * t:16 + 8 * t]
                inverse_rms(s, P, sem("subln_rstd"))
            turned("att", [(lambda j: ch("subln"), act_hi, act_lo)])
            ahead_4("att_out")
            post(6, STEP["att_out"] + 4)
            norm(7, gate_s[:, 0, :])
            turned("pre_ffn1", [(lambda j: ch("pre_ffn1", j), h_hi, h_lo)])
            ffn_and_ple(1, 7)

        @block.vector
        def _(dve):
            own, count = sem("dve_own"), [0]

            def mark(ins):
                count[0] += 1
                ins.then_inc(own, 1)

            def settle():
                dve.wait_ge(own, count[0])

            def link(ins):
                mark(ins)
                settle()

            def signal(which, n=1):
                settle()
                dve.sem_inc(which, n)

            tt, ts, stt = dve.tensor_tensor, dve.tensor_scalar, dve.scalar_tensor_tensor

            def split(n, slot):
                dve.wait_ge(hi_ready, n + 1)
                tt(w_lo[:, slot, :], raw[:, slot, :], w_hi[:, slot, :].bitcast(F), ALU.subtract).then_inc(lo_ready, 1)

            def ahead(n):
                if n + 2 < N_BLOCKS:
                    split(n + 2, (n + 2) % RING)

            def norm(k, squares):
                s = stat[:, 2 * (k % 2) + 1:2 * (k % 2) + 2]
                if k > 1:
                    dve.wait_ge(sem("x_tile"), 2 * k - 2)
                dve.tensor_tensor_reduce(squares, x[:, 1, :], x[:, 1, :], 1.0, 0.0, ALU.mult, ALU.add, s) \
                    .then_inc(sem("squares1"), 1)
                dve.wait_ge(sem("rstd1"), k)
                ts(xn[:, 1, :], x[:, 1, :], s, None, ALU.mult).then_inc(sem("tokens1_ready"), 1)

            def turned(name, operands, bank=4):
                _, p0, chunks = TURN[name]
                for b in range(chunks // 2):
                    dve.wait_ge(part_hi, p0 + b + 1)
                    for gain, hi, lo in operands:
                        for j in (2 * b, 2 * b + 1):
                            src = PS[:, bank + b, (j % 2) * TOK:(j % 2 + 1) * TOK]
                            if gain is None:
                                ins = tt(lo[:, j, :], src, hi[:, j, :].bitcast(F), ALU.subtract)
                            else:
                                ins = stt(lo[:, j, :], src, gain(j), hi[:, j, :].bitcast(F), ALU.mult, ALU.subtract)
                    ins.then_inc(part_ready, 1)

            dve.wait_ge(inputs, N_INPUTS)
            norm(1, z_lv.rearrange("p a n -> p (a n)")[:, 0:D])
            split(0, 0)
            split(1, 1)
            turned("norm1", [(lambda j: ch("norm1", j), h_hi, h_lo)])

            def sigmoid_rest(v):
                link(ts(v, v, 1.0, None, ALU.add))
                dve.reciprocal(v, v)

            def gates():
                dve.wait_ge(sem("proj_bank_read0"), 1)
                dve.wait_ge(sem("mix_inputs"), 48)
                tt(gate_z, small[:, :, 0:8], row[:, 0:8].rearrange("p (o n) -> p o n", o=1).to_broadcast([P, TT, 8]),
                   ALU.add).then_inc(sem("gates_z"), 1)
                dve.wait_ge(sem("gates_exp"), 1)
                mark(stt(lf, gate_z[:, :, 0:4], 0.0, gate_l[:, :, 0:4], ALU.min, ALU.subtract))
                mark(stt(gd, gate_z[:, :, 4:8], 0.0, gate_l[:, :, 4:8], ALU.max, ALU.add))
                mark(ts(beta, beta, 1.0, None, ALU.add))
                settle()
                mark(ts(nlf, lf, -1.0, None, ALU.mult))
                mark(dve.reciprocal(beta, beta))
                mark(tt(ngd, gd, ea.rearrange("p (o n) -> p o n", o=1).to_broadcast([P, TT, 4]), ALU.mult))
                settle()
                ts(gd, ngd, -1.0, None, ALU.mult).then_inc(sem("gates_ready"), 1)
                dve.wait_ge(sem("gate_exps"), 1)
                mark(tt(be_g, beta, e_g, ALU.mult))
                dve.wait_ge(sem("gk_projected"), 1)
                b = rows("b_gk", P).rearrange("p (o n) -> p o n", o=1).to_broadcast([P, TT, P])
                ins = tt(la[:, :, 2, :], PS[:, 1, 256:512].rearrange("p (t n) -> p t n", t=TT), b, ALU.add)
                ins.then_inc(sem("logits_z"), 1)
                dve.wait_ge(sem("logits_z"), 1)
                dve.wait_ge(sem("logits_ln"), 1)
                s = sq[:, 0:256].rearrange("p (t n) -> p t n", t=TT)
                link(stt(la[:, :, 2, :], la[:, :, 2, :], 0.0, s, ALU.min, ALU.subtract))
                mark(ts(la[:, :, 2, :], la[:, :, 2, :], 1.0 / 16.0, None, ALU.mult))
                settle()
                signal(sem("gk_read"), 1)

            def gdn_taps(s, n):
                dve.wait_ge(sem("gdn_last_tap"), s + 1)
                for d in range(1, 4):
                    for f in range(2):
                        dst = chm[:, 2 * s + f, d:TOK]
                        mark(stt(dst, PS[:, 4 + n % 2, f * TOK:(f + 1) * TOK - d], ch("gdn_conv", (3 - d) * 6 + 2 * s + f),
                                 dst, ALU.mult, ALU.add))
                    settle()
                signal(sem(f"proj_bank_read{n % 2}"), 1)

            def gdn_tokens():
                signal(sem("gdn_taps"), 1)
                signal(sem("sq_free"), 1)
                dve.wait_ge(sem("gdn_squares"), 1)
                dve.tensor_reduce(stat[:, 8:24], sq.rearrange("p (u d) -> p u d", d=DH), AX, ALU.add) \
                    .then_inc(sem("gdn_sums"), 1)
                dve.wait_ge(sem("gdn_rstd"), 1)
                link(ts(stat[:, 8:16], stat[:, 8:16], DH ** -0.5, None, ALU.mult))
                psu = lambda b: PS[:, b, :].rearrange("p (u d) -> p u d", d=DH)
                mark(tt(qn, psu(0), unit(stat[:, 8:16], DH), ALU.mult))
                mark(tt(kn, psu(1), unit(stat[:, 16:24], DH), ALU.mult))
                mark(tt(vb, psu(2), unit(th(beta), DH), ALU.mult))
                settle()
                mark(tt(qi, qn, unit(th(e_g), DH), ALU.mult))
                mark(tt(kbg, kn, unit(th(be_g), DH), ALU.mult))
                settle()
                tt(ko, kn, unit(th(e_rest), DH), ALU.mult).then_inc(sem("gdn_normed"), 1)

            bank2 = lambda b: PS[:, b:b + 2, :].rearrange("p b n -> p (b n)").rearrange("p (u n) -> p u n", n=P)

            def gdn_grams():
                dve.wait_ge(sem("decay"), 1)
                for t, h in ALL_UNITS:
                    u = u_of(t, h)
                    ins = stt(m_gd[:, u, :], bank2(0)[:, u, :], beta[:, t, h:h + 1], dec[:, u, :], ALU.mult, ALU.mult)
                ins.then_inc(sem("m_ready"), 1)
                dve.wait_ge(sem("m_ready"), 1)
                dve.wait_ge(sem("decay_t"), 1)
                dve.wait_ge(sem("qk_gram"), 1)
                mark(tt(a_qk, bank2(6), dec_t, ALU.mult))
                dve.wait_ge(sem("mt_ready"), 1)
                mark(tt(inv, m_gd, units(mask("m1"), 8), ALU.mult))
                settle()
                mark(tt(inv_t, mt_gd, units(mask("t1"), 8), ALU.mult))
                mark(tt(inv, units(ident[:, :], 8), inv, ALU.subtract))
                settle()
                tt(inv_t, units(ident[:, :], 8), inv_t, ALU.subtract).then_inc(sem("inv_ready"), 1)
                tt(c_t, mt_gd, units(mask("t2"), 8), ALU.mult).then_inc(sem("ct_ready"), 1)

            def gdn_invert(lv):
                dve.wait_ge(sem("xcx"), lv + 1)
                if lv < 4:
                    tt(c_t, mt_gd, units(mask(f"t{4 << lv}"), 8), ALU.mult).then_inc(sem("ct_ready"), 1)
                    mark(tt(inv, inv, bank2(6), ALU.subtract))
                    settle()
                tt(inv_t, inv_t, bank2(0), ALU.subtract).then_inc(sem("inv_ready"), 1)

            def gdn_solve():
                dve.memset(state, 0.0).then_inc(sem("state_ready"), 1)
                dve.wait_ge(sem("solution"), 1)

            def gdn_chunk(c):
                t, half = divmod(c, 2)
                r = slice(64 * half, 64 * half + 64)
                dve.wait_ge(sem("w_state"), c + 1)
                for hh in range(2):
                    us = slice(t * 4 + hh, t * 4 + hh + 3, 2)
                    ins = tt(v_new[r, us, :], u_gd[r, us, :], PS[r, 3 * hh, 0:P].rearrange("p (h d) -> p h d", d=DH),
                             ALU.subtract)
                ins.then_inc(sem("v_new"), 1)
                dve.wait_ge(sem("chunk_done"), c + 1)
                if c == 3:
                    return
                for h in range(HEADS):
                    a = slice(64 * (h % 2), 64 * (h % 2) + 64)
                    s = state[a, h // 2, :]
                    ins = stt(s, s, e_last[a, t, half, h:h + 1], PS[a, 2, (h // 2) * DH:(h // 2 + 1) * DH],
                              ALU.mult, ALU.add)
                ins.then_inc(sem("state_ready"), 1)

            def head_out(grp, src, scale=None):
                dst = group_view(grp)
                ps = src.rearrange("p (t n) -> p t n", t=TT)
                if scale is None:
                    ins = dve.tensor_copy(dst, ps)
                else:
                    ins = tt(dst.rearrange("p t (h d) -> p t h d", d=DH), ps.rearrange("p t (h d) -> p t h d", d=DH), scale,
                             ALU.mult)
                return ins

            def head_post(k, grp, gain):
                dve.wait_ge(sem("group_squares"), k + 1)
                dve.tensor_reduce(stat[:, 8:16], sq[:, 0:512].rearrange("p (u d) -> p u d", d=DH), AX, ALU.add) \
                    .then_inc(sem("group_sums"), 1)
                dve.wait_ge(sem("group_rstd"), k + 1)
                for t in range(TT):
                    v = group_view(grp)[:, t, :].rearrange("p (h d) -> p h d", d=DH)
                    mark(tt(v, v, unit(stat[:, 8 + 4 * t:12 + 4 * t], DH), ALU.mult))
                settle()
                for t in range(TT):
                    v = group_view(grp)[:, t, :].rearrange("p (h d) -> p h d", d=DH)
                    g = gain if gain is not None else tokm[:, t, 5 + grp, :].rearrange("p (h d) -> p h d", d=DH)
                    mark(tt(v, v, g, ALU.mult))
                settle()

            def silu_gates():
                dve.wait_ge(sem("gates_silu"), 1)
                for i, name in enumerate(("gdn_on", "hg_on", "gla_on")):
                    for t in range(TT):
                        v = tokm[:, t, 6 + i, :].rearrange("p (h d) -> p h d", d=DH)
                        mark(tt(v, v, units(rows(name, DH), HEADS), ALU.mult))
                mark(ts(chm[:, 6:8, :], chm[:, 6:8, :], DH ** -0.5, None, ALU.mult))
                settle()

            def gdn_post():
                mark(head_out(1, PS[:, 1, :]))
                settle()
                for t in range(TT):
                    for hh in range(2):
                        v = group_view(1)[:, t, :].rearrange("p (h d) -> p h d", d=DH)[:, hh:hh + 3:2, :]
                        at = P * (1 + t)
                        ins = tt(v, v, PS[:, 3 * hh, at:at + P].rearrange("p (h d) -> p h d", d=DH), ALU.add)
                ins.then_inc(sem("group_out"), 1)
                head_post(0, 1, None)

            def fox():
                signal(sem("sq_free"), 2)
                dve.wait_ge(sem("fox_squares"), 1)
                dve.tensor_reduce(stat[:, 8:24], sq.rearrange("p (u d) -> p u d", d=DH), AX, ALU.add) \
                    .then_inc(sem("fox_sums"), 1)
                dve.wait_ge(sem("fox_rstd"), 1)
                st = stat[:, 8:24].rearrange("p (t s h) -> p t s h", t=TT, s=2)
                for t in range(TT):
                    for s in range(2):
                        v = tokm[:, t, s, :].rearrange("p (h d) -> p h d", d=DH)
                        mark(tt(v, v, unit(st[:, t, s, :], DH), ALU.mult))
                settle()
                for t in range(TT):
                    for s, name in enumerate(("fox_qn", "fox_kn")):
                        v = tokm[:, t, s, :].rearrange("p (h d) -> p h d", d=DH)
                        mark(tt(v, v, units(rows(name, DH), HEADS), ALU.mult))
                settle()
                ts(tokm[:, :, 0, :], tokm[:, :, 0, :], DH ** -0.5, None, ALU.mult).then_inc(sem("fox_normed"), 1)
                dve.wait_ge(sem("fox_logits"), 1)
                dve.tensor_reduce(stat[:, 24:28], PS[:, 2:4, 0:2 * P].rearrange("p b (h n) -> p b h n", n=P), AX, ALU.max,
                                  negate=True).then_inc(sem("fox_max"), 1)
                dve.tensor_reduce(stat[:, 28:32], PS[:, 0:2, :].rearrange("p b n -> p (b n)")
                                  .rearrange("p (h n) -> p h n", n=TOK), AX, ALU.max, negate=True) \
                    .then_inc(sem("fox_max"), 1)
                dve.wait_ge(sem("fox_probs"), 8)
                link(dve.reciprocal(stat[:, 32:40], stat[:, 32:40]))
                dve.wait_ge(sem("fox_out"), 1)
                for t in range(TT):
                    v = group_view(0)[:, t, :].rearrange("p (h d) -> p h d", d=DH)
                    ins = tt(v, PS[:, 2, t * 256:(t + 1) * 256].rearrange("p (h d) -> p h d", d=DH),
                             unit(stat[:, 32 + 4 * t:36 + 4 * t], DH), ALU.mult)
                ins.then_inc(sem("group_out"), 1)
                head_post(1, 0, units(rows("fox_on", DH), HEADS))

            def la_keys():
                z = tokm[:, :, TOKM["hg_f"], :]
                signal(sem("logits_z"), 1)
                dve.wait_ge(sem("logits_ln"), 2)
                s = sq[:, 512:1024].rearrange("p (t n) -> p t n", t=TT)
                mark(stt(la[:, :, 0:2, :].rearrange("p t f n -> p t (f n)"), z, 0.0, s, ALU.min, ALU.subtract))
                link(stt(z, z, 0.0, s, ALU.max, ALU.add))
                ts(z, z, -1.0, None, ALU.mult).then_inc(sem("hg_keys_log"), 1)
                signal(sem("la_ready"), 1)

            def la_all():
                mark(dve.memset(a_la, 0.0))
                signal(sem("pairs_free"), 1)
                three = lambda v, b: v.rearrange("p (m two n) -> p m two n", two=2, n=b)
                hg_pairs = PS[:, 0:2, :].rearrange("p b n -> p (b n)").rearrange("p (u n) -> p u n", n=P)
                gla_pairs = PS[:, 2:6, 0:2 * P].rearrange("p b (t n) -> p b t n", t=TT)
                gla_a = a_la[:, 8:16, :].rearrange("p (b t) n -> p b t n", t=TT)
                q3 = chm[:, 6:9, :].rearrange("p f n -> p (f n)")
                k3 = chm[:, 9:12, :].rearrange("p f n -> p (f n)")

                def operand(lv):
                    b = 1 << lv
                    dve.wait_ge(sem("level_exp"), lv + 1)
                    if lv == 0:
                        dve.wait_ge(sem("la_keys"), 1)
                    w, z = three(w_lv[:, lv % 2, :], b), three(z_lv[:, lv % 2, :], b)
                    if lv >= 2:
                        dve.wait_ge(sem("pairs"), lv)
                    mark(tt(z[:, :, 0, :], w[:, :, 0, :], three(k3, b)[:, :, 0, :], ALU.mult))
                    tt(z[:, :, 1, :], w[:, :, 1, :], three(q3, b)[:, :, 1, :], ALU.mult).then_inc(sem("level_operand"), 1)

                def select(lv):
                    dve.wait_ge(sem("pairs"), lv + 2)
                    if lv < 0:
                        m = ident[:, :]
                    elif lv < 6:
                        m = mask(f"t{1 << lv}")
                    if lv < 6:
                        m = m.bitcast(I32)
                        mark(dve.copy_predicated(a_la[:, 0:8, :], units(m, 8), hg_pairs))
                        m4 = m.rearrange("p (a b n) -> p a b n", a=1, b=1).to_broadcast([P, 4, TT, P])
                        ins = dve.copy_predicated(gla_a, m4, gla_pairs)
                    elif lv == 6:
                        mark(dve.tensor_copy(a_la[0:64, 0:8, 64:P], hg_pairs[0:64, :, 64:P]))
                        ins = dve.tensor_copy(gla_a[0:64, :, :, 64:P], gla_pairs[0:64, :, :, 64:P])
                    else:
                        top = a_top.rearrange("p (b u) n -> p b (u n)", b=4)
                        mark(dve.tensor_copy(top[:, 0:2, :], PS[:, 0:2, 0:2 * P]))
                        ins = dve.tensor_copy(a_top[:, 4:8, :], PS[:, 2:6, 0:P])
                    ins.then_inc(sem("pairs_read"), 1)
                    dve.wait_ge(sem("pairs_read"), lv + 2)

                operand(0)
                select(-1)
                for lv in range(8):
                    if lv < 7:
                        operand(lv + 1)
                    select(lv)
                dve.wait_ge(sem("la_out"), 1)
                mark(head_out(2, PS[:, 6, :]))
                head_out(3, PS[:, 7, :]).then_inc(sem("group_out"), 2)
                head_post(2, 2, None)
                head_post(3, 3, None)

            between = {0: [gates], 3: [gdn_tokens], 4: [gdn_grams],
                       5: [lambda: gdn_invert(0)], 6: [lambda: gdn_invert(1)], 7: [lambda: gdn_invert(2)],
                       8: [lambda: gdn_invert(3)], 9: [lambda: gdn_invert(4)], 10: [gdn_solve],
                       11: [lambda: gdn_chunk(0)], 12: [lambda: gdn_chunk(1)], 13: [lambda: gdn_chunk(2)],
                       14: [lambda: gdn_chunk(3), silu_gates, gdn_post, fox, la_keys, la_all]}
            for n, what in enumerate(MIX_ORDER):
                ahead(n)
                if 1 <= n <= 3:
                    gdn_taps(n - 1, n)
                for piece in between.get(n, ()):
                    piece()
            settle()
            signal(sem("mix_done"), 1)
            turned("mixed", [(None, act_hi, act_lo)])

            def ahead_4(name):
                for j in range(4):
                    ahead(STEP[name] + j)

            def residual(k, n_used):
                for t in range(TT):
                    if t == 0:
                        dve.wait_ge(sem("tile_summed"), k)
                    else:
                        dve.wait_ge(block_used, n_used)
                    tt(x[:, t, :], x[:, t, :], low4[:, t, :], ALU.add).then_inc(sem("x_tile"), 1)

            ahead_4("mix_out")
            residual(1, STEP["mix_out"] + 4)
            norm(2, junk[:, 1, :])
            turned("norm2", [(lambda j: ch("norm2", j), h_hi, h_lo)])

            def older_taps(y, src, col, two_ft, ready):
                for c in range(2):
                    stt(y[:, c, 1:TOK], src[:, c, 0:TOK - 1], channel[:, bass.ds(col(1) + c, 1)], y[:, c, 1:TOK],
                        ALU.mult, ALU.add).then_inc(ready[0], 1)
                dve.wait_ge(ready[0], ready[1])
                for c in range(2):
                    ins = stt(y[:, c, 2:TOK], src[:, c, 0:TOK - 2], channel[:, bass.ds(col(0) + c, 1)], y[:, c, 2:TOK],
                              ALU.mult, ALU.add)
                return ins

            def ffn(f, p_name=None):
                n0 = STEP[f"ffn{f}"]
                conv = PC[f"ffn_conv{f}"]
                bank = lambda b: PS[:, b, :].rearrange("p (c n) -> p c n", c=2)

                def gate(i):
                    dve.wait_ge(sem("gate_last_tap"), i + (PAIRS * f + 1))
                    ins = older_taps(y_gate, bank(4), lambda tap: 2 * i + (conv + tap * 2 * FT), 0,
                                     (sem("gate_tap1"), 2 * i + (2 * PAIRS * f + 2)))
                    ins.then_inc(sem("gate_convolved"), 1)
                    dve.wait_ge(sem("gate_convolved"), i + (PAIRS * f + 1))

                def up(i):
                    dve.wait_ge(sem("up_last_tap"), i + (PAIRS * f + 1))
                    ins = older_taps(y_up, bank(5), lambda tap: 2 * i + (conv + tap * 2 * FT + FT), 0,
                                     (sem("up_tap1"), 2 * i + (2 * PAIRS * f + 2)))
                    ins.then_inc(sem("up_read"), 1)
                    dve.wait_ge(sem("up_read"), i + (PAIRS * f + 1))
                    dve.wait_ge(sem("gate_silu"), i + (PAIRS * f + 1))
                    tt(hidden, s_gate, y_up, ALU.mult).then_inc(sem("hidden_ready"), 1)

                def hid(i):
                    dve.wait_ge(sem("hidden_hi"), i + (PAIRS * f + 1))
                    tt(hid_lo, hidden, hid_hi.bitcast(F), ALU.subtract).then_inc(sem("hidden_split"), 1)

                ahead(n0)
                gate(0)
                ahead(n0 + 1)
                up(0)
                hid(0)
                if p_name:
                    turned(p_name, [(None, p_hi, p_lo)], 6)
                with dve.Fori(1, PAIRS) as i:
                    n = n0 - 1
                    split(n + 2 + 3 * i, (n + 2) % RING)
                    gate(i)
                    split(n + 3 + 3 * i, (n + 3) % RING)
                    up(i)
                    split(n + 4 + 3 * i, (n + 4) % RING)
                    hid(i)
                ahead(n0 + 3 * PAIRS - 1)

            ffn(0)
            residual(2, STEP["ffn0"] + 3 * PAIRS)
            norm(3, junk[:, 1, :])
            turned("pre_mix0", [(lambda j: ch("pre_mix0", j), h_hi, h_lo)])

            n0 = STEP["sc_in"]
            signal(sem("sc_bank_read"), 3)
            with dve.Fori(0, 4) as i:
                split(n0 + 2 + 3 * i, (n0 + 2) % RING)
                split(n0 + 3 + 3 * i, (n0 + 3) % RING)
                dve.wait_ge(sem("sc_gc"), i + 1)
                dve.wait_ge(block_used, n0 + 2 + 3 * i)
                tt(y_up, s_gate, PS[:, 5, :].rearrange("p (c n) -> p c n", c=2), ALU.mult).then_inc(sem("sc_product"), 1)
                dve.wait_ge(sem("sc_product"), i + 1)
                dve.sem_inc(sem("sc_bank_read"), 2)
                dve.wait_ge(sem("sc_last_tap"), i + 1)
                ins = older_taps(y_gate, y_up, lambda tap: 2 * i + (PC["sc_conv"] + tap * 8), 0, (sem("sc_tap1"), 2 * i + 2))
                ins.then_inc(sem("sc_convolved"), 1)
                dve.wait_ge(sem("sc_convolved"), i + 1)
                split(n0 + 4 + 3 * i, (n0 + 4) % RING)
                dve.wait_ge(block_used, n0 + 3 + 3 * i)
                tt(hidden, y_gate, PS[:, 6, :].rearrange("p (c n) -> p c n", c=2), ALU.mult).then_inc(sem("sc_gated"), 1)
                dve.wait_ge(sem("sc_gated"), i + 1)
                dve.sem_inc(sem("sc_bank_read"), 1)
                dve.wait_ge(sem("sc_hi"), i + 1)
                tt(act_lo[:, bass.ds(2 * i, 2), :], hidden, act_hi[:, bass.ds(2 * i, 2), :].bitcast(F), ALU.subtract) \
                    .then_inc(sem("sc_hidden"), 1)
            ahead_4("sc_out")

            posts = [0]

            def post(acc):
                q = posts[0]
                posts[0] += 1
                dve.wait_ge(sem("post_loaded"), 16 * (q + 1))
                for t in range(TT):
                    dve.wait_ge(sem("post_rstd"), 2 * q + t + 1)
                    link(stt(junk[:, t, :], acc[:, t, :], stat[:, 4 + t:5 + t], post_g, ALU.mult, ALU.mult))
                    if t == 1:
                        dve.sem_inc(sem("post_used"), 1)
                    tt(x[:, t, :], x[:, t, :], junk[:, t, :], ALU.add).then_inc(sem("x_tile"), 1)

            post(low4)
            norm(4, gate_s[:, 1, :])
            turned("pre_ffn0", [(lambda j: ch("pre_ffn0", j), h_hi, h_lo)])

            def ffn_and_ple(layer, k):
                ffn(1 + layer, f"p{layer}")
                post(low4)
                norm(k + 1, gate_s[:, 1, :])
                turned(f"pre_ple{layer}", [(lambda j: ch(f"pre_ple{layer}", j), h_hi, h_lo)])
                ahead(STEP[f"ple_proj{layer}"])
                for j in range(4):
                    ahead(STEP[f"ple_gate{layer}"] + j)
                for t in range(TT):
                    dve.wait_ge(sem("ple_gate"), 2 * layer + t + 1)
                    tt(gate_s[:, t, :], gate_s[:, t, :], low4[:, t, :], ALU.mult).then_inc(sem("ple_product"), 1)
                post(gate_s)

            ffn_and_ple(0, 4)
            norm(6, junk[:, 1, :])
            turned("pre_mix1", [(lambda j: ch("pre_mix1", j), h_hi, h_lo), (lambda j: ch("kv", j), act_hi, act_lo)])

            lv4 = rows("lambda", 256).rearrange("p (a b d) -> p a b d", a=2, b=2)
            lj = lg1.rearrange("p a n -> p (a n)")[:, 0:P].rearrange("p (a d) -> p a d", a=2)
            link(tt(lj, lv4[:, :, 0, :], lv4[:, :, 1, :], ALU.mult))
            dve.tensor_reduce(lam[:, 0:2], lj, AX, ALU.add).then_inc(sem("lambda_sums"), 1)
            dve.wait_ge(sem("lambda_exps"), 1)
            link(tt(lam[:, 2:3], lam[:, 1:2], lam[:, 0:1], ALU.subtract))
            link(ts(lam[:, 3:4], lam[:, 2:3], -LAMBDA_INIT, None, ALU.add))

            def head(h):
                a = att_stat
                dve.wait_ge(sem("logits"), h + 1)
                b1 = bias_t[:, h, :].rearrange("p (o n) -> p o n", o=1).to_broadcast([P, 2, TOK])
                b0 = bias_t[:, h, P:TOK].rearrange("p (o n) -> p o n", o=1).to_broadcast([P, 2, P])
                mark(tt(lg1, PS[:, 6:8, 0:TOK], b1, ALU.add))
                mark(tt(lg0, PS[:, 6:8, TOK:TOK + P], b0, ALU.add))
                settle()
                dve.sem_inc(sem("logits_read"), 1)
                dve.tensor_reduce(a[:, 0:2], lg1, AX, ALU.max, negate=True).then_inc(sem("att_max"), 1)
                dve.tensor_reduce(a[:, 2:4], lg0, AX, ALU.max, negate=True).then_inc(sem("att_max"), 1)

            def combine(h):
                a = att_stat
                dve.wait_ge(sem("att_exp"), h + 1)
                if h:
                    dve.wait_ge(sem("att_turned"), h)
                link(dve.reciprocal(a[:, 8:12], a[:, 4:8]))
                mark(tt(a[:, 9:12:2], a[:, 9:12:2], lam[:, 3:4].to_broadcast([P, 2]), ALU.mult))
                mark(ts(lg1[:, 0, :], lg1[:, 0, :], a[:, 8:9], None, ALU.mult))
                mark(ts(lg0[:, 0, :], lg0[:, 0, :], a[:, 10:11], None, ALU.mult))
                settle()
                w1 = at_w[:, 0:2, :].rearrange("p a n -> p (a n)")
                mark(stt(w1, lg1[:, 1, :], a[:, 9:10], lg1[:, 0, :], ALU.mult, ALU.add))
                stt(at_w[:, 2, :], lg0[:, 1, :], a[:, 11:12], lg0[:, 0, :], ALU.mult, ALU.add) \
                    .then_inc(sem("att_weights"), 1)
                dve.wait_ge(sem("att_weights"), h + 1)

            for j in range(8):
                ahead(STEP["att_k"] + j)
                if j == 5:
                    dve.wait_ge(sem("bias_copied"), 1)
                if j >= 5:
                    head(j - 5)
                    combine(j - 5)
            for j in range(4):
                ahead(STEP["att_v"] + j)
                head(j + 3)
                combine(j + 3)
            head(7)
            combine(7)
            for t in range(TT):
                dve.wait_ge(sem("head_squares"), t + 1)
                heads = lambda v: v.rearrange("p (u d) -> p u d", d=P)
                s = stat[:, 8 + 8 * t:16 + 8 * t]
                dve.tensor_reduce(s, heads(xn[:, t, :]), AX, ALU.add).then_inc(sem("subln_sums"), 1)
                dve.wait_ge(sem("subln_rstd"), t + 1)
                link(ts(s, s, 1.0 - LAMBDA_INIT, None, ALU.mult))
                tt(heads(xn[:, t, :]), heads(low4[:, t, :]), unit(s, P), ALU.mult).then_inc(sem("heads_normed"), 1)
            turned("att", [(lambda j: ch("subln"), act_hi, act_lo)])
            ahead_4("att_out")
            post(low4)
            norm(7, gate_s[:, 1, :])
            turned("pre_ffn1", [(lambda j: ch("pre_ffn1", j), h_hi, h_lo)])
            ffn_and_ple(1, 7)


def column_block(w, c0, n=256):
    b = np.zeros((P, KC, 256), np.float32)
    b[:, :, 0:n] = w[:, c0:c0 + n].reshape(KC, P, n).transpose(1, 0, 2)
    return b.reshape(P, BLK)


def row_block_of(w, j):
    return w[256 * j:256 * (j + 1)].reshape(2, P, D).transpose(1, 0, 2).reshape(P, BLK)


def weight_stream(a):
    blocks = []
    w = a["w_in"][0]
    small = np.concatenate([w[:, W_IN[n]:W_IN[n] + m] for n, m in
                            (("fox_f", 4), ("gdn_a", 4), ("gdn_b", 4), ("gla_gk", 16))], axis=1)
    for what in MIX_ORDER:
        blocks.append(column_block(small, 0, SMALL) if what == "small" else column_block(w, W_IN[what]))

    def rows_of(w, n=4):
        blocks.extend(row_block_of(w, j) for j in range(n))

    def ffn(up, down):
        for i in range(PAIRS):
            blocks.append(column_block(up, 256 * i))
            blocks.append(column_block(up, D_FF + 256 * i))
            if i:
                blocks.append(row_block_of(down, i - 1))
        blocks.append(row_block_of(down, PAIRS - 1))

    rows_of(a["w_out"][0])
    ffn(a["w_up"][0], a["w_down"][0])
    w = a["w_sc_in_2"][0]
    for i in range(4):
        for part in (1, 2, 0):
            blocks.append(column_block(w, part * D + 256 * i))
    rows_of(a["w_sc_out_2"][0])
    for layer in range(2):
        if layer == 1:
            for i in range(4):
                blocks.append(column_block(a["w_kv_2"], 256 * i))
            for i in range(4):
                blocks.append(column_block(a["w_q_2"][0], 256 * i))
            rows_of(a["w_kv_2"][:, D:])
            rows_of(a["w_o_2"][0])
        ffn(a["w_ffn_up_2"][layer], a["w_ffn_down_2"][layer])
        rows_of(a["w_ple_proj_2"][layer], 1)
        rows_of(a["w_ple_gate_2"][layer])
    assert len(blocks) == N_BLOCKS
    return np.stack(blocks)


def channel_columns(a):
    def cols(v):
        return v.reshape(-1, P).T

    parts = [cols(a["norm1_g"][0]), cols(a["norm2_g"][0]), cols(a["g_pre_mix_2"][0]), cols(a["g_pre_ffn_2"][0]),
             cols(a["g_pre_ple_2"][0]), cols(a["g_pre_mix_2"][1]), cols(a["g_kv_2"]), cols(a["g_pre_ffn_2"][1]),
             cols(a["g_pre_ple_2"][1]), cols(a["g_subln_2"][0]), cols(a["w_sc_conv_2"][0]), cols(a["gdn_conv_w"][0]),
             cols(a["ffn_conv_w"][0]), cols(a["ffn_conv_b"][0]), cols(a["w_ffn_conv_2"][0]), cols(a["w_ffn_conv_2"][1])]
    return np.ascontiguousarray(np.concatenate(parts, axis=1))


def mask_table():
    i = np.arange(P)
    r, c = i[:, None], i[None, :]
    same = r // CHUNK == c // CHUNK
    one = {"tri": r <= c, "ones": r >= 0 * c, "after": r > c, "blk_tri": same & (r <= c), "blk_after": same & (r > c),
           "ind0": (r < CHUNK) & (c >= 0), "ind1": (r >= CHUNK) & (c >= 0),
           "m1": (r // 2 == c // 2) & (c < r)}
    for lv in range(6):
        b = 1 << lv
        one[f"t{b}"] = (r // (2 * b) == c // (2 * b)) & (r % (2 * b) < b) & (c % (2 * b) >= b)
    for lv in range(7):
        b = 1 << lv
        mid = c // (2 * b) * (2 * b) + b - 1
        right = c % (2 * b) >= b
        one[f"e{b}"] = np.where(right, (r > mid) & (r <= c), (r > c) & (r <= mid))
    add = {"fox_add": c <= r, "gdn_add": same & (c <= r)}
    rows = [np.where(add[n], 0.0, NEG) if n in add else one[n] + np.zeros((P, P)) for n in MASKS]
    return np.stack(rows, axis=1).astype(np.float32)


def distance_one_hot():
    dist = 255 - np.arange(N_DIST)
    n, exact, far = 32, 16, 128
    safe = np.maximum(dist, 1).astype(np.float32)
    large = exact + (np.log(safe / np.float32(exact)) / np.float32(math.log(far / exact)) * (n - exact)).astype(np.int32)
    bucket = np.where(dist < 0, n, np.where(dist < exact, dist, np.minimum(large, n - 1)))
    return (np.arange(BIAS_ROWS)[:, None] == bucket[None, :]).astype(np.float32)


def kernel(**inputs):
    import concourse.bacc as bacc
    from concourse.bass_utils import run_bass_kernel_spmd

    a = {k: np.asarray(v) for k, v in inputs.items()}
    row = np.concatenate([a["fox_b_f"][0], a["gdn_dt_bias"][0], a["gdn_a_log"][0], a["fox_qn_g"][0], a["fox_kn_g"][0],
                          a["fox_on_g"][0], a["gdn_on_g"][0], a["hg_on_g"][0], a["gla_on_g"][0], a["gla_b_gk"][0],
                          a["diff_lambda_2"][0].reshape(-1)])
    post = np.stack([a["g_post_mix_2"][0], a["g_post_ffn_2"][0], a["g_post_ple_2"][0],
                     a["g_post_mix_2"][1], a["g_post_ffn_2"][1], a["g_post_ple_2"][1]])
    arrays = {
        "weights": weight_stream(a), "x_in": a["x"][0], "masks_in": mask_table(), "ident_in": np.eye(P, dtype=np.float32),
        "channel_in": channel_columns(a), "row_in": row, "w_gk_in": a["gla_w_gk"][0], "post_in": post,
        "p_in": a["p_2"][:, 0], "table_in": a["rel_bias_2"], "onehot_in": distance_one_hot(),
        "flip_in": np.eye(P, dtype=np.float32)[::-1],
    }
    arrays = {k: np.ascontiguousarray(v) for k, v in arrays.items()}
    nc = bacc.Bacc("TRN2", target_bir_lowering=False, num_devices=1)
    args = [nc.dram_tensor(k, v.shape, mybir.dt.from_np(v.dtype), kind="ExternalInput").ap() for k, v in arrays.items()]
    result = nc.dram_tensor("result", (TOK, D), F, kind="ExternalOutput").ap()
    build(nc, *args, result)
    r = run_bass_kernel_spmd(nc, [arrays], core_ids=[0])
    return r.results[0]["result"].reshape(1, TOK, D)
```

```python
import math
from contextlib import ExitStack

import numpy as np

import concourse.bass as bass
from concourse import mybir

F = mybir.dt.float32
R = mybir.dt.float32r
I32 = mybir.dt.int32
ALU = mybir.AluOpType
ACT = mybir.ActivationFunctionType
AX = mybir.AxisListType.X

P = 128
TOK = 256
TT = TOK // P
D = 1024
KC = D // P
BLK = 2048
RING = 3
EPS = 1e-6
ARENA = 24448
NEG = -1e30
D_FF = 2816
FT = D_FF // P
PAIRS = FT // 2
HEADS = 4
DH = 64
CHUNK = 64
GROUP = 256
TABLES = "natural_log_exp_and_others"

STEP = {}
N_BLOCKS = 0
for _name, _n in (("mix_in", 15), ("mix_out", 4), ("ffn0", 3 * PAIRS), ("sc_in", 12), ("sc_out", 4),
                  ("ffn1", 3 * PAIRS), ("ple_proj0", 1), ("ple_gate0", 4), ("att_k", 4), ("att_q", 4),
                  ("att_v", 4), ("att_out", 4), ("ffn2", 3 * PAIRS), ("ple_proj1", 1), ("ple_gate1", 4)):
    STEP[_name] = N_BLOCKS
    N_BLOCKS += _n

W_IN = {"fox_q": 0, "fox_k": 256, "fox_v": 512, "fox_f": 768, "gdn_q": 772, "gdn_k": 1028, "gdn_v": 1284,
        "gdn_b": 1540, "gdn_a": 1544, "gdn_z": 1548, "hg_q": 1804, "hg_f": 2060, "hg_i": 2316,
        "hg_g": 2572, "gla_qk": 2828, "gla_v": 3084, "gla_gk": 3340, "gla_g": 3356}
MIX_ORDER = ("small", "gdn_q", "gdn_k", "gdn_v", "hg_f", "fox_q", "fox_k", "hg_q", "fox_v", "gla_qk",
             "gla_v", "hg_i", "gdn_z", "hg_g", "gla_g")
CHANNEL_MAJOR = ("gdn_q", "gdn_k", "gdn_v", "hg_q", "gla_qk")
TOKM = {n: i for i, n in enumerate(("fox_q", "fox_k", "fox_v", "hg_f", "hg_i", "gla_v", "gdn_z", "hg_g", "gla_g"))}
SMALL = 28

MASKS = ("e1", "e2", "e4", "e8", "e16", "e32", "e64", "after", "tri", "ones", "tri_again",
         "fox_add", "gdn_add", "eye", "blk_tri", "blk_after", "ind0", "ind1", "m1", "t1", "t2", "t4", "t8", "t16", "t32",
         "packed0", "packed1", "packed2", "packed3")
MASK = {n: i for i, n in enumerate(MASKS)}
N_LEVEL_MASKS = MASK["blk_tri"] + 1

PC, N_PC = {}, 0
for _name, _n in (("norm1", 8), ("norm2", 8), ("pre_mix0", 8), ("pre_ffn0", 8), ("pre_ple0", 8),
                  ("pre_mix1", 8), ("kv", 8), ("pre_ffn1", 8), ("pre_ple1", 8), ("subln", 1),
                  ("sc_conv", 24), ("gdn_conv", 24), ("ffn_conv0", 3 * 2 * FT), ("ffn_bias", 2 * FT),
                  ("ffn_conv1", 3 * 2 * FT), ("ffn_conv2", 3 * 2 * FT)):
    PC[_name] = N_PC
    N_PC += _n

ROW, N_ROW = {}, 0
for _name, _n in (("fox_b_f", 4), ("gdn_dt", 4), ("gdn_a_log", 4), ("fox_qn", 64), ("fox_kn", 64), ("fox_on", 64),
                  ("gdn_on", 64), ("hg_on", 64), ("gla_on", 64), ("b_gk", 128), ("lambda", 256)):
    ROW[_name] = N_ROW
    N_ROW += _n

TURN = {}
_chunks = 0
for _name, _n in (("norm1", 8), ("mixed", 8), ("norm2", 8), ("pre_mix0", 8), ("pre_ffn0", 8), ("p0", 2), ("pre_ple0", 8),
                  ("pre_mix1", 8), ("att", 8), ("pre_ffn1", 8), ("p1", 2), ("pre_ple1", 8)):
    TURN[_name] = (_chunks, _chunks // 2, _n)
    _chunks += _n

N_HEADS = 8
LAMBDA_INIT = 0.8 - 0.6 * math.exp(-0.3)
N_DIST = 384
BIAS_ROWS = 33


def build(nc, weights, x_in, masks_in, ident_in, channel_in, row_in, w_gk_in, post_in, p_in, table_in,
          onehot_in, flip_in, out):
    bias_dram = nc.dram_tensor("bias_by_distance", (N_HEADS, N_DIST), F, kind="Internal").ap()
    with ExitStack() as ctx:
        sems = {}

        def sem(name):
            if name not in sems:
                sems[name] = ctx.enter_context(nc.semaphore(name))
            return sems[name]

        def sb(name, shape, dt=F):
            return ctx.enter_context(nc.sbuf_tensor(name, shape, dt))

        raw = sb("raw", [P, RING, BLK])
        w_hi = sb("w_hi", [P, RING, BLK], R)
        w_lo = sb("w_lo", [P, RING, BLK], R)
        x = sb("x", [P, TT, D])
        xn = sb("xn", [P, TT, D])
        h_hi = sb("h_hi", [P, KC, TOK], R)
        h_lo = sb("h_lo", [P, KC, TOK], R)
        channel = sb("channel", [P, N_PC])
        row = sb("row", [P, N_ROW])
        ident = sb("ident", [P, P])
        stat = sb("stat", [P, 64])
        eps = sb("eps", [P, 1])
        nlf_hi = sb("nlf_hi", [P, TT, HEADS], R)
        nlf_lo = sb("nlf_lo", [P, TT, HEADS], R)
        gd_hi = sb("gd_hi", [P, TT, HEADS], R)
        gd_lo = sb("gd_lo", [P, TT, HEADS], R)
        zeros_r = sb("zeros_r", [P, 512], R)
        arena_offset = -(-nc.sbuf_base // 32) * 32
        arena_store = sb("arena", [P, ARENA])

        arena = {"at": 0, "n": 0}

        def place(shape):
            n = int(np.prod(shape[1:]))
            at = arena["at"]
            arena["at"] += n
            assert arena["at"] <= ARENA, arena
            v = arena_store[0:shape[0], at:at + n]
            if len(shape) == 3:
                v = v.rearrange("p (a b) -> p a b", a=shape[1])
            elif len(shape) == 4:
                v = v.rearrange("p (a b c) -> p a b c", a=shape[1], b=shape[2])
            return v

        def rounded(name, shape, at):
            return nc.alloc_sbuf_tensor_at(name, shape, R, offset=arena_offset + 4 * at)

        masks = place([P, len(MASKS), P])
        level_masks = rounded("level_masks", [P, N_LEVEL_MASKS, P], 0)
        tokm_at = arena["at"]
        tokm = place([P, TT, len(TOKM), GROUP])
        la_lo = rounded("la_lo", [P, TT, 3, P], arena["at"])
        la = place([P, TT, 3, P])
        small = place([P, TT, SMALL])
        chm = place([P, 12, TOK])
        gate_z = place([P, TT, 8])
        gate_l = place([P, TT, 8])
        lf = place([P, TT, HEADS])
        nlf = place([P, TT, HEADS])
        gd = place([P, TT, HEADS])
        ngd = place([P, TT, HEADS])
        beta = place([P, TT, HEADS])
        ea = place([P, HEADS])
        e_g = place([P, TT, HEADS])
        e_rest = place([P, TT, HEADS])
        e_last = place([P, TT, 2, HEADS])
        be_g = place([P, TT, HEADS])
        sq = place([P, 1024])
        mix_at = arena["at"]
        small_t = place([SMALL, TOK])
        gk_t = small_t[0:16, :]
        w_gk = place([16, P])
        arena["at"] = mix_at
        qn = place([P, 8, DH])
        kn = place([P, 8, DH])
        kbg = place([P, 8, DH])
        vb = place([P, 8, DH])
        ko = place([P, 8, DH])
        qi = place([P, 8, DH])
        w_t = place([P, 2, TOK])
        u_gd = place([P, 8, DH])
        v_new = place([P, 8, DH])
        state = place([P, 2, DH])
        dec_t = place([P, 8, P])
        a_qk = place([P, 8, P])
        dec_at = arena["at"]
        dec = place([P, 8, P])
        m_gd = place([P, 8, P])
        mt_gd = place([P, 8, P])
        c_t = place([P, 8, P])
        inv, inv_t, y_gd = dec, dec_t, m_gd
        arena["at"] = dec_at
        fq_t = place([P, 2, TOK])
        fk_t = place([P, 2, TOK])
        probs0 = place([P, HEADS, P])
        probs1 = place([P, HEADS, TOK])
        probs_t = place([P, HEADS, 3, P])
        arena["at"] = mix_at
        z_lv = place([P, 2, 768])
        w_lv = place([P, 4, 768])
        a_packed = place([P, 16, CHUNK])
        a_top = place([P, 8, P])
        assert arena["at"] <= dec_at
        arena["at"] = dec_at
        a_la = place([P, 16, P])
        la_hi = rounded("la_hi", [P, TT, len(TOKM) * GROUP], tokm_at)[:, :, 0:3 * P]

        PS = ctx.enter_context(nc.psum_tensor("PS", [P, 8, 512], F))
        low4 = PS[:, 0:4, :].rearrange("p b n -> p (b n)").rearrange("p (t n) -> p t n", t=TT)
        high4 = PS[:, 4:8, :].rearrange("p b n -> p (b n)").rearrange("p (t n) -> p t n", t=TT)

        operand_offset = arena_offset + 4 * (ARENA - 2 * KC * TOK)
        act_hi = nc.alloc_sbuf_tensor_at("act_hi", [P, KC, TOK], R, offset=operand_offset)
        act_lo = nc.alloc_sbuf_tensor_at("act_lo", [P, KC, TOK], R, offset=operand_offset + 4 * KC * TOK)
        arena["at"] = 0
        hid_hi = act_hi[:, 0:2, :]
        hid_lo = act_lo[:, 0:2, :]
        p_hi = act_hi[:, 2:4, :]
        p_lo = act_lo[:, 2:4, :]
        y_gate = place([P, 2, TOK])
        y_up = place([P, 2, TOK])
        s_gate = place([P, 2, TOK])
        hidden = place([P, 2, TOK])
        wt_at = arena["at"]
        junk = place([P, TT, D])
        gate_s = place([P, TT, D])
        post_g = place([P, D])
        p_tok = place([P, TT, TOK])
        q_t = place([P, N_HEADS, TOK])
        k_t = place([P, N_HEADS, TOK])
        v_tok = place([P, TT, D])
        bias_t = place([P, N_HEADS, TOK])
        bias_rev = q_t
        flip = place([P, P])
        lg1 = [place([P, 2, TOK]) for _ in range(2)]
        lg0 = [place([P, 2, P]) for _ in range(2)]
        at_w = [place([P, 3, P]) for _ in range(2)]
        at_wt = arena_store[:, wt_at:wt_at + N_HEADS * 3 * P].rearrange("p (h j n) -> p h j n", h=N_HEADS, j=3)
        table = place([BIAS_ROWS, N_HEADS])
        onehot = place([BIAS_ROWS, N_DIST])
        bias_row = place([N_HEADS, N_DIST])
        lam = place([P, 8])
        att_stat = [place([P, 16]) for _ in range(2)]
        assert arena["at"] <= ARENA - 2 * KC * TOK

        def mask(name):
            if MASK[name] < N_LEVEL_MASKS:
                return level_masks[:, MASK[name], :].bitcast(F)
            return masks[:, MASK[name], :]

        def packed(lv):
            at = (MASK["packed0"] * P) + (lv + 1) * CHUNK
            return masks.rearrange("p m n -> p (m n)")[:, at:at + CHUNK]

        def ch(name, j=0):
            return channel[:, PC[name] + j:PC[name] + j + 1]

        def rows(name, n):
            return row[:, ROW[name]:ROW[name] + n]

        def unit(v, n):
            return v.rearrange("p (u o) -> p u o", o=1).to_broadcast([P, v.shape[1], n])

        def units(v, n):
            return v.rearrange("p (o m) -> p o m", o=1).to_broadcast([P, n, v.shape[1]])

        def group_view(grp):
            return xn[:, :, grp * GROUP:(grp + 1) * GROUP]

        def u_of(t, h):
            return (h % 2) * 4 + t * 2 + h // 2

        def la_unit(t, h):
            return u_of(t, h) if h < 4 else 8 + (h - 4) * 2 + t

        def pair_bank(t, h):
            bank, at = (h % 2, (t * 2 + h // 2) * P) if h < 4 else (h - 2, t * P)
            return PS[:, bank, at:at + P]

        def chunk_pair_bank(t, h, c):
            bank, at = (h % 2, (t * 2 + h // 2) * CHUNK) if h < 4 else (h - 2, t * CHUNK)
            return PS[c * CHUNK:(c + 1) * CHUNK, bank, at:at + CHUNK]

        def la_top_unit(h):
            return (h % 2) * 2 + h // 2 if h < 4 else h

        def projected(engine, what):
            n = MIX_ORDER.index(what)
            engine.wait_ge(sem(f"proj_bank_read{n % 2}"), n // 2 + 1)

        ALL_UNITS = [(t, h) for t in range(TT) for h in range(HEADS)]

        def th(v):
            return v.rearrange("p t h -> p (t h)")

        raw_loaded = [sem(f"raw_loaded{s}") for s in range(RING)]
        hi_ready, lo_ready, block_used = sem("hi_ready"), sem("lo_ready"), sem("block_used")
        chunks_turned, part_hi, part_ready = sem("chunks_turned"), sem("part_hi"), sem("part_ready")
        inputs = sem("inputs_loaded")
        N_INPUTS = 2 * 16

        block = ctx.enter_context(nc.Block())

        @block.sync
        def _(sp):
            sp.dma_start(x[:, :, :], x_in.rearrange("(t p) n -> p t n", p=P)).then_inc(sem("x_loaded"), 16)
            sp.dma_start(ident[:, :], ident_in).then_inc(inputs, 16)
            sp.dma_start(raw[:, 0, :], weights[0]).then_inc(raw_loaded[0], 16)
            sp.dma_start(channel[:, :], channel_in).then_inc(inputs, 16)
            for s in range(1, RING):
                sp.dma_start(raw[:, s, :], weights[s]).then_inc(raw_loaded[s], 16)
            sp.dma_start(row[:, :], row_in.partition_broadcast(P)).then_inc(sem("mix_inputs"), 16)
            sp.dma_start(w_gk, w_gk_in).then_inc(sem("mix_inputs"), 16)
            sp.dma_start(masks, masks_in).then_inc(sem("mix_inputs"), 16)
            whole = (N_BLOCKS - RING) // RING
            with sp.Fori(1, 1 + whole) as i:
                for s in range(RING):
                    sp.wait_ge(lo_ready, RING * i + (s - RING + 1))
                    sp.dma_start(raw[:, s, :], weights[bass.ds(RING * i + s, 1)].rearrange("a p n -> (a p) n")) \
                        .then_inc(raw_loaded[s], 16)
            for n in range(RING + whole * RING, N_BLOCKS):
                sp.wait_ge(lo_ready, n - RING + 1)
                sp.dma_start(raw[:, n % RING, :], weights[n]).then_inc(raw_loaded[n % RING], 16)
            for t in range(TT):
                sp.wait_ge(sem("x_tile"), 15 + t)
                sp.dma_start(out[t * P:(t + 1) * P, :], x[:, t, :]).then_inc(sem("stored"), 16)
            sp.wait_ge(sem("stored"), 16 * TT)

        @block.gpsimd
        def _(pool):
            pool.memset(zeros_r[:, :].bitcast(F), 0.0).then_inc(sem("zeros"), 1)
            pool.memset(eps[:, :], EPS).then_inc(sem("eps_set"), 1)
            pool.wait_ge(sem("mix_done"), 1)
            pool.dma_start(flip, flip_in).then_inc(sem("bias_loaded"), 16)
            pool.memset(table, NEG).then_inc(sem("table_row"), 1)
            pool.wait_ge(sem("table_row"), 1)
            pool.dma_start(table[0:BIAS_ROWS - 1, :], table_in).then_inc(sem("table_loaded"), 16)
            pool.dma_start(onehot, onehot_in).then_inc(sem("table_loaded"), 16)
            pool.wait_ge(sem("bias_rows"), 1)
            pool.dma_start(bias_dram, bias_row).then_inc(sem("bias_stored"), 16)
            pool.wait_ge(sem("bias_stored"), 16)
            toeplitz = bass.AP(tensor=bias_dram.tensor, offset=0, ap=[[1, P], [N_DIST, N_HEADS], [1, TOK]])
            pool.dma_start(bias_rev, toeplitz).then_inc(sem("bias_loaded"), 16)
            for n in range(6):
                if n:
                    pool.wait_ge(sem("post_used"), n)
                pool.dma_start(post_g, post_in[n].partition_broadcast(P)).then_inc(sem("post_loaded"), 16)
                if n in (0, 3):
                    if n == 3:
                        pool.wait_ge(chunks_turned, TURN["p0"][1] + 1)
                    pool.dma_start(p_tok, p_in[n // 3].rearrange("(t p) n -> p t n", p=P)).then_inc(sem("p_loaded"), 16)

        @block.tensor
        def _(pe):
            def mm(o, lhs, rhs, start=True, stop=True):
                return pe.matmul(o, lhs, rhs, start=start, stop=stop)

            def block_ready(n):
                pe.wait_ge(hi_ready, n + 1)
                pe.wait_ge(lo_ready, n + 1)

            def chunks_ready(name, k):
                pe.wait_ge(part_ready, TURN[name][1] + k // 2 + 1)

            def columns(n0, slot, bank, operand, channel_major=True, fresh=None, middle=()):
                block_ready(n0)
                a_hi, a_lo = operand
                for f in range(2):
                    if f == 1:
                        for piece in middle:
                            piece()
                    for k in range(KC):
                        if fresh and f == 0 and k % 2 == 0:
                            chunks_ready(fresh, k)
                        if channel_major:
                            at = k * 256 + f * P
                            ws_hi, ws_lo = w_hi[:, slot, at:at + P], w_lo[:, slot, at:at + P]
                            o = PS[:, bank, f * TOK:(f + 1) * TOK]
                            mm(o, ws_hi, a_hi[:, k, :], k == 0, False)
                            mm(o, ws_hi, a_lo[:, k, :], False, False)
                            last = mm(o, ws_lo, a_hi[:, k, :], False, k == KC - 1)
                        else:
                            tok = slice(f * P, (f + 1) * P)
                            at = slice(k * 256, (k + 1) * 256)
                            ws_hi, ws_lo = w_hi[:, slot, at], w_lo[:, slot, at]
                            o = PS[:, bank, f * 256:(f + 1) * 256]
                            mm(o, a_hi[:, k, tok], ws_hi, k == 0, False)
                            mm(o, a_hi[:, k, tok], ws_lo, False, False)
                            last = mm(o, a_lo[:, k, tok], ws_hi, False, k == KC - 1)
                last.then_inc(block_used, 1)

            def row_block(n0, slot, acc, operand, k0, first, final, tiles=False, middle=()):
                block_ready(n0)
                a_hi, a_lo = operand
                parts = ((a_hi, w_hi), (a_hi, w_lo), (a_lo, w_hi))
                order = [(kk, t) for t in range(TT) for kk in range(2)] if final else \
                    [(kk, t) for kk in range(2) for t in range(TT)]
                for step, (kk, t) in enumerate(order):
                    if step == 2:
                        for piece in middle:
                            piece()
                    tok = slice(t * P, (t + 1) * P)
                    for j, (a, w) in enumerate(parts):
                        for half in range(2):
                            at = kk * D + half * 512
                            last = pe.matmul(acc[:, t, half * 512:(half + 1) * 512], a[:, k0 + kk, tok],
                                             w[:, slot, at:at + 512], start=first and kk == 0 and j == 0,
                                             stop=final and kk == 1 and j == 2, skip_group_check=True)
                    if tiles and (kk, t) == (1, 0):
                        last.then_inc(sem("tile_summed"), 1)
                last.then_inc(block_used, 1)

            def turn(name, src, bank=4, tile_ready=None, banks=None):
                for t in range(TT):
                    if callable(tile_ready):
                        pe.wait_ge(*tile_ready(t))
                    elif tile_ready:
                        pe.wait_ge(sem(f"tokens{t}_ready"), tile_ready)
                    for j in range(TURN[name][2]) if banks is None else [2 * b + j for b in banks for j in range(2)]:
                        at = (j % 2) * TOK + t * P
                        last = pe.transpose(PS[:, bank + j // 2, at:at + P], src[:, t, j * P:(j + 1) * P], ident[:, :])
                        if t == TT - 1 and j % 2:
                            last.then_inc(chunks_turned, 1)

            pe.wait_ge(inputs, N_INPUTS)
            turn("norm1", xn, tile_ready=1)

            def gates():
                pe.wait_ge(sem("gates_ready"), 1)
                pe.wait_ge(sem("masks_rounded"), 1)
                o = PS[:, 0, :]
                for t in range(TT):
                    mm(o[:, t * 4:t * 4 + 4], mask("blk_tri"), gd[:, t, :])
                    mm(o[:, 8 + t * 4:12 + t * 4], mask("blk_after"), gd[:, t, :])
                    for c in range(2):
                        at = 16 + (t * 2 + c) * 4
                        last = mm(o[:, at:at + 4], mask(f"ind{c}"), gd[:, t, :])
                last.then_inc(sem("gate_sums"), 1)

            def small_columns():
                block_ready(0)
                o = PS[0:SMALL, 4, 0:TOK]
                for k in range(KC):
                    if k % 2 == 0:
                        chunks_ready("norm1", k)
                    at = slice(k * 256, k * 256 + SMALL)
                    mm(o, w_hi[:, 0, at], h_hi[:, k, :], k == 0, False)
                    mm(o, w_hi[:, 0, at], h_lo[:, k, :], False, False)
                    last = mm(o, w_lo[:, 0, at], h_hi[:, k, :], False, k == KC - 1)
                last.then_inc(block_used, 1)

            def turn_small():
                pe.wait_ge(sem("proj_bank_read0"), 1)
                for t in range(TT):
                    last = pe.transpose(PS[:, 1, t * SMALL:(t + 1) * SMALL], small_t[:, t * P:(t + 1) * P],
                                        ident[0:SMALL, 0:SMALL])
                last.then_inc(sem("small_turned"), 1)

            def gk_product():
                for t in range(TT):
                    last = mm(PS[:, 1, 256 + t * P:256 + (t + 1) * P], gk_t[:, t * P:(t + 1) * P], w_gk)
                last.then_inc(sem("gk_projected"), 1)

            def exact(name):
                return level_masks[:, MASK[name], :]

            def add(o, lhs, rhs, start=False):
                return pe.matmul(o, lhs, rhs, start=start, stop=False, skip_group_check=True)

            def gdn_tokens():
                pe.wait_ge(sem("gk_read"), 1)
                for s in range(3):
                    pe.wait_ge(sem("gdn_convolved"), s + 1)
                    for t in range(TT):
                        for f in range(2):
                            last = pe.transpose(PS[:, s, t * TOK + f * P:t * TOK + (f + 1) * P],
                                                chm[:, 2 * s + f, t * P:(t + 1) * P], ident[:, :])
                last.then_inc(sem("gdn_token_major"), 1)

            def gdn_channels():
                pe.wait_ge(sem("gdn_normed"), 1)
                for s, v in enumerate((qn, kn, qi)):
                    w = v.rearrange("p (t c) d -> p t (c d)", t=TT)
                    for pair in range(2):
                        for t in range(TT):
                            last = pe.transpose(PS[:, s, pair * TOK + t * P:pair * TOK + (t + 1) * P],
                                                w[:, t, pair * P:(pair + 1) * P], ident[:, :])
                last.then_inc(sem("gdn_channel_major"), 1)

            def unit_of(v, t, h):
                return v[64 * (h % 2):64 * (h % 2) + 64, h // 2, t * P:(t + 1) * P]

            qn_t, kn_t, qi_t = chm[:, 0:2, :], chm[:, 2:4, :], chm[:, 4:6, :]
            bank2 = lambda b: PS[:, b:b + 2, :].rearrange("p b n -> p (b n)").rearrange("p (u n) -> p u n", n=P)

            def gdn_grams():
                pe.wait_ge(sem("gdn_copied"), 1)
                for hh in range(2):
                    o = PS[:, 2 + hh, :]
                    add(o.rearrange("p (u n) -> p u n", n=P), exact("eye"), units(exact("gdn_add"), 4), start=True)
                    for part in (gd_hi, gd_lo):
                        g = part[:, :, hh:hh + 3:2].rearrange("p t (h o) -> p t h o", o=1).to_broadcast([P, TT, 2, P])
                        add(o.rearrange("p (t h n) -> p t h n", t=TT, n=P), exact("blk_tri"), g)
                for t, h in ALL_UNITS:
                    u = u_of(t, h)
                    mm(bank2(0)[:, u, :], unit_of(kn_t, t, h), unit_of(kn_t, t, h))
                    last = add(bank2(2)[:, u, :], ngd[:, t, h:h + 1].to_broadcast([P, P]), mask("blk_tri"))
                last.then_inc(sem("decay_logs"), 1)
                for t, h in ALL_UNITS:
                    last = mm(bank2(6)[:, u_of(t, h), :], unit_of(kn_t, t, h), unit_of(qn_t, t, h))
                last.then_inc(sem("qk_gram"), 1)

            def gdn_turn_decay():
                pe.wait_ge(sem("decay"), 1)
                for u in range(8):
                    last = pe.transpose(bank2(2)[:, u, :], dec[:, u, :], ident[:, :])
                last.then_inc(sem("decay_turned"), 1)

            def gdn_turn_m():
                pe.wait_ge(sem("m_ready"), 1)
                for u in range(8):
                    last = pe.transpose(bank2(0)[:, u, :], m_gd[:, u, :], ident[:, :])
                last.then_inc(sem("m_turned"), 1)

            def gdn_cx(lv):
                pe.wait_ge(sem("inv_ready"), lv + 1)
                pe.wait_ge(sem("ct_ready"), lv + 1)
                for u in range(8):
                    last = mm(bank2(2)[:, u, :], c_t[:, u, :], inv[:, u, :])
                last.then_inc(sem("cx"), 1)

            def gdn_xcx(lv):
                pe.wait_ge(sem("cx_copied"), lv + 1)
                pe.wait_ge(sem("inv_t_ready"), lv + 1)
                if lv == 0:
                    pe.wait_ge(sem("la_keys"), 1)
                for u in range(8):
                    if lv < 4:
                        mm(bank2(6)[:, u, :], inv_t[:, u, :], y_gd[:, u, :])
                    last = mm(bank2(0)[:, u, :], y_gd[:, u, :], inv_t[:, u, :])
                last.then_inc(sem("xcx"), 1)

            def gdn_solve():
                pe.wait_ge(sem("inv_t_ready"), 6)
                for t, h in ALL_UNITS:
                    m, u = u_of(t, h), t * HEADS + h
                    mm(PS[:, 2, u * DH:(u + 1) * DH], inv_t[:, m, :], vb[:, u, :])
                    a = 64 * (h % 2)
                    at = (h // 2) * TOK + t * P
                    last = mm(PS[a:a + 64, 3, at:at + P], kbg[:, u, :], inv_t[:, m, :])
                last.then_inc(sem("solved"), 1)

            def gdn_state_in(c):
                t, half = divmod(c, 2)
                r = slice(64 * half, 64 * half + 64)
                tok = slice(c * CHUNK, (c + 1) * CHUNK)
                pe.wait_ge(sem("state_ready"), c + 1)
                if c == 0:
                    pe.wait_ge(sem("solution"), 1)
                for h in range(HEADS):
                    a = slice(64 * (h % 2), 64 * (h % 2) + 64)
                    bank, at = 3 * (h % 2), (h // 2) * DH
                    mm(PS[r, bank, at:at + DH], w_t[a, h // 2, tok], state[a, h // 2, :])
                    at += P * (1 + t)
                    last = mm(PS[r, bank, at:at + DH], qi_t[a, h // 2, tok], state[a, h // 2, :])
                last.then_inc(sem("w_state"), 1)

            def gdn_state_out(c):
                t, half = divmod(c, 2)
                r = slice(64 * half, 64 * half + 64)
                pe.wait_ge(sem("v_new"), c + 1)
                for h in range(HEADS):
                    a = slice(64 * (h % 2), 64 * (h % 2) + 64)
                    u = t * HEADS + h
                    mm(PS[r, 1, u * DH:(u + 1) * DH], a_qk[r, u_of(t, h), 64 * half:64 * half + 64], v_new[r, u, :])
                    last = mm(PS[a, 2, (h // 2) * DH:(h // 2 + 1) * DH], ko[r, u, :], v_new[r, u, :])
                last.then_inc(sem("chunk_done"), 1)

            def fox_turn():
                pe.wait_ge(sem("fox_normed"), 1)
                for s in range(2):
                    for pair in range(2):
                        for t in range(TT):
                            last = pe.transpose(PS[:, 6 + s, pair * TOK + t * P:pair * TOK + (t + 1) * P],
                                                tokm[:, t, s, pair * P:(pair + 1) * P], ident[:, :])
                last.then_inc(sem("fox_turned"), 1)

            def fox_logits(r):
                if r == 0:
                    pe.wait_ge(sem("fox_copied"), 1)
                else:
                    pe.wait_ge(sem("fox_out_read"), r)
                tri3 = level_masks[:, MASK["tri"]:MASK["tri"] + 3, :].rearrange("p a n -> p (a n)")
                for hh in range(2):
                    h = 2 * r + hh
                    a = slice(64 * hh, 64 * hh + 64)
                    q, k = fq_t[a, r, :], fk_t[a, r, :]
                    o = PS[:, 6 + hh, 0:3 * P]
                    add(o, zeros_r[:, 0:P], zeros_r[:, 0:3 * P], start=True)
                    add(o[:, P:3 * P].rearrange("p (u n) -> p u n", n=P), exact("eye"), units(exact("fox_add"), 2))
                    for part in (nlf_hi, nlf_lo):
                        add(o, part[:, 0, h:h + 1].to_broadcast([P, P]), tri3)
                        add(o[:, P:TOK], part[:, 1, h:h + 1].to_broadcast([P, P]), exact("tri"))
                    add(o[:, 0:TOK], q[:, P:TOK], k)
                    last = add(o[:, TOK:3 * P], q[:, 0:P], k[:, 0:P])
                last.then_inc(sem("fox_logits"), 1)

            def fox_turn_probs(r):
                pe.wait_ge(sem("fox_probs"), 4 * (r + 1))
                for hh in range(2):
                    h = 2 * r + hh
                    pe.transpose(PS[:, 6 + hh, 2 * P:3 * P], probs0[:, h, :], ident[:, :])
                    for j in range(2):
                        last = pe.transpose(PS[:, 6 + hh, j * P:(j + 1) * P], probs1[:, h, j * P:(j + 1) * P], ident[:, :])
                last.then_inc(sem("fox_probs_turned"), 1)

            def fox_values(r):
                pe.wait_ge(sem("fox_probs_copied"), r + 1)
                for hh in range(2):
                    h = 2 * r + hh
                    v = lambda t: tokm[:, t, TOKM["fox_v"], h * DH:(h + 1) * DH]
                    o = PS[:, 6 + hh, 3 * P:512]
                    mm(o[:, 0:DH], probs_t[:, h, 2, :], v(0))
                    mm(o[:, DH:P], probs_t[:, h, 0, :], v(0), True, False)
                    last = mm(o[:, DH:P], probs_t[:, h, 1, :], v(1), False, True)
                last.then_inc(sem("fox_out"), 1)

            def la_turn_keys():
                pe.wait_ge(sem("hg_keys"), 1)
                pe.wait_ge(sem("qk_gram_read"), 1)
                for f in range(2):
                    for t in range(TT):
                        last = pe.transpose(PS[:, 7, f * TOK + t * P:f * TOK + (t + 1) * P],
                                            tokm[:, t, TOKM["hg_f"], f * P:(f + 1) * P], ident[:, :])
                last.then_inc(sem("hg_keys_turned"), 1)

            def la_exponents(k, part):
                if part == 0 and k == 0:
                    pe.wait_ge(sem("la_split"), 1)
                elif part == 0:
                    pe.wait_ge(sem("level_exp"), k)
                else:
                    pe.wait_ge(sem("hg_exp"), k + 1)
                for t in range(TT):
                    first, second = MASK["e1"] + 2 * k, MASK["tri"] if k == 3 and t == 1 else MASK["e1"] + 2 * k + 1
                    rhs = level_masks[:, first:second + 1:second - first, :]
                    for f in range(2) if part == 0 else (2,):
                        o = PS[:, 6 + t, f * TOK:(f + 1) * TOK] if part == 0 else PS[:, 6, t * TOK:(t + 1) * TOK]
                        o = o.rearrange("p (m n) -> p m n", m=2)
                        mm(o, la_hi[:, t, f * P:(f + 1) * P], rhs, True, False)
                        last = mm(o, la_lo[:, t, f, :], rhs, False, True)
                last.then_inc(sem("hg_exps" if part == 0 else "gla_exps"), 1)

            def la_rows(h):
                if h < 4:
                    return slice(64 * (h % 2), 64 * (h % 2) + 64), h // 2
                return slice(32 * (h - 4), 32 * (h - 4) + 32), 2

            def la_pairs(lv, heads):
                hg = heads[0] < 4
                if lv >= 0:
                    pe.wait_ge(sem("level_operand"), lv + 1)
                    pe.wait_ge(sem("hg_pairs_read" if hg else "gla_pairs_read"), lv + 1)
                def operands(h):
                    r, f = la_rows(h)
                    return ((chm[r, 9 + f, :], chm[r, 6 + f, :]) if lv < 0 else
                            (z_lv[r, lv % 2, f * TOK:(f + 1) * TOK],) * 2)

                for t in range(TT if lv < 7 else 1):
                    for j in range(2 if lv < 6 else 1):
                        for h in heads:
                            k, q = operands(h)
                            if lv < 6:
                                c = (h + j) % 2
                                tok = slice(t * P + c * CHUNK, t * P + (c + 1) * CHUNK)
                                last = mm(chunk_pair_bank(t, h, c), k[:, tok], q[:, tok])
                            elif lv == 6:
                                last = mm(chunk_pair_bank(t, h, 0), k[:, t * P:t * P + CHUNK],
                                          q[:, t * P + CHUNK:(t + 1) * P])
                            else:
                                last = mm(pair_bank(0, h), k[:, 0:P], q[:, P:TOK])
                last.then_inc(sem("hg_pairs" if hg else "gla_pairs"), 1)

            def la_all():
                pe.wait_ge(sem("fox_out_read"), 2)
                la_exponents(0, 0)
                la_exponents(0, 1)
                pe.wait_ge(sem("pairs_free"), 1)
                hg, gla = range(4), range(4, 8)
                la_pairs(-1, hg)
                la_pairs(-1, gla)
                for lv in range(8):
                    if lv < 6:
                        la_exponents(lv // 2 + 1, lv % 2)
                    la_pairs(lv, hg)
                    la_pairs(lv, gla)
                src = lambda h, t: tokm[:, t, TOKM["hg_i"] if h < 4 else TOKM["gla_v"], (h % 4) * DH:(h % 4 + 1) * DH]
                o = lambda h, t: PS[:, 6 + h // 4, t * 256 + (h % 4) * DH:t * 256 + (h % 4 + 1) * DH]
                pe.wait_ge(sem("hg_pairs_read"), 8)
                pe.wait_ge(sem("gla_pairs_read"), 8)
                pe.wait_ge(sem("diagonals_spread"), 1)
                pe.wait_ge(sem("zeros"), 1)
                for bank in (6, 7):
                    pe.matmul(PS[:, bank, :], zeros_r[:, 0:P], zeros_r[:, :], start=True, stop=False, skip_group_check=True)
                for h in range(8):
                    for t in range(TT):
                        pe.matmul(o(h, t), a_la[:, la_unit(t, h), :], src(h, t), start=False, stop=False,
                                  skip_group_check=True)
                for h in range(8):
                    if h % 4 == 0:
                        pe.wait_ge(sem("hg_pairs_read" if h == 0 else "gla_pairs_read"), 9)
                    last = pe.matmul(o(h, 1), a_top[:, la_top_unit(h), :], src(h, 0), start=False, stop=True,
                                     skip_group_check=True)
                    if h % 4 == 3:
                        last.then_inc(sem("la_out"), 1)

            before = {3: [gates], 6: [gdn_channels], 7: [gdn_turn_decay], 14: [gdn_solve]}
            middle = {1: [turn_small], 3: [gk_product], 4: [gdn_tokens], 6: [gdn_grams], 7: [gdn_turn_m], 8: [la_turn_keys], 14: [fox_turn]}
            for lv in range(5):
                before[9 + lv] = [lambda lv=lv: gdn_cx(lv)]
                middle[9 + lv] = [lambda lv=lv: gdn_xcx(lv)]
            for n, what in enumerate(MIX_ORDER):
                if n == 0:
                    small_columns()
                    continue
                for piece in before.get(n, ()):
                    piece()
                if n >= 2:
                    pe.wait_ge(sem(f"proj_bank_read{n % 2}"), n // 2)
                columns(n, n % RING, 4 + n % 2, (h_hi, h_lo), what in CHANNEL_MAJOR, middle=middle.get(n, ()))
            gdn_state_in(0)
            fox_logits(0)
            gdn_state_out(0)
            gdn_state_in(1)
            fox_turn_probs(0)
            gdn_state_out(1)
            gdn_state_in(2)
            fox_values(0)
            gdn_state_out(2)
            gdn_state_in(3)
            fox_logits(1)
            gdn_state_out(3)
            fox_turn_probs(1)
            fox_values(1)
            la_all()

            def rows_4(name, acc, operand, fresh=None, tiles=True):
                for j in range(4):
                    n = STEP[name] + j
                    if fresh:
                        chunks_ready(fresh, 2 * j)
                    row_block(n, n % RING, acc, operand, 2 * j, j == 0, j == 3, tiles and j == 3)

            for j in range(4):
                if j % 2 == 0:
                    pe.wait_ge(sem("group_normed"), j + 2)
                    turn("mixed", xn, banks=(j, j + 1))
                n = STEP["mix_out"] + j
                chunks_ready("mixed", 2 * j)
                row_block(n, n % RING, low4, (act_hi, act_lo), 2 * j, j == 0, j == 3, j == 3)

            def ffn(f, fresh, p_name=None):
                n0 = STEP[f"ffn{f}"]
                slot = lambda j: (n0 + j) % RING
                for t in range(TT):
                    for half in range(2):
                        pe.matmul(low4[:, t, half * 512:(half + 1) * 512], zeros_r[:, 0:P], zeros_r[:, :],
                                  start=True, stop=False, skip_group_check=True)
                chunks_ready(fresh, 1)
                columns(n0, slot(0), 4, (h_hi, h_lo), fresh=fresh)
                columns(n0 + 1, slot(1), 5, (h_hi, h_lo))
                if p_name:
                    pe.wait_ge(sem("p_loaded"), 16 * f)
                    turn(p_name, p_tok, 6)
                with pe.Fori(1, PAIRS) as i:
                    n = n0 - 1 + 3 * i
                    pe.wait_ge(sem("gate_convolved"), PAIRS * f + i)
                    columns(n, slot(2), 4, (h_hi, h_lo))
                    pe.wait_ge(sem("up_read"), PAIRS * f + i)
                    columns(n + 1, slot(0), 5, (h_hi, h_lo))
                    pe.wait_ge(sem("hidden_split"), PAIRS * f + i)
                    row_block(n + 2, slot(1), low4, (hid_hi, hid_lo), 0, False, False)
                pe.wait_ge(sem("hidden_split"), PAIRS * (f + 1))
                n = n0 + 3 * PAIRS - 1
                row_block(n, n % RING, low4, (hid_hi, hid_lo), 0, False, True, True)

            turn("norm2", xn, tile_ready=2)
            ffn(0, "norm2")

            turn("pre_mix0", xn, tile_ready=3)
            n0 = STEP["sc_in"]
            with pe.Fori(0, 4) as i:
                for j in range(3):
                    pe.wait_ge(sem("sc_bank_read"), 3 * i + (j + 1))
                    columns(n0 + j + 3 * i, (n0 + j) % RING, 4 + j, (h_hi, h_lo), fresh="pre_mix0" if j == 0 else None)
            pe.wait_ge(sem("table_loaded"), 32)
            mm(PS[0:N_HEADS, 7, 0:N_DIST], table, onehot).then_inc(sem("bias_by_head"), 1)
            for j in range(4):
                n = STEP["sc_out"] + j
                pe.wait_ge(sem("sc_hidden"), j + 1)
                row_block(n, n % RING, low4, (act_hi, act_lo), 2 * j, j == 0, j == 3, j == 3)

            def ffn_and_ple(layer):
                k = 4 if layer == 0 else 7
                turn(f"pre_ffn{layer}", xn, tile_ready=k)
                ffn(1 + layer, f"pre_ffn{layer}", f"p{layer}")
                chunks_ready(f"p{layer}", 1)
                n = STEP[f"ple_proj{layer}"]
                row_block(n, n % RING, high4, (p_hi, p_lo), 0, True, True)
                pe.wait_ge(sem("x_tile"), 2 * k)
                turn(f"pre_ple{layer}", xn, 0, tile_ready=k + 1)
                chunks_ready(f"pre_ple{layer}", 7)
                rows_4(f"ple_gate{layer}", low4, (h_hi, h_lo))

            ffn_and_ple(0)

            pe.wait_ge(sem("ple_gate"), 2)
            pe.wait_ge(sem("bias_loaded"), 2 * 16)
            for b in range(4):
                last = mm(PS[:, b, :], flip, bias_rev[:, 2 * b:2 * b + 2, :].rearrange("p h n -> p (h n)"))
            last.then_inc(sem("bias_flipped"), 1)
            turn("pre_mix1", xn, tile_ready=6)

            def turn_weights(h):
                if h == 0:
                    pe.wait_ge(sem("att_bank_read0"), 4)
                else:
                    pe.wait_ge(sem("att_copied"), h)
                pe.wait_ge(sem("att_weights"), h + 1)
                for j in range(3):
                    last = pe.transpose(PS[:, 4, j * P:(j + 1) * P], at_w[h % 2][:, j, :], ident[:, :])
                last.then_inc(sem("att_turned"), 1)

            def logits(h):
                if h:
                    pe.wait_ge(sem("logits_read"), h)
                else:
                    pe.wait_ge(sem("att_bank_read0"), 3)
                if h == 2:
                    pe.wait_ge(sem("att_bank_read1"), 3)
                if h == 4:
                    pe.wait_ge(sem("att_bank_read0"), 4)
                if h == 6:
                    pe.wait_ge(sem("att_bank_read1"), 4)
                for m in range(2):
                    r = slice(64 * m, 64 * m + 64)
                    mm(PS[:, 6 + m, 0:TOK], q_t[r, h, P:TOK], k_t[r, h, :])
                    last = mm(PS[:, 6 + m, TOK:TOK + P], q_t[r, h, 0:P], k_t[r, h, 0:P])
                last.then_inc(sem("logits"), 1)

            for j in range(8):
                n = STEP["att_k"] + j
                if j == 1:
                    chunks_ready("pre_mix1", 7)
                if j >= 2:
                    pe.wait_ge(sem(f"att_bank_read{j % 2}"), j // 2)
                pieces = [lambda: logits(j - 5)] if j >= 5 else []
                if j == 5:
                    pieces.insert(0, lambda: pe.wait_ge(sem("bias_copied"), 1))
                if j == 7:
                    pieces.insert(0, lambda: turn_weights(0))
                columns(n, n % RING, 4 + j % 2, (act_hi, act_lo) if j < 4 else (h_hi, h_lo),
                        fresh="pre_mix1" if j == 0 else None, middle=pieces)
            for j in range(4):
                n = STEP["att_v"] + j
                row_block(n, n % RING, low4, (act_hi, act_lo), 2 * j, j == 0, j == 3,
                          middle=(lambda: turn_weights(j + 1), lambda: logits(j + 3)))
            turn_weights(5)
            logits(7)
            pe.wait_ge(sem("v_copied"), 2)

            def head_out(h, t):
                v = lambda t: v_tok[:, t, h * P:(h + 1) * P]
                o = low4[:, t, h * P:(h + 1) * P]
                if t == 0:
                    return mm(o, at_wt[:, h, 2, :], v(0))
                mm(o, at_wt[:, h, 0, :], v(0), True, False)
                return mm(o, at_wt[:, h, 1, :], v(1), False, True)

            for h in range(6):
                pe.wait_ge(sem("att_copied"), h + 1)
                for t in range(TT):
                    head_out(h, t)
            turn_weights(6)
            turn_weights(7)
            for t in range(TT):
                for h in (6, 7):
                    pe.wait_ge(sem("att_copied"), h + 1)
                    last = head_out(h, t)
                last.then_inc(sem("head_out"), 1)
            turn("att", xn, tile_ready=lambda t: (sem("heads_normed"), t + 1))
            rows_4("att_out", low4, (act_hi, act_lo), "att")
            ffn_and_ple(1)

        @block.scalar
        def _(act):
            own, count = sem("act_own"), [0]

            def mark(ins):
                count[0] += 1
                ins.then_inc(own, 1)

            def link(ins):
                mark(ins)
                act.wait_ge(own, count[0])

            def split(n, slot, lap, steady=True):
                act.wait_ge(raw_loaded[slot], 16 * lap)
                if steady:
                    act.wait_ge(block_used, n - (RING - 1))
                act.activation(w_hi[:, slot, :], raw[:, slot, :], ACT.Copy).then_inc(hi_ready, 1)

            def ahead(n):
                if n + 2 < N_BLOCKS:
                    split(n + 2, (n + 2) % RING, (n + 2) // RING + 1, n + 2 >= RING)

            def ahead_in_loop(n_base, i):
                m = n_base + 2
                split(m + 3 * i, m % RING, i + (m // RING + 1))

            def inverse_rms(s, n, done=None):
                link(act.activation(s, s, ACT.Ln, scale=1.0 / n, bias=eps[:, :]))
                ins = act.activation(s, s, ACT.Exp, scale=-0.5)
                if done is None:
                    link(ins)
                else:
                    ins.then_inc(done, 1)

            def norm(k, squares):
                s = stat[:, 2 * (k % 2):2 * (k % 2) + 2]
                if k > 1:
                    act.wait_ge(sem("x_tile"), 2 * k - 3)
                link(act.activation(squares, x[:, 0, :], ACT.Square, accum_out=s[:, 0:1]))
                inverse_rms(s[:, 0:1], D)
                act.activation(xn[:, 0, :], x[:, 0, :], ACT.Copy, scale=s[:, 0:1]).then_inc(sem("tokens0_ready"), 1)
                act.wait_ge(sem("squares1"), k)
                inverse_rms(s[:, 1:2], D, sem("rstd1"))

            def turned(name, operands, bank=4, banks=None):
                _, p0, chunks = TURN[name]
                for b in banks or range(chunks // 2):
                    act.wait_ge(chunks_turned, p0 + b + 1)
                    for gain, hi, _ in operands:
                        for j in (2 * b, 2 * b + 1):
                            src = PS[:, bank + b, (j % 2) * TOK:(j % 2 + 1) * TOK]
                            if gain is None:
                                ins = act.activation(hi[:, j, :], src, ACT.Copy)
                            else:
                                ins = act.activation(hi[:, j, :], src, ACT.Identity, scale=gain(j))
                    ins.then_inc(part_hi, 1)

            act.preload_act_table_set(TABLES)
            act.wait_ge(sem("x_loaded"), 16)
            act.wait_ge(sem("eps_set"), 1)
            norm(1, sq)
            act.wait_ge(inputs, N_INPUTS)
            split(0, 0, 1, False)
            turned("norm1", [(lambda j: ch("norm1", j), h_hi, h_lo)])
            split(1, 1, 1, False)

            def gates():
                act.wait_ge(sem("mix_inputs"), 48)
                act.wait_ge(sem("small_turned"), 1)
                act.activation(small.rearrange("p t n -> p (t n)"), PS[:, 1, 0:TT * SMALL], ACT.Copy) \
                    .then_inc(sem("small_ready"), 1)
                act.activation(level_masks[:, :, :], masks[:, 0:N_LEVEL_MASKS, :], ACT.Copy) \
                    .then_inc(sem("masks_rounded"), 1)
                act.wait_ge(sem("gates_z"), 1)
                link(act.activation(gate_l, gate_z, ACT.Abs))
                link(act.activation(gate_l, gate_l, ACT.Exp, scale=-1.0))
                act.activation(gate_l, gate_l, ACT.Ln, bias=1.0)
                act.activation(ea, rows("gdn_a_log", 4), ACT.Exp)
                act.activation(beta, small[:, :, 24:28], ACT.Exp, scale=-1.0).then_inc(sem("gates_exp"), 1)

            def gate_exps():
                act.wait_ge(sem("gate_sums"), 1)
                act.activation(th(e_g), PS[:, 0, 0:8], ACT.Exp)
                act.activation(th(e_rest), PS[:, 0, 8:16], ACT.Exp)
                act.activation(e_last.rearrange("p t c h -> p (t c h)"), PS[:, 0, 16:32], ACT.Exp) \
                    .then_inc(sem("gate_exps"), 1)

            def gk_logs():
                act.wait_ge(sem("gk_logits"), 1)
                log_sigmoid(la[:, :, 2, :], 1)

            def log_sigmoid(dst, k):
                s = sq[:, (k - 1) * 512:(k - 1) * 512 + dst.shape[1] * dst.shape[2]].rearrange("p (t n) -> p t n", t=TT)
                link(act.activation(s, dst, ACT.Abs))
                link(act.activation(s, s, ACT.Exp, scale=-1.0))
                act.activation(s, s, ACT.Ln, bias=1.0).then_inc(sem("logits_ln"), 1)

            def gdn_silu(s):
                act.wait_ge(sem("gdn_taps"), s + 1)
                v = chm[:, 2 * s:2 * s + 2, :].rearrange("p f n -> p (f n)")
                act.activation(v, v, ACT.Silu).then_inc(sem("gdn_convolved"), 1)

            def gdn_tokens():
                gdn_silu(2)
                act.preload_act_table_set(TABLES)

            def gdn_norms():
                act.wait_ge(sem("gdn_token_major"), 1)
                act.wait_ge(sem("gk_read"), 1)
                act.activation(sq, PS[:, 0:2, :].rearrange("p b n -> p (b n)"), ACT.Square).then_inc(sem("gdn_squares"), 1)
                rstd16("gdn_sums", "gdn_rstd", 1.0)

            def rstd16(ready, done, scale, n=16):
                act.wait_ge(sem(ready), 1)
                s = stat[:, 8:8 + n]
                link(act.activation(s, s, ACT.Ln, scale=scale, bias=eps[:, :]))
                act.activation(s, s, ACT.Exp, scale=-0.5).then_inc(sem(done), 1)

            def gdn_channels():
                act.wait_ge(sem("gdn_channel_major"), 1)
                act.activation(chm[:, 0:6, :].rearrange("p f n -> p (f n)"),
                               PS[:, 0:3, :].rearrange("p b n -> p (b n)"), ACT.Copy).then_inc(sem("gdn_copied"), 1)

            bank2 = lambda b: PS[:, b:b + 2, :].rearrange("p b n -> p (b n)")
            flat = lambda v: v.rearrange("p u n -> p (u n)")

            def gdn_grams():
                act.wait_ge(sem("decay_logs"), 1)
                act.activation(flat(dec), bank2(2), ACT.Exp).then_inc(sem("decay"), 1)

            def gdn_turn_decay():
                act.wait_ge(sem("decay_turned"), 1)
                act.activation(flat(dec_t), bank2(2), ACT.Copy).then_inc(sem("decay_t"), 1)

            def gdn_turn_m():
                act.wait_ge(sem("m_turned"), 1)
                act.activation(flat(mt_gd), bank2(0), ACT.Copy).then_inc(sem("mt_ready"), 1)

            def gdn_cx(lv):
                act.wait_ge(sem("cx"), lv + 1)
                act.activation(flat(y_gd), bank2(2), ACT.Copy).then_inc(sem("cx_copied"), 1)

            def gdn_solve():
                act.wait_ge(sem("solved"), 1)
                act.activation(flat(u_gd), PS[:, 2, :], ACT.Copy)
                act.activation(flat(w_t), PS[:, 3, :], ACT.Copy).then_inc(sem("solution"), 1)

            def head_post(k, grp):
                act.wait_ge(sem("group_out"), k + 1)
                half = k % 2
                act.activation(sq[:, 512 * half:512 * half + 512].rearrange("p (t n) -> p t n", t=TT), group_view(grp),
                               ACT.Square) \
                    .then_inc(sem("group_squares"), 1)
                act.wait_ge(sem("group_sums"), k + 1)
                s = stat[:, 8 + 8 * half:16 + 8 * half]
                link(act.activation(s, s, ACT.Ln, scale=1.0 / DH, bias=eps[:, :]))
                act.activation(s, s, ACT.Exp, scale=-0.5).then_inc(sem("group_rstd"), 1)

            def silu_gates():
                act.wait_ge(sem("proj_bank_read0"), 8)
                act.wait_ge(sem("proj_bank_read1"), 7)
                act.activation(tokm[:, :, 6:9, :], tokm[:, :, 6:9, :], ACT.Silu)
                act.activation(chm[:, 6:8, :], chm[:, 6:8, :], ACT.Silu).then_inc(sem("gates_silu"), 1)
                act.preload_act_table_set(TABLES)

            def fox_norms():
                projected(act, "fox_k")
                act.activation(sq.rearrange("p (t s n) -> p t s n", t=TT, s=2), tokm[:, :, 0:2, :], ACT.Square) \
                    .then_inc(sem("fox_squares"), 1)
                rstd16("fox_sums", "fox_rstd", 1.0 / DH)

            def fox_turn():
                act.wait_ge(sem("fox_turned"), 1)
                act.activation(flat(fq_t), PS[:, 6, :], ACT.Copy)
                act.activation(flat(fk_t), PS[:, 7, :], ACT.Copy).then_inc(sem("fox_copied"), 1)
                act.wait_ge(sem("la_ready"), 1)
                act.activation(la_hi, la.rearrange("p t f n -> p t (f n)"), ACT.Copy).then_inc(sem("la_hi"), 1)

            def fox_exps(r):
                act.wait_ge(sem("fox_max"), 2 * (r + 1))
                for hh in range(2):
                    h = 2 * r + hh
                    act.activation(probs0[:, h, :], PS[:, 6 + hh, 2 * P:3 * P], ACT.Exp, bias=stat[:, 24 + h:25 + h],
                                   accum_out=stat[:, 32 + h:33 + h]).then_inc(sem("fox_probs"), 1)
                    act.activation(probs1[:, h, :], PS[:, 6 + hh, 0:TOK], ACT.Exp, bias=stat[:, 28 + h:29 + h],
                                   accum_out=stat[:, 36 + h:37 + h]).then_inc(sem("fox_probs"), 1)

            def fox_copy(r):
                act.wait_ge(sem("fox_probs_turned"), r + 1)
                act.activation(probs_t[:, 2 * r:2 * r + 2, :, :].rearrange("p h j n -> p h (j n)"), PS[:, 6:8, 0:3 * P],
                               ACT.Copy).then_inc(sem("fox_probs_copied"), 1)

            def la_keys():
                projected(act, "hg_f")
                log_sigmoid(tokm[:, :, TOKM["hg_f"], :], 2)
                act.wait_ge(sem("hg_keys_log"), 1)
                z = tokm[:, :, TOKM["hg_f"], :]
                act.activation(z, z, ACT.Exp).then_inc(sem("hg_keys"), 1)

            def la_turn_keys():
                act.wait_ge(sem("hg_keys_turned"), 1)
                act.activation(chm[:, 9:11, :].rearrange("p f n -> p (f n)"), PS[:, 7, :], ACT.Copy) \
                    .then_inc(sem("la_keys"), 1)

            def la_all():
                tfn = lambda v: v.rearrange("p (f t n) -> p t f n", t=TT, n=P)
                for k in range(4):
                    if k >= 2:
                        act.wait_ge(sem("level_operand"), 2 * k - 2)
                    act.wait_ge(sem("hg_exps"), k + 1)
                    slot = 2 * (k % 2)
                    for j in range(2):
                        src = PS[:, 6:8, :].rearrange("p t (f l n) -> p t f l n", l=2, n=P)[:, :, :, j, :]
                        ins = act.activation(tfn(w_lv[:, slot + j, 0:512]), src, ACT.Exp)
                    ins.then_inc(sem("hg_exp"), 1)
                    act.wait_ge(sem("gla_exps"), k + 1)
                    src = PS[:, 6, :].rearrange("p (t l n) -> p l t n", l=2, n=P)
                    act.activation(w_lv[:, slot:slot + 2, 512:768].rearrange("p l (t n) -> p l t n", n=P), src, ACT.Exp) \
                        .then_inc(sem("level_exp"), 1)
                    if k == 1:
                        head_post(0, 1)
                    if k == 2:
                        head_post(1, 0)
                act.wait_ge(sem("hg_pairs_read"), 7)
                act.wait_ge(sem("gla_pairs_read"), 7)
                act.activation(a_la[0:CHUNK, :, 0:CHUNK], a_packed[0:CHUNK, :, :], ACT.Copy)
                act.activation(a_la[CHUNK:P, :, CHUNK:P], a_packed[CHUNK:P, :, :], ACT.Copy) \
                    .then_inc(sem("diagonals_spread"), 1)

            before = {3: [lambda: gdn_silu(0), gate_exps], 4: [lambda: gdn_silu(1), gdn_tokens], 6: [gdn_channels, la_keys], 7: [gdn_turn_decay],
                      14: [gdn_solve]}
            middle = {1: [gates], 3: [gk_logs], 4: [gdn_norms], 6: [gdn_grams], 7: [gdn_turn_m], 8: [la_turn_keys], 10: [fox_norms],
                      14: [fox_turn]}
            for lv in range(5):
                before[9 + lv] = [lambda lv=lv: gdn_cx(lv)]
            for n, what in enumerate(MIX_ORDER):
                for piece in before.get(n, ()):
                    piece()
                ahead(n)
                for piece in middle.get(n, ()):
                    piece()
                act.wait_ge(block_used, n + 1)
                bank = PS[:, 4 + n % 2, :]
                read = sem(f"proj_bank_read{n % 2}")
                if what == "small":
                    act.activation(small_t, bank[0:SMALL, 0:TOK], ACT.Copy).then_inc(read, 1)
                elif what.startswith("gdn_") and what in CHANNEL_MAJOR:
                    s = ("gdn_q", "gdn_k", "gdn_v").index(what)
                    for f in range(2):
                        ins = act.activation(chm[:, 2 * s + f, :], bank[:, f * TOK:(f + 1) * TOK], ACT.Identity,
                                             scale=ch("gdn_conv", 3 * 6 + 2 * s + f))
                    ins.then_inc(sem("gdn_last_tap"), 1)
                elif what == "hg_q":
                    act.activation(chm[:, 6:8, :].rearrange("p f n -> p (f n)"), bank, ACT.Copy).then_inc(read, 1)
                elif what == "gla_qk":
                    act.activation(chm[:, 8, :], bank[:, 0:TOK], ACT.Copy, scale=32.0 ** -0.5)
                    act.activation(chm[:, 11, :], bank[:, TOK:512], ACT.Copy).then_inc(read, 1)
                else:
                    act.activation(tokm[:, :, TOKM[what], :], bank.rearrange("p (t n) -> p t n", t=TT), ACT.Copy) \
                        .then_inc(read, 1)
            silu_gates()
            fox_exps(0)
            fox_copy(0)
            fox_exps(1)
            fox_copy(1)
            la_all()
            turned("mixed", [(None, act_hi, act_lo)], banks=(0, 1))
            head_post(2, 2)
            ahead(STEP["mix_out"])
            head_post(3, 3)
            ahead(STEP["mix_out"] + 1)
            turned("mixed", [(None, act_hi, act_lo)], banks=(2, 3))
            ahead(STEP["mix_out"] + 2)

            def ahead_4(name):
                for j in range(4):
                    ahead(STEP[name] + j)

            ahead(STEP["mix_out"] + 3)

            norm(2, junk[:, 0, :])
            turned("norm2", [(lambda j: ch("norm2", j), h_hi, h_lo)])

            def ffn(f, p_name=None):
                n0 = STEP[f"ffn{f}"]
                conv = PC[f"ffn_conv{f}"]

                def last_tap(dst, bank, i, half, ready):
                    for c in range(2):
                        col = i * 2 + (half * FT + c)
                        w = channel[:, bass.ds(col + (conv + 2 * 2 * FT), 1)]
                        b = channel[:, bass.ds(col + PC["ffn_bias"], 1)] if f == 0 else 0.0
                        ins = act.activation(dst[:, c, :], PS[:, bank, c * TOK:(c + 1) * TOK], ACT.Identity,
                                             scale=w, bias=b)
                    ins.then_inc(ready, 1)

                def gate(i, n_used):
                    act.wait_ge(block_used, n_used)
                    last_tap(y_gate, 4, i, 0, sem("gate_last_tap"))

                def up(i, n_used):
                    act.wait_ge(sem("gate_convolved"), i + (PAIRS * f + 1))
                    act.activation(s_gate, y_gate, ACT.Silu).then_inc(sem("gate_silu"), 1)
                    act.wait_ge(block_used, n_used)
                    last_tap(y_up, 5, i, 1, sem("up_last_tap"))

                def hid(i):
                    act.wait_ge(sem("hidden_ready"), i + (PAIRS * f + 1))
                    act.activation(hid_hi, hidden, ACT.Copy).then_inc(sem("hidden_hi"), 1)

                ahead(n0)
                gate(0, n0 + 1)
                ahead(n0 + 1)
                up(0, n0 + 2)
                hid(0)
                if p_name:
                    turned(p_name, [(None, p_hi, p_lo)], 6)
                with act.Fori(1, PAIRS) as i:
                    n = n0 - 1
                    ahead_in_loop(n, i)
                    gate(i, n + 1 + 3 * i)
                    ahead_in_loop(n + 1, i)
                    up(i, n + 2 + 3 * i)
                    ahead_in_loop(n + 2, i)
                    act.wait_ge(block_used, n + 3 + 3 * i)
                    hid(i)
                ahead(n0 + 3 * PAIRS - 1)
                act.preload_act_table_set(TABLES)

            ffn(0)

            norm(3, junk[:, 0, :])
            turned("pre_mix0", [(lambda j: ch("pre_mix0", j), h_hi, h_lo)])
            n0 = STEP["sc_in"]
            with act.Fori(0, 4) as i:
                ahead_in_loop(n0, i)
                act.wait_ge(block_used, n0 + 1 + 3 * i)
                act.activation(flat(s_gate), PS[:, 4, :], ACT.Copy).then_inc(sem("sc_gc"), 1)
                ahead_in_loop(n0 + 1, i)
                act.wait_ge(sem("sc_product"), i + 1)
                for c in range(2):
                    ins = act.activation(y_gate[:, c, :], y_up[:, c, :], ACT.Identity,
                                         scale=channel[:, bass.ds(2 * i + (PC["sc_conv"] + 16 + c), 1)])
                ins.then_inc(sem("sc_last_tap"), 1)
                ahead_in_loop(n0 + 2, i)
                act.wait_ge(sem("sc_gated"), i + 1)
                act.activation(act_hi[:, bass.ds(2 * i, 2), :], hidden, ACT.Copy).then_inc(sem("sc_hi"), 1)
            ahead(STEP["sc_out"])
            act.wait_ge(sem("bias_by_head"), 1)
            act.activation(bias_row, PS[0:N_HEADS, 7, 0:N_DIST], ACT.Copy).then_inc(sem("bias_rows"), 1)
            for j in range(1, 4):
                ahead(STEP["sc_out"] + j)

            def post(k, n_used):
                for t in range(TT):
                    if t == 0:
                        act.wait_ge(sem("tile_summed"), k)
                    else:
                        act.wait_ge(block_used, n_used)
                    s = stat[:, 4 + t:5 + t]
                    link(act.activation(junk[:, t, :], low4[:, t, :], ACT.Square, accum_out=s))
                    inverse_rms(s, D, sem("post_rstd"))

            post(3, STEP["sc_out"] + 4)
            norm(4, gate_s[:, 0, :])
            turned("pre_ffn0", [(lambda j: ch("pre_ffn0", j), h_hi, h_lo)])

            def ffn_and_ple(layer, k):
                ffn(1 + layer, f"p{layer}")
                post(k, STEP[f"ffn{1 + layer}"] + 3 * PAIRS)
                norm(k + 1, gate_s[:, 0, :])
                turned(f"pre_ple{layer}", [(lambda j: ch(f"pre_ple{layer}", j), h_hi, h_lo)], 0)
                ahead(STEP[f"ple_proj{layer}"])
                for j in range(3):
                    ahead(STEP[f"ple_gate{layer}"] + j)
                act.wait_ge(sem("tile_summed"), k + 1)
                act.activation(gate_s[:, 0, :], low4[:, 0, :], ACT.Sigmoid).then_inc(sem("ple_gate"), 1)
                ahead(STEP[f"ple_gate{layer}"] + 3)
                act.wait_ge(block_used, STEP[f"ple_gate{layer}"] + 4)
                act.activation(gate_s[:, 1, :], low4[:, 1, :], ACT.Sigmoid).then_inc(sem("ple_gate"), 1)
                act.preload_act_table_set(TABLES)
                for t in range(TT):
                    act.wait_ge(sem("ple_product"), 2 * layer + t + 1)
                    s = stat[:, 4 + t:5 + t]
                    link(act.activation(junk[:, t, :], gate_s[:, t, :], ACT.Square, accum_out=s))
                    inverse_rms(s, D, sem("post_rstd"))

            ffn_and_ple(0, 4)
            norm(6, junk[:, 0, :])
            turned("pre_mix1", [(lambda j: ch("pre_mix1", j), h_hi, h_lo), (lambda j: ch("kv", j), act_hi, act_lo)])

            def soften(h):
                act.wait_ge(sem("att_max"), 2 * (h + 1))
                a, l1, l0 = att_stat[h % 2], lg1[h % 2], lg0[h % 2]
                for m in range(2):
                    act.activation(l1[:, m, :], l1[:, m, :], ACT.Exp, bias=a[:, m:m + 1], accum_out=a[:, 4 + m:5 + m])
                    ins = act.activation(l0[:, m, :], l0[:, m, :], ACT.Exp, bias=a[:, 2 + m:3 + m],
                                         accum_out=a[:, 6 + m:7 + m])
                ins.then_inc(sem("att_exp"), 1)

            def copy_weights(h):
                act.wait_ge(sem("att_turned"), h + 1)
                act.activation(flat(at_wt[:, h, :, :]), PS[:, 4, 0:384], ACT.Copy) \
                    .then_inc(sem("att_copied"), 1)

            for j in range(8):
                n = STEP["att_k"] + j
                ahead(n)
                if j >= 7:
                    copy_weights(j - 7)
                if j >= 5:
                    soften(j - 5)
                act.wait_ge(block_used, n + 1)
                dst, scale = (k_t, 1.0) if j < 4 else (q_t, DH ** -0.5)
                i = 2 * (j % 4)
                act.activation(flat(dst[:, i:i + 2, :]), PS[:, 4 + j % 2, :], ACT.Copy, scale=scale) \
                    .then_inc(sem(f"att_bank_read{j % 2}"), 1)
                if j == 0:
                    act.wait_ge(sem("lambda_sums"), 1)
                    act.activation(lam[:, 0:2], lam[:, 0:2], ACT.Exp).then_inc(sem("lambda_exps"), 1)
                if j == 2:
                    act.wait_ge(sem("bias_flipped"), 1)
                    act.activation(flat(bias_t), PS[:, 0:4, :].rearrange("p b n -> p (b n)"), ACT.Copy) \
                        .then_inc(sem("bias_copied"), 1)
            for j in range(4):
                ahead(STEP["att_v"] + j)
                copy_weights(j + 1)
                soften(j + 3)
            act.wait_ge(block_used, STEP["att_v"] + 4)
            act.activation(v_tok, low4, ACT.Copy).then_inc(sem("v_copied"), 2)
            copy_weights(5)
            soften(7)
            copy_weights(6)
            copy_weights(7)
            for t in range(TT):
                act.wait_ge(sem("head_out"), t + 1)
                act.activation(xn[:, t, :], low4[:, t, :], ACT.Square).then_inc(sem("head_squares"), 1)
                act.wait_ge(sem("subln_sums"), t + 1)
                s = stat[:, 8 + 8 * t:16 + 8 * t]
                inverse_rms(s, P, sem("subln_rstd"))
            turned("att", [(lambda j: ch("subln"), act_hi, act_lo)])
            ahead_4("att_out")
            post(6, STEP["att_out"] + 4)
            norm(7, gate_s[:, 0, :])
            turned("pre_ffn1", [(lambda j: ch("pre_ffn1", j), h_hi, h_lo)])
            ffn_and_ple(1, 7)

        @block.vector
        def _(dve):
            own, count = sem("dve_own"), [0]

            def mark(ins):
                count[0] += 1
                ins.then_inc(own, 1)

            def settle():
                dve.wait_ge(own, count[0])

            def link(ins):
                mark(ins)
                settle()

            def signal(which, n=1):
                settle()
                dve.sem_inc(which, n)

            tt, ts, stt = dve.tensor_tensor, dve.tensor_scalar, dve.scalar_tensor_tensor

            def split(n, slot):
                dve.wait_ge(hi_ready, n + 1)
                tt(w_lo[:, slot, :], raw[:, slot, :], w_hi[:, slot, :].bitcast(F), ALU.subtract).then_inc(lo_ready, 1)

            def ahead(n):
                if n + 2 < N_BLOCKS:
                    split(n + 2, (n + 2) % RING)

            def norm(k, squares):
                s = stat[:, 2 * (k % 2) + 1:2 * (k % 2) + 2]
                if k > 1:
                    dve.wait_ge(sem("x_tile"), 2 * k - 2)
                dve.tensor_tensor_reduce(squares, x[:, 1, :], x[:, 1, :], 1.0, 0.0, ALU.mult, ALU.add, s) \
                    .then_inc(sem("squares1"), 1)
                dve.wait_ge(sem("rstd1"), k)
                ts(xn[:, 1, :], x[:, 1, :], s, None, ALU.mult).then_inc(sem("tokens1_ready"), 1)

            def turned(name, operands, bank=4, banks=None):
                _, p0, chunks = TURN[name]
                for b in banks or range(chunks // 2):
                    dve.wait_ge(part_hi, p0 + b + 1)
                    for gain, hi, lo in operands:
                        for j in (2 * b, 2 * b + 1):
                            src = PS[:, bank + b, (j % 2) * TOK:(j % 2 + 1) * TOK]
                            if gain is None:
                                ins = tt(lo[:, j, :], src, hi[:, j, :].bitcast(F), ALU.subtract)
                            else:
                                ins = stt(lo[:, j, :], src, gain(j), hi[:, j, :].bitcast(F), ALU.mult, ALU.subtract)
                    ins.then_inc(part_ready, 1)

            dve.wait_ge(sem("x_loaded"), 16)
            norm(1, w_lv.rearrange("p a n -> p (a n)")[:, 0:D])
            split(0, 0)
            dve.wait_ge(inputs, N_INPUTS)
            turned("norm1", [(lambda j: ch("norm1", j), h_hi, h_lo)])
            split(1, 1)

            def sigmoid_rest(v):
                link(ts(v, v, 1.0, None, ALU.add))
                dve.reciprocal(v, v)

            def gates():
                dve.wait_ge(sem("small_ready"), 1)
                dve.wait_ge(sem("mix_inputs"), 48)
                tt(gate_z, small[:, :, 16:24], row[:, 0:8].rearrange("p (o n) -> p o n", o=1).to_broadcast([P, TT, 8]),
                   ALU.add).then_inc(sem("gates_z"), 1)
                dve.wait_ge(sem("gates_exp"), 1)
                mark(stt(lf, gate_z[:, :, 0:4], 0.0, gate_l[:, :, 0:4], ALU.min, ALU.subtract))
                mark(stt(gd, gate_z[:, :, 4:8], 0.0, gate_l[:, :, 4:8], ALU.max, ALU.add))
                mark(ts(beta, beta, 1.0, None, ALU.add))
                settle()
                mark(ts(nlf, lf, -1.0, None, ALU.mult))
                mark(dve.reciprocal(beta, beta))
                mark(tt(ngd, gd, ea.rearrange("p (o n) -> p o n", o=1).to_broadcast([P, TT, 4]), ALU.mult))
                settle()
                ts(gd, ngd, -1.0, None, ALU.mult).then_inc(sem("gates_ready"), 1)

            def gate_parts():
                dve.wait_ge(sem("gates_ready"), 1)
                mark(dve.tensor_copy(nlf_hi[:, :, :], nlf))
                mark(dve.tensor_copy(gd_hi[:, :, :], gd))
                settle()
                mark(tt(nlf_lo[:, :, :], nlf, nlf_hi[:, :, :].bitcast(F), ALU.subtract))
                mark(tt(gd_lo[:, :, :], gd, gd_hi[:, :, :].bitcast(F), ALU.subtract))
                settle()

            def gk_logs():
                dve.wait_ge(sem("gate_exps"), 1)
                mark(tt(be_g, beta, e_g, ALU.mult))
                dve.wait_ge(sem("gk_projected"), 1)
                b = rows("b_gk", P).rearrange("p (o n) -> p o n", o=1).to_broadcast([P, TT, P])
                ins = tt(la[:, :, 2, :], PS[:, 1, 256:512].rearrange("p (t n) -> p t n", t=TT), b, ALU.add)
                ins.then_inc(sem("gk_logits"), 1)
                dve.wait_ge(sem("gk_logits"), 1)
                dve.wait_ge(sem("logits_ln"), 1)
                s = sq[:, 0:256].rearrange("p (t n) -> p t n", t=TT)
                link(stt(la[:, :, 2, :], la[:, :, 2, :], 0.0, s, ALU.min, ALU.subtract))
                mark(ts(la[:, :, 2, :], la[:, :, 2, :], 1.0 / 16.0, None, ALU.mult))
                settle()
                signal(sem("gk_read"), 1)

            def gdn_taps(s, n):
                dve.wait_ge(sem("gdn_last_tap"), s + 1)
                for d in range(1, 4):
                    for f in range(2):
                        dst = chm[:, 2 * s + f, d:TOK]
                        mark(stt(dst, PS[:, 4 + n % 2, f * TOK:(f + 1) * TOK - d], ch("gdn_conv", (3 - d) * 6 + 2 * s + f),
                                 dst, ALU.mult, ALU.add))
                    settle()
                signal(sem(f"proj_bank_read{n % 2}"), 1)
                dve.sem_inc(sem("gdn_taps"), 1)

            def gdn_tokens():
                dve.wait_ge(sem("gdn_squares"), 1)
                dve.tensor_reduce(stat[:, 8:24], sq.rearrange("p (u d) -> p u d", d=DH), AX, ALU.add) \
                    .then_inc(sem("gdn_sums"), 1)
                dve.wait_ge(sem("gdn_rstd"), 1)
                link(ts(stat[:, 8:16], stat[:, 8:16], DH ** -0.5, None, ALU.mult))
                psu = lambda b: PS[:, b, :].rearrange("p (u d) -> p u d", d=DH)
                mark(tt(qn, psu(0), unit(stat[:, 8:16], DH), ALU.mult))
                mark(tt(kn, psu(1), unit(stat[:, 16:24], DH), ALU.mult))
                mark(tt(vb, psu(2), unit(th(beta), DH), ALU.mult))
                settle()
                mark(tt(qi, qn, unit(th(e_g), DH), ALU.mult))
                mark(tt(kbg, kn, unit(th(be_g), DH), ALU.mult))
                settle()
                tt(ko, kn, unit(th(e_rest), DH), ALU.mult).then_inc(sem("gdn_normed"), 1)

            bank2 = lambda b: PS[:, b:b + 2, :].rearrange("p b n -> p (b n)").rearrange("p (u n) -> p u n", n=P)

            def gdn_grams():
                dve.wait_ge(sem("decay"), 1)
                for t, h in ALL_UNITS:
                    u = u_of(t, h)
                    ins = stt(m_gd[:, u, :], bank2(0)[:, u, :], beta[:, t, h:h + 1], dec[:, u, :], ALU.mult, ALU.mult)
                ins.then_inc(sem("m_ready"), 1)

            def gdn_a_qk():
                dve.wait_ge(sem("decay_t"), 1)
                dve.wait_ge(sem("qk_gram"), 1)
                tt(a_qk, bank2(6), dec_t, ALU.mult).then_inc(sem("qk_gram_read"), 1)

            def gdn_first_level():
                dve.wait_ge(sem("m_ready"), 1)
                dve.wait_ge(sem("qk_gram_read"), 1)
                dve.wait_ge(sem("mt_ready"), 1)
                mark(tt(inv, m_gd, units(mask("m1"), 8), ALU.mult))
                settle()
                mark(tt(inv_t, mt_gd, units(mask("t1"), 8), ALU.mult))
                tt(inv, units(ident[:, :], 8), inv, ALU.subtract).then_inc(sem("inv_ready"), 1)
                tt(c_t, mt_gd, units(mask("t2"), 8), ALU.mult).then_inc(sem("ct_ready"), 1)
                settle()
                tt(inv_t, units(ident[:, :], 8), inv_t, ALU.subtract).then_inc(sem("inv_t_ready"), 1)

            def gdn_xcx(lv):
                if lv < 4:
                    dve.wait_ge(sem("cx"), lv + 1)
                    tt(c_t, mt_gd, units(mask(f"t{4 << lv}"), 8), ALU.mult).then_inc(sem("ct_ready"), 1)
                    dve.wait_ge(sem("xcx"), lv + 1)
                    tt(inv, inv, bank2(6), ALU.subtract).then_inc(sem("inv_ready"), 1)
                else:
                    dve.wait_ge(sem("xcx"), lv + 1)
                tt(inv_t, inv_t, bank2(0), ALU.subtract).then_inc(sem("inv_t_ready"), 1)

            def gdn_solve():
                dve.memset(state, 0.0).then_inc(sem("state_ready"), 1)

            def gdn_state_in(c):
                t, half = divmod(c, 2)
                r = slice(64 * half, 64 * half + 64)
                if c == 0:
                    dve.wait_ge(sem("solution"), 1)
                dve.wait_ge(sem("w_state"), c + 1)
                for hh in range(2):
                    us = slice(t * 4 + hh, t * 4 + hh + 3, 2)
                    ins = tt(v_new[r, us, :], u_gd[r, us, :], PS[r, 3 * hh, 0:P].rearrange("p (h d) -> p h d", d=DH),
                             ALU.subtract)
                ins.then_inc(sem("v_new"), 1)

            def gdn_state_out(c):
                t, half = divmod(c, 2)
                dve.wait_ge(sem("chunk_done"), c + 1)
                for h in range(HEADS):
                    a = slice(64 * (h % 2), 64 * (h % 2) + 64)
                    s = state[a, h // 2, :]
                    ins = stt(s, s, e_last[a, t, half, h:h + 1], PS[a, 2, (h // 2) * DH:(h // 2 + 1) * DH],
                              ALU.mult, ALU.add)
                ins.then_inc(sem("state_ready"), 1)

            def head_out(grp, src):
                return dve.tensor_copy(group_view(grp), src.rearrange("p (t n) -> p t n", t=TT))

            def head_sums(k):
                dve.wait_ge(sem("group_squares"), k + 1)
                half = k % 2
                dve.tensor_reduce(stat[:, 8 + 8 * half:16 + 8 * half],
                                  sq[:, 512 * half:512 * half + 512].rearrange("p (u d) -> p u d", d=DH), AX, ALU.add) \
                    .then_inc(sem("group_sums"), 1)

            def head_post(k, grp, gain):
                dve.wait_ge(sem("group_rstd"), k + 1)
                for t in range(TT):
                    v = group_view(grp)[:, t, :].rearrange("p (h d) -> p h d", d=DH)
                    at = 8 + 8 * (k % 2) + 4 * t
                    mark(tt(v, v, unit(stat[:, at:at + 4], DH), ALU.mult))
                settle()
                for t in range(TT):
                    v = group_view(grp)[:, t, :].rearrange("p (h d) -> p h d", d=DH)
                    g = gain if gain is not None else tokm[:, t, 5 + grp, :].rearrange("p (h d) -> p h d", d=DH)
                    mark(tt(v, v, g, ALU.mult))
                signal(sem("group_normed"), 1)

            def scale_queries():
                dve.wait_ge(sem("gates_silu"), 1)
                mark(ts(chm[:, 6:8, :], chm[:, 6:8, :], DH ** -0.5, None, ALU.mult))
                settle()

            def silu_gates():
                for i, name in enumerate(("gdn_on", "hg_on", "gla_on")):
                    for t in range(TT):
                        v = tokm[:, t, 6 + i, :].rearrange("p (h d) -> p h d", d=DH)
                        mark(tt(v, v, units(rows(name, DH), HEADS), ALU.mult))
                settle()

            def gdn_out():
                dve.wait_ge(sem("chunk_done"), 4)
                mark(head_out(1, PS[:, 1, :]))
                settle()
                for t in range(TT):
                    for hh in range(2):
                        v = group_view(1)[:, t, :].rearrange("p (h d) -> p h d", d=DH)[:, hh:hh + 3:2, :]
                        at = P * (1 + t)
                        ins = tt(v, v, PS[:, 3 * hh, at:at + P].rearrange("p (h d) -> p h d", d=DH), ALU.add)
                ins.then_inc(sem("group_out"), 1)

            def fox_norms():
                dve.wait_ge(sem("fox_squares"), 1)
                dve.tensor_reduce(stat[:, 8:24], sq.rearrange("p (u d) -> p u d", d=DH), AX, ALU.add) \
                    .then_inc(sem("fox_sums"), 1)

            def fox_scale():
                dve.wait_ge(sem("fox_rstd"), 1)
                st = stat[:, 8:24].rearrange("p (t s h) -> p t s h", t=TT, s=2)
                for t in range(TT):
                    for s in range(2):
                        v = tokm[:, t, s, :].rearrange("p (h d) -> p h d", d=DH)
                        mark(tt(v, v, unit(st[:, t, s, :], DH), ALU.mult))
                settle()
                for t in range(TT):
                    for s, name in enumerate(("fox_qn", "fox_kn")):
                        v = tokm[:, t, s, :].rearrange("p (h d) -> p h d", d=DH)
                        mark(tt(v, v, units(rows(name, DH), HEADS), ALU.mult))
                settle()
                ts(tokm[:, :, 0, :], tokm[:, :, 0, :], DH ** -0.5, None, ALU.mult).then_inc(sem("fox_normed"), 1)

            def fox_max(r):
                dve.wait_ge(sem("fox_logits"), r + 1)
                dve.tensor_reduce(stat[:, 24 + 2 * r:26 + 2 * r], PS[:, 6:8, 2 * P:3 * P], AX, ALU.max,
                                  negate=True).then_inc(sem("fox_max"), 1)
                dve.tensor_reduce(stat[:, 28 + 2 * r:30 + 2 * r], PS[:, 6:8, 0:TOK], AX, ALU.max,
                                  negate=True).then_inc(sem("fox_max"), 1)

            def fox_out(r):
                dve.wait_ge(sem("fox_probs"), 4 * (r + 1))
                sums = stat[:, 32:40].rearrange("p (t h) -> p t h", t=TT)[:, :, 2 * r:2 * r + 2]
                link(dve.reciprocal(sums, sums))
                dve.wait_ge(sem("fox_out"), r + 1)
                for t in range(TT):
                    v = group_view(0)[:, t, r * P:(r + 1) * P].rearrange("p (h d) -> p h d", d=DH)
                    at = 3 * P + t * DH
                    ins = tt(v, PS[:, 6:8, at:at + DH], unit(sums[:, t, :], DH), ALU.mult)
                    mark(ins)
                signal(sem("fox_out_read"), 1)

            def la_keys():
                z = tokm[:, :, TOKM["hg_f"], :]
                dve.wait_ge(sem("logits_ln"), 2)
                s = sq[:, 512:1024].rearrange("p (t n) -> p t n", t=TT)
                mark(stt(la[:, :, 0:2, :].rearrange("p t f n -> p t (f n)"), z, 0.0, s, ALU.min, ALU.subtract))
                link(stt(z, z, 0.0, s, ALU.max, ALU.add))
                ts(z, z, -1.0, None, ALU.mult).then_inc(sem("hg_keys_log"), 1)
                signal(sem("la_ready"), 1)

            def la_all():
                mark(dve.memset(a_la[CHUNK:P, :, 0:CHUNK], 0.0))
                mark(dve.memset(a_packed, 0.0))
                signal(sem("pairs_free"), 1)
                three = lambda v, b: v.rearrange("p (m two n) -> p m two n", two=2, n=b)
                hg_pairs = PS[:, 0:2, 0:4 * CHUNK].rearrange("p b (u n) -> p b u n", n=CHUNK)
                gla_pairs = PS[:, 2:6, 0:TT * CHUNK].rearrange("p b (t n) -> p b t n", t=TT)
                hg_packed = a_packed[:, 0:8, :].rearrange("p (b u) n -> p b u n", b=2)
                gla_packed = a_packed[:, 8:16, :].rearrange("p (b t) n -> p b t n", t=TT)
                hg_a = a_la[:, 0:8, :].rearrange("p (b u) n -> p b u n", b=2)
                gla_a = a_la[:, 8:16, :].rearrange("p (b t) n -> p b t n", t=TT)
                q3 = chm[:, 6:9, :].rearrange("p f n -> p (f n)")
                k3 = chm[:, 9:12, :].rearrange("p f n -> p (f n)")

                def operand(lv):
                    b = 1 << lv
                    dve.wait_ge(sem("level_exp"), lv // 2 + 1)
                    if lv == 0:
                        dve.wait_ge(sem("la_keys"), 1)
                    w, z = three(w_lv[:, lv % 4, :], b), three(z_lv[:, lv % 2, :], b)
                    if lv >= 2:
                        dve.wait_ge(sem("gla_pairs"), lv)
                    mark(tt(z[:, :, 0, :], w[:, :, 0, :], three(k3, b)[:, :, 0, :], ALU.mult))
                    tt(z[:, :, 1, :], w[:, :, 1, :], three(q3, b)[:, :, 1, :], ALU.mult).then_inc(sem("level_operand"), 1)

                def select(lv):
                    for hg in (True, False):
                        dve.wait_ge(sem("hg_pairs" if hg else "gla_pairs"), lv + 2)
                        pairs, in_chunk = (hg_pairs, hg_packed) if hg else (gla_pairs, gla_packed)
                        in_tile = hg_a if hg else gla_a
                        if lv < 6:
                            m = packed(lv).bitcast(I32).rearrange("p (a b n) -> p a b n", a=1, b=1)
                            ins = dve.copy_predicated(in_chunk, m.to_broadcast([P] + list(pairs.shape[1:])), pairs)
                        elif lv == 6:
                            ins = dve.tensor_copy(in_tile[0:CHUNK, :, :, CHUNK:P], pairs[0:CHUNK])
                        elif hg:
                            ins = dve.tensor_copy(a_top[:, 0:4, :].rearrange("p (b u) n -> p b (u n)", b=2),
                                                  PS[:, 0:2, 0:2 * P])
                        else:
                            ins = dve.tensor_copy(a_top[:, 4:8, :], PS[:, 2:6, 0:P])
                        ins.then_inc(sem("hg_pairs_read" if hg else "gla_pairs_read"), 1)
                    dve.wait_ge(sem("hg_pairs_read"), lv + 2)
                    dve.wait_ge(sem("gla_pairs_read"), lv + 2)

                operand(0)
                select(-1)
                for lv in range(8):
                    if lv < 7:
                        operand(lv + 1)
                    select(lv)
                    if lv == 0:
                        silu_gates()
                    if lv in (1, 3):
                        head_sums(lv // 2)
                    if lv == 2:
                        head_post(0, 1, None)
                    if lv == 4:
                        head_post(1, 0, units(rows("fox_on", DH), HEADS))

            before = {4: [gate_parts], 6: [la_keys], 7: [gdn_a_qk], 14: [gdn_solve]}
            middle = {1: [gates], 3: [gk_logs], 4: [gdn_tokens], 6: [gdn_grams], 7: [gdn_first_level]}
            for lv in range(5):
                middle[9 + lv] = [lambda lv=lv: gdn_xcx(lv)]
            middle[10].append(fox_norms)
            middle[11].append(fox_scale)
            for n, what in enumerate(MIX_ORDER):
                for piece in before.get(n, ()):
                    piece()
                ahead(n)
                for piece in middle.get(n, ()):
                    piece()
                if 1 <= n <= 3:
                    gdn_taps(n - 1, n)
            gdn_state_in(0)
            fox_max(0)
            gdn_state_out(0)
            gdn_state_in(1)
            gdn_state_out(1)
            scale_queries()
            dve.wait_ge(sem("la_hi"), 1)
            tt(la_lo[:, :, :, :].rearrange("p t f n -> p t (f n)"), la.rearrange("p t f n -> p t (f n)"), la_hi.bitcast(F),
               ALU.subtract).then_inc(sem("la_split"), 1)
            gdn_state_in(2)
            fox_out(0)
            gdn_state_out(2)
            gdn_state_in(3)
            fox_max(1)
            gdn_out()
            fox_out(1)
            dve.sem_inc(sem("group_out"), 1)
            la_all()
            for g in (2, 3):
                dve.wait_ge(sem("la_out"), g - 1)
                head_out(g, PS[:, 4 + g, :]).then_inc(sem("group_out"), 1)
            turned("mixed", [(None, act_hi, act_lo)], banks=(0, 1))
            head_sums(2)
            head_sums(3)
            ahead(STEP["mix_out"])
            head_post(2, 2, None)
            head_post(3, 3, None)
            ahead(STEP["mix_out"] + 1)
            turned("mixed", [(None, act_hi, act_lo)], banks=(2, 3))
            ahead(STEP["mix_out"] + 2)
            signal(sem("mix_done"), 1)
            def ahead_4(name):
                for j in range(4):
                    ahead(STEP[name] + j)

            def residual(k, n_used):
                for t in range(TT):
                    if t == 0:
                        dve.wait_ge(sem("tile_summed"), k)
                    else:
                        dve.wait_ge(block_used, n_used)
                    tt(x[:, t, :], x[:, t, :], low4[:, t, :], ALU.add).then_inc(sem("x_tile"), 1)

            residual(1, STEP["mix_out"] + 4)
            norm(2, junk[:, 1, :])
            turned("norm2", [(lambda j: ch("norm2", j), h_hi, h_lo)])
            ahead(STEP["mix_out"] + 3)

            def older_taps(y, src, col, two_ft, ready):
                for c in range(2):
                    stt(y[:, c, 1:TOK], src[:, c, 0:TOK - 1], channel[:, bass.ds(col(1) + c, 1)], y[:, c, 1:TOK],
                        ALU.mult, ALU.add).then_inc(ready[0], 1)
                dve.wait_ge(ready[0], ready[1])
                for c in range(2):
                    ins = stt(y[:, c, 2:TOK], src[:, c, 0:TOK - 2], channel[:, bass.ds(col(0) + c, 1)], y[:, c, 2:TOK],
                              ALU.mult, ALU.add)
                return ins

            def ffn(f, p_name=None):
                n0 = STEP[f"ffn{f}"]
                conv = PC[f"ffn_conv{f}"]
                bank = lambda b: PS[:, b, :].rearrange("p (c n) -> p c n", c=2)

                def gate(i):
                    dve.wait_ge(sem("gate_last_tap"), i + (PAIRS * f + 1))
                    ins = older_taps(y_gate, bank(4), lambda tap: 2 * i + (conv + tap * 2 * FT), 0,
                                     (sem("gate_tap1"), 2 * i + (2 * PAIRS * f + 2)))
                    ins.then_inc(sem("gate_convolved"), 1)
                    dve.wait_ge(sem("gate_convolved"), i + (PAIRS * f + 1))

                def up(i):
                    dve.wait_ge(sem("up_last_tap"), i + (PAIRS * f + 1))
                    ins = older_taps(y_up, bank(5), lambda tap: 2 * i + (conv + tap * 2 * FT + FT), 0,
                                     (sem("up_tap1"), 2 * i + (2 * PAIRS * f + 2)))
                    ins.then_inc(sem("up_read"), 1)
                    dve.wait_ge(sem("up_read"), i + (PAIRS * f + 1))
                    dve.wait_ge(sem("gate_silu"), i + (PAIRS * f + 1))
                    tt(hidden, s_gate, y_up, ALU.mult).then_inc(sem("hidden_ready"), 1)

                def hid(i):
                    dve.wait_ge(sem("hidden_hi"), i + (PAIRS * f + 1))
                    tt(hid_lo, hidden, hid_hi.bitcast(F), ALU.subtract).then_inc(sem("hidden_split"), 1)

                ahead(n0)
                gate(0)
                ahead(n0 + 1)
                up(0)
                hid(0)
                if p_name:
                    turned(p_name, [(None, p_hi, p_lo)], 6)
                with dve.Fori(1, PAIRS) as i:
                    n = n0 - 1
                    split(n + 2 + 3 * i, (n + 2) % RING)
                    gate(i)
                    split(n + 3 + 3 * i, (n + 3) % RING)
                    up(i)
                    split(n + 4 + 3 * i, (n + 4) % RING)
                    hid(i)

            ffn(0)
            residual(2, STEP["ffn0"] + 3 * PAIRS)
            norm(3, junk[:, 1, :])
            turned("pre_mix0", [(lambda j: ch("pre_mix0", j), h_hi, h_lo)])
            ahead(STEP["ffn0"] + 3 * PAIRS - 1)

            n0 = STEP["sc_in"]
            signal(sem("sc_bank_read"), 3)
            with dve.Fori(0, 4) as i:
                split(n0 + 2 + 3 * i, (n0 + 2) % RING)
                split(n0 + 3 + 3 * i, (n0 + 3) % RING)
                dve.wait_ge(sem("sc_gc"), i + 1)
                dve.wait_ge(block_used, n0 + 2 + 3 * i)
                tt(y_up, s_gate, PS[:, 5, :].rearrange("p (c n) -> p c n", c=2), ALU.mult).then_inc(sem("sc_product"), 1)
                dve.wait_ge(sem("sc_product"), i + 1)
                dve.sem_inc(sem("sc_bank_read"), 2)
                dve.wait_ge(sem("sc_last_tap"), i + 1)
                ins = older_taps(y_gate, y_up, lambda tap: 2 * i + (PC["sc_conv"] + tap * 8), 0, (sem("sc_tap1"), 2 * i + 2))
                ins.then_inc(sem("sc_convolved"), 1)
                dve.wait_ge(sem("sc_convolved"), i + 1)
                split(n0 + 4 + 3 * i, (n0 + 4) % RING)
                dve.wait_ge(block_used, n0 + 3 + 3 * i)
                tt(hidden, y_gate, PS[:, 6, :].rearrange("p (c n) -> p c n", c=2), ALU.mult).then_inc(sem("sc_gated"), 1)
                dve.wait_ge(sem("sc_gated"), i + 1)
                dve.sem_inc(sem("sc_bank_read"), 1)
                dve.wait_ge(sem("sc_hi"), i + 1)
                tt(act_lo[:, bass.ds(2 * i, 2), :], hidden, act_hi[:, bass.ds(2 * i, 2), :].bitcast(F), ALU.subtract) \
                    .then_inc(sem("sc_hidden"), 1)
            ahead_4("sc_out")

            posts = [0]

            def post(acc):
                q = posts[0]
                posts[0] += 1
                dve.wait_ge(sem("post_loaded"), 16 * (q + 1))
                for t in range(TT):
                    dve.wait_ge(sem("post_rstd"), 2 * q + t + 1)
                    link(stt(junk[:, t, :], acc[:, t, :], stat[:, 4 + t:5 + t], post_g, ALU.mult, ALU.mult))
                    if t == 1:
                        dve.sem_inc(sem("post_used"), 1)
                    tt(x[:, t, :], x[:, t, :], junk[:, t, :], ALU.add).then_inc(sem("x_tile"), 1)

            post(low4)
            norm(4, gate_s[:, 1, :])
            turned("pre_ffn0", [(lambda j: ch("pre_ffn0", j), h_hi, h_lo)])

            def ffn_and_ple(layer, k):
                ffn(1 + layer, f"p{layer}")
                ahead(STEP[f"ffn{1 + layer}"] + 3 * PAIRS - 1)
                post(low4)
                norm(k + 1, gate_s[:, 1, :])
                turned(f"pre_ple{layer}", [(lambda j: ch(f"pre_ple{layer}", j), h_hi, h_lo)], 0)
                ahead(STEP[f"ple_proj{layer}"])
                for j in range(4):
                    ahead(STEP[f"ple_gate{layer}"] + j)
                for t in range(TT):
                    dve.wait_ge(sem("ple_gate"), 2 * layer + t + 1)
                    tt(gate_s[:, t, :], gate_s[:, t, :], high4[:, t, :], ALU.mult).then_inc(sem("ple_product"), 1)
                post(gate_s)

            ffn_and_ple(0, 4)
            norm(6, junk[:, 1, :])
            turned("pre_mix1", [(lambda j: ch("pre_mix1", j), h_hi, h_lo), (lambda j: ch("kv", j), act_hi, act_lo)])

            lv4 = rows("lambda", 256).rearrange("p (a b d) -> p a b d", a=2, b=2)
            lj = lg1[0].rearrange("p a n -> p (a n)")[:, 0:P].rearrange("p (a d) -> p a d", a=2)
            link(tt(lj, lv4[:, :, 0, :], lv4[:, :, 1, :], ALU.mult))
            dve.tensor_reduce(lam[:, 0:2], lj, AX, ALU.add).then_inc(sem("lambda_sums"), 1)
            dve.wait_ge(sem("lambda_exps"), 1)
            link(tt(lam[:, 2:3], lam[:, 1:2], lam[:, 0:1], ALU.subtract))
            link(ts(lam[:, 3:4], lam[:, 2:3], -LAMBDA_INIT, None, ALU.add))

            def head(h):
                a, l1, l0 = att_stat[h % 2], lg1[h % 2], lg0[h % 2]
                dve.wait_ge(sem("logits"), h + 1)
                b1 = bias_t[:, h, :].rearrange("p (o n) -> p o n", o=1).to_broadcast([P, 2, TOK])
                b0 = bias_t[:, h, P:TOK].rearrange("p (o n) -> p o n", o=1).to_broadcast([P, 2, P])
                mark(tt(l1, PS[:, 6:8, 0:TOK], b1, ALU.add))
                mark(tt(l0, PS[:, 6:8, TOK:TOK + P], b0, ALU.add))
                settle()
                dve.sem_inc(sem("logits_read"), 1)
                dve.tensor_reduce(a[:, 0:2], l1, AX, ALU.max, negate=True).then_inc(sem("att_max"), 1)
                dve.tensor_reduce(a[:, 2:4], l0, AX, ALU.max, negate=True).then_inc(sem("att_max"), 1)

            def combine(h):
                a, l1, l0 = att_stat[h % 2], lg1[h % 2], lg0[h % 2]
                dve.wait_ge(sem("att_exp"), h + 1)
                if h >= 2:
                    dve.wait_ge(sem("att_turned"), h - 1)
                link(dve.reciprocal(a[:, 8:12], a[:, 4:8]))
                mark(tt(a[:, 9:12:2], a[:, 9:12:2], lam[:, 3:4].to_broadcast([P, 2]), ALU.mult))
                mark(ts(l1[:, 0, :], l1[:, 0, :], a[:, 8:9], None, ALU.mult))
                mark(ts(l0[:, 0, :], l0[:, 0, :], a[:, 10:11], None, ALU.mult))
                settle()
                w1 = at_w[h % 2][:, 0:2, :].rearrange("p a n -> p (a n)")
                mark(stt(w1, l1[:, 1, :], a[:, 9:10], l1[:, 0, :], ALU.mult, ALU.add))
                stt(at_w[h % 2][:, 2, :], l0[:, 1, :], a[:, 11:12], l0[:, 0, :], ALU.mult, ALU.add) \
                    .then_inc(sem("att_weights"), 1)
                dve.wait_ge(sem("att_weights"), h + 1)

            for j in range(12):
                n = STEP["att_k"] + j
                if j == 5:
                    dve.wait_ge(sem("bias_copied"), 1)
                if j >= 5:
                    head(j - 5)
                ahead(n)
                if j >= 5:
                    combine(j - 5)
            head(7)
            combine(7)
            for t in range(TT):
                dve.wait_ge(sem("head_squares"), t + 1)
                heads = lambda v: v.rearrange("p (u d) -> p u d", d=P)
                s = stat[:, 8 + 8 * t:16 + 8 * t]
                dve.tensor_reduce(s, heads(xn[:, t, :]), AX, ALU.add).then_inc(sem("subln_sums"), 1)
                dve.wait_ge(sem("subln_rstd"), t + 1)
                link(ts(s, s, 1.0 - LAMBDA_INIT, None, ALU.mult))
                tt(heads(xn[:, t, :]), heads(low4[:, t, :]), unit(s, P), ALU.mult).then_inc(sem("heads_normed"), 1)
            turned("att", [(lambda j: ch("subln"), act_hi, act_lo)])
            ahead_4("att_out")
            post(low4)
            norm(7, gate_s[:, 1, :])
            turned("pre_ffn1", [(lambda j: ch("pre_ffn1", j), h_hi, h_lo)])
            ffn_and_ple(1, 7)


def column_block(w, c0, n=256):
    b = np.zeros((P, KC, 256), np.float32)
    b[:, :, 0:n] = w[:, c0:c0 + n].reshape(KC, P, n).transpose(1, 0, 2)
    return b.reshape(P, BLK)


def row_block_of(w, j):
    return w[256 * j:256 * (j + 1)].reshape(2, P, D).transpose(1, 0, 2).reshape(P, BLK)


def weight_stream(a):
    blocks = []
    w = a["w_in"][0]
    small = np.concatenate([w[:, W_IN[n]:W_IN[n] + m] for n, m in
                            (("gla_gk", 16), ("fox_f", 4), ("gdn_a", 4), ("gdn_b", 4))], axis=1)
    for what in MIX_ORDER:
        blocks.append(column_block(small, 0, SMALL) if what == "small" else column_block(w, W_IN[what]))

    def rows_of(w, n=4):
        blocks.extend(row_block_of(w, j) for j in range(n))

    def ffn(up, down):
        for i in range(PAIRS):
            blocks.append(column_block(up, 256 * i))
            blocks.append(column_block(up, D_FF + 256 * i))
            if i:
                blocks.append(row_block_of(down, i - 1))
        blocks.append(row_block_of(down, PAIRS - 1))

    rows_of(a["w_out"][0])
    ffn(a["w_up"][0], a["w_down"][0])
    w = a["w_sc_in_2"][0]
    for i in range(4):
        for part in (1, 2, 0):
            blocks.append(column_block(w, part * D + 256 * i))
    rows_of(a["w_sc_out_2"][0])
    for layer in range(2):
        if layer == 1:
            for i in range(4):
                blocks.append(column_block(a["w_kv_2"], 256 * i))
            for i in range(4):
                blocks.append(column_block(a["w_q_2"][0], 256 * i))
            rows_of(a["w_kv_2"][:, D:])
            rows_of(a["w_o_2"][0])
        ffn(a["w_ffn_up_2"][layer], a["w_ffn_down_2"][layer])
        rows_of(a["w_ple_proj_2"][layer], 1)
        rows_of(a["w_ple_gate_2"][layer])
    assert len(blocks) == N_BLOCKS
    return np.stack(blocks)


def channel_columns(a):
    def cols(v):
        return v.reshape(-1, P).T

    parts = [cols(a["norm1_g"][0]), cols(a["norm2_g"][0]), cols(a["g_pre_mix_2"][0]), cols(a["g_pre_ffn_2"][0]),
             cols(a["g_pre_ple_2"][0]), cols(a["g_pre_mix_2"][1]), cols(a["g_kv_2"]), cols(a["g_pre_ffn_2"][1]),
             cols(a["g_pre_ple_2"][1]), cols(a["g_subln_2"][0]), cols(a["w_sc_conv_2"][0]), cols(a["gdn_conv_w"][0]),
             cols(a["ffn_conv_w"][0]), cols(a["ffn_conv_b"][0]), cols(a["w_ffn_conv_2"][0]), cols(a["w_ffn_conv_2"][1])]
    return np.ascontiguousarray(np.concatenate(parts, axis=1))


def mask_table():
    i = np.arange(P)
    r, c = i[:, None], i[None, :]
    same = r // CHUNK == c // CHUNK
    one = {"tri": r <= c, "ones": r >= 0 * c, "after": r > c, "blk_tri": same & (r <= c), "blk_after": same & (r > c),
           "ind0": (r < CHUNK) & (c >= 0), "ind1": (r >= CHUNK) & (c >= 0),
           "m1": (r // 2 == c // 2) & (c < r)}
    for lv in range(6):
        b = 1 << lv
        one[f"t{b}"] = (r // (2 * b) == c // (2 * b)) & (r % (2 * b) < b) & (c % (2 * b) >= b)
    pack = [r % CHUNK == c[:, 0:CHUNK]]
    for lv in range(6):
        pack.append(np.concatenate([one[f"t{1 << lv}"][0:CHUNK, 0:CHUNK], one[f"t{1 << lv}"][CHUNK:, CHUNK:]]))
    pack.append(0 * pack[0])
    for j in range(4):
        one[f"packed{j}"] = np.concatenate(pack[2 * j:2 * j + 2], axis=1)
    for lv in range(7):
        b = 1 << lv
        mid = c // (2 * b) * (2 * b) + b - 1
        right = c % (2 * b) >= b
        one[f"e{b}"] = np.where(right, (r > mid) & (r <= c), (r > c) & (r <= mid))
    one["tri_again"], one["eye"] = one["tri"], r == c
    add = {"fox_add": c <= r, "gdn_add": same & (c <= r)}
    rows = [np.where(add[n], 0.0, NEG) if n in add else one[n] + np.zeros((P, P)) for n in MASKS]
    return np.stack(rows, axis=1).astype(np.float32)


def distance_one_hot():
    dist = 255 - np.arange(N_DIST)
    n, exact, far = 32, 16, 128
    safe = np.maximum(dist, 1).astype(np.float32)
    large = exact + (np.log(safe / np.float32(exact)) / np.float32(math.log(far / exact)) * (n - exact)).astype(np.int32)
    bucket = np.where(dist < 0, n, np.where(dist < exact, dist, np.minimum(large, n - 1)))
    return (np.arange(BIAS_ROWS)[:, None] == bucket[None, :]).astype(np.float32)


def kernel(**inputs):
    import concourse.bacc as bacc
    from concourse.bass_utils import run_bass_kernel_spmd

    a = {k: np.asarray(v) for k, v in inputs.items()}
    row = np.concatenate([a["fox_b_f"][0], a["gdn_dt_bias"][0], a["gdn_a_log"][0], a["fox_qn_g"][0], a["fox_kn_g"][0],
                          a["fox_on_g"][0], a["gdn_on_g"][0], a["hg_on_g"][0], a["gla_on_g"][0], a["gla_b_gk"][0],
                          a["diff_lambda_2"][0].reshape(-1)])
    post = np.stack([a["g_post_mix_2"][0], a["g_post_ffn_2"][0], a["g_post_ple_2"][0],
                     a["g_post_mix_2"][1], a["g_post_ffn_2"][1], a["g_post_ple_2"][1]])
    arrays = {
        "weights": weight_stream(a), "x_in": a["x"][0], "masks_in": mask_table(), "ident_in": np.eye(P, dtype=np.float32),
        "channel_in": channel_columns(a), "row_in": row, "w_gk_in": a["gla_w_gk"][0], "post_in": post,
        "p_in": a["p_2"][:, 0], "table_in": a["rel_bias_2"], "onehot_in": distance_one_hot(),
        "flip_in": np.eye(P, dtype=np.float32)[::-1],
    }
    arrays = {k: np.ascontiguousarray(v) for k, v in arrays.items()}
    nc = bacc.Bacc("TRN2", target_bir_lowering=False, num_devices=1)
    args = [nc.dram_tensor(k, v.shape, mybir.dt.from_np(v.dtype), kind="ExternalInput").ap() for k, v in arrays.items()]
    result = nc.dram_tensor("result", (TOK, D), F, kind="ExternalOutput").ap()
    build(nc, *args, result)
    r = run_bass_kernel_spmd(nc, [arrays], core_ids=[0])
    return r.results[0]["result"].reshape(1, TOK, D)
```
